# Optimizing a Trainium2 kernel written in Bass

```python
import jax, jax.numpy as jnp
from jax import lax
import numpy as np
import math
import jax
import jax.numpy as jnp

D_MODEL = 1024
BATCH = 1
SEQ = 256
DEPTH = 2

POOL_WINDOWS = (2, 4, 8, 16)
POOL_GROUP = 128
POOL_WIDTH = POOL_GROUP * len(POOL_WINDOWS)
ATTN_HEADS = 8
HEAD_DIM = 64
ATTN_WIDTH = ATTN_HEADS * HEAD_DIM
MOBA_BLOCK = 256
MOBA_TOPK = 3
Q_CHUNK = 64
RNN_BLOCKS = 10
RNN_BLOCK = 128
RNN_WIDTH = RNN_BLOCKS * RNN_BLOCK
RNN_CONV = 4
RG_C = 8.0
D_FF = 2816
FFN_CONV = 3
EPS = 1e-6
NEG_INF = -1e30
N_EVEN = (DEPTH + 1) // 2
N_ODD = DEPTH // 2


def rms_norm(x, g):
    x32 = x.astype(jnp.float32)
    y = x32 * lax.rsqrt(jnp.mean(x32 * x32, axis=-1, keepdims=True) + EPS)
    return (y * g.astype(jnp.float32)).astype(x.dtype)

def causal_dwconv(x, w, b):
    K, C = w.shape
    y = lax.conv_general_dilated(
        x, w[:, None, :].astype(x.dtype), window_strides=(1,), padding=[(K - 1, 0)],
        dimension_numbers=('NWC', 'WIO', 'NWC'), feature_group_count=C)
    return y + b.astype(x.dtype)

def multiscale_pool_minus_identity(u):
    S = u.shape[1]
    u32 = u.astype(jnp.float32)
    cs = jnp.cumsum(u32, axis=1)
    count = jnp.arange(1, S + 1, dtype=jnp.float32)[None, :, None]
    outs = []
    for gi, w in enumerate(POOL_WINDOWS):
        sl = slice(gi * POOL_GROUP, (gi + 1) * POOL_GROUP)
        c = cs[..., sl]
        prev = jnp.pad(c, ((0, 0), (w, 0), (0, 0)))[:, :S]
        outs.append((c - prev) / jnp.minimum(count, float(w)) - u32[..., sl])
    return jnp.concatenate(outs, axis=-1)

def head_rms(t, g):
    t32 = t.astype(jnp.float32)
    return t32 * lax.rsqrt(jnp.mean(t32 * t32, axis=-1, keepdims=True) + EPS) * g.astype(jnp.float32)

def moba_attention(q, k, v, q_gain, k_gain):
    B, S, H, Dh = q.shape
    nb = -(-S // MOBA_BLOCK)
    s_pad = nb * MOBA_BLOCK
    pad = ((0, 0), (0, s_pad - S), (0, 0), (0, 0))
    qn = jnp.pad(head_rms(q, q_gain), pad).transpose(0, 2, 1, 3)
    kn = jnp.pad(head_rms(k, k_gain), pad).transpose(0, 2, 1, 3)
    vp = jnp.pad(v.astype(jnp.float32), pad).transpose(0, 2, 1, 3)
    k_blocks = kn.reshape(B, H, nb, MOBA_BLOCK, Dh)
    v_blocks = vp.reshape(B, H, nb, MOBA_BLOCK, Dh)
    slopes = 2.0 ** (-8.0 * jnp.arange(1, H + 1, dtype=jnp.float32) / H)
    scale = Dh ** -0.5
    topk = min(MOBA_TOPK, nb - 1)
    q_blk = jnp.arange(s_pad) // MOBA_BLOCK
    if topk > 0:
        k_mean = jnp.mean(k_blocks, axis=3)
        gate = jnp.einsum('bhqd,bhnd->bhqn', qn, k_mean)
        past = jnp.arange(nb)[None, :] < q_blk[:, None]
        gate = jnp.where(past[None, None], gate, -jnp.inf)
        _, sel_idx = lax.top_k(gate, topk)
        sel_valid = sel_idx < q_blk[None, None, :, None]
    bi = jnp.arange(B)[:, None, None, None]
    hi = jnp.arange(H)[None, :, None, None]
    kpos = jnp.arange(MOBA_BLOCK)

    def chunk(c):
        start = c * Q_CHUNK
        q_c = lax.dynamic_slice_in_dim(qn, start, Q_CHUNK, axis=2)
        t_c = start + jnp.arange(Q_CHUNK)
        own = start // MOBA_BLOCK
        k_own = lax.dynamic_index_in_dim(k_blocks, own, axis=2, keepdims=False)
        v_own = lax.dynamic_index_in_dim(v_blocks, own, axis=2, keepdims=False)
        dist_own = (t_c[:, None] - (own * MOBA_BLOCK + kpos)[None, :]).astype(jnp.float32)
        logit_own = (jnp.einsum('bhqd,bhkd->bhqk', q_c, k_own) * scale
                     - slopes[None, :, None, None] * dist_own[None, None])
        logit_own = jnp.where((dist_own >= 0)[None, None], logit_own, NEG_INF)
        if topk == 0:
            p_own = jax.nn.softmax(logit_own, axis=-1)
            return jnp.einsum('bhqk,bhkd->bhqd', p_own, v_own)
        idx_c = lax.dynamic_slice_in_dim(sel_idx, start, Q_CHUNK, axis=2)
        valid_c = lax.dynamic_slice_in_dim(sel_valid, start, Q_CHUNK, axis=2)
        k_sel = k_blocks[bi, hi, idx_c]
        v_sel = v_blocks[bi, hi, idx_c]
        s_pos = idx_c[..., None] * MOBA_BLOCK + kpos
        dist_sel = (t_c[None, None, :, None, None] - s_pos).astype(jnp.float32)
        logit_sel = (jnp.einsum('bhqd,bhqjkd->bhqjk', q_c, k_sel) * scale
                     - slopes[None, :, None, None, None] * dist_sel)
        logit_sel = jnp.where(valid_c[..., None], logit_sel, NEG_INF)
        n_sel = topk * MOBA_BLOCK
        logits = jnp.concatenate([logit_sel.reshape(B, H, Q_CHUNK, n_sel), logit_own], axis=-1)
        p = jax.nn.softmax(logits, axis=-1)
        p_sel = p[..., :n_sel].reshape(B, H, Q_CHUNK, topk, MOBA_BLOCK)
        p_own = p[..., n_sel:]
        return (jnp.einsum('bhqjk,bhqjkd->bhqd', p_sel, v_sel)
                + jnp.einsum('bhqk,bhkd->bhqd', p_own, v_own))

    outs = lax.map(chunk, jnp.arange(s_pad // Q_CHUNK))
    out = outs.transpose(1, 0, 3, 2, 4).reshape(B, s_pad, H * Dh)
    return out[:, :S]

def pool_attn_mixer(h, w_in, pool_w, pool_scale, q_gain, k_gain, w_out):
    B, S, _ = h.shape
    z = h @ w_in
    u, q, k, v = jnp.split(z, [POOL_WIDTH, POOL_WIDTH + ATTN_WIDTH, POOL_WIDTH + 2 * ATTN_WIDTH], axis=-1)
    p = multiscale_pool_minus_identity(u).astype(h.dtype)
    p = jnp.einsum('bsgc,gcd->bsgd', p.reshape(B, S, len(POOL_WINDOWS), POOL_GROUP), pool_w)
    p = p.reshape(B, S, POOL_WIDTH) * pool_scale
    a = moba_attention(q.reshape(B, S, ATTN_HEADS, HEAD_DIM), k.reshape(B, S, ATTN_HEADS, HEAD_DIM),
                       v.reshape(B, S, ATTN_HEADS, HEAD_DIM), q_gain, k_gain)
    return jnp.concatenate([p, a.astype(h.dtype)], axis=-1) @ w_out

def rglru_mixer(h, w_in, conv_w, conv_b, w_a, b_a, w_x, b_x, lam, w_out):
    B, S, _ = h.shape
    z = h @ w_in
    gate, xr = jnp.split(z, 2, axis=-1)
    xr = causal_dwconv(xr, conv_w, conv_b)
    xb = xr.reshape(B, S, RNN_BLOCKS, RNN_BLOCK)
    r = jax.nn.sigmoid((jnp.einsum('bsnc,ncd->bsnd', xb, w_a).reshape(B, S, RNN_WIDTH) + b_a).astype(jnp.float32))
    i = jax.nn.sigmoid((jnp.einsum('bsnc,ncd->bsnd', xb, w_x).reshape(B, S, RNN_WIDTH) + b_x).astype(jnp.float32))
    log_a = -RG_C * r * jax.nn.softplus(-lam.astype(jnp.float32))
    a = jnp.exp(log_a)
    b = jnp.sqrt(-jnp.expm1(2.0 * log_a)) * (i * xr.astype(jnp.float32))

    def combine(left, right):
        a1, b1 = left
        a2, b2 = right
        return a1 * a2, a2 * b1 + b2

    _, hs = lax.associative_scan(combine, (a, b), axis=1)
    y = jax.nn.gelu(gate) * hs.astype(gate.dtype)
    return y @ w_out

def conv_ffn(h, w_in, conv_w, conv_b, w_out):
    z = causal_dwconv(h @ w_in, conv_w, conv_b)
    u, g = jnp.split(z, 2, axis=-1)
    return (jax.nn.gelu(g) * u) @ w_out

def first_inputs(seed: int = 0) -> dict:
    key = jax.random.key(seed)
    ks = jax.random.split(key, 24)
    f32 = jnp.float32
    nrm = lambda k, shape, s: jax.random.normal(k, shape, f32) * s
    u = jax.random.uniform(ks[16], (N_ODD, RNN_WIDTH), f32, minval=0.9, maxval=0.999)
    a0 = u ** (1.0 / RG_C)
    return {
        "x": nrm(ks[0], (BATCH, SEQ, D_MODEL), 1.0),
        "norm_mix": 1.0 + nrm(ks[1], (DEPTH, D_MODEL), 0.05),
        "norm_ffn": 1.0 + nrm(ks[2], (DEPTH, D_MODEL), 0.05),
        "pa_w_in": nrm(ks[3], (N_EVEN, D_MODEL, POOL_WIDTH + 3 * ATTN_WIDTH), D_MODEL ** -0.5),
        "pa_pool_w": nrm(ks[4], (N_EVEN, len(POOL_WINDOWS), POOL_GROUP, POOL_GROUP), POOL_GROUP ** -0.5),
        "pa_pool_scale": 1.0 + nrm(ks[5], (N_EVEN, POOL_WIDTH), 0.1),
        "pa_q_gain": 1.0 + nrm(ks[6], (N_EVEN, HEAD_DIM), 0.05),
        "pa_k_gain": 1.0 + nrm(ks[7], (N_EVEN, HEAD_DIM), 0.05),
        "pa_w_out": nrm(ks[8], (N_EVEN, POOL_WIDTH + ATTN_WIDTH, D_MODEL), (POOL_WIDTH + ATTN_WIDTH) ** -0.5),
        "rg_w_in": nrm(ks[9], (N_ODD, D_MODEL, 2 * RNN_WIDTH), D_MODEL ** -0.5),
        "rg_conv_w": nrm(ks[10], (N_ODD, RNN_CONV, RNN_WIDTH), RNN_CONV ** -0.5),
        "rg_conv_b": nrm(ks[11], (N_ODD, RNN_WIDTH), 0.01),
        "rg_w_a": nrm(ks[12], (N_ODD, RNN_BLOCKS, RNN_BLOCK, RNN_BLOCK), RNN_BLOCK ** -0.5),
        "rg_b_a": nrm(ks[13], (N_ODD, RNN_WIDTH), 0.01),
        "rg_w_x": nrm(ks[14], (N_ODD, RNN_BLOCKS, RNN_BLOCK, RNN_BLOCK), RNN_BLOCK ** -0.5),
        "rg_b_x": nrm(ks[15], (N_ODD, RNN_WIDTH), 0.01),
        "rg_lambda": jnp.log(a0) - jnp.log1p(-a0),
        "rg_w_out": nrm(ks[17], (N_ODD, RNN_WIDTH, D_MODEL), RNN_WIDTH ** -0.5),
        "ffn_w_in": nrm(ks[18], (DEPTH, D_MODEL, 2 * D_FF), D_MODEL ** -0.5),
        "ffn_conv_w": nrm(ks[19], (DEPTH, FFN_CONV, 2 * D_FF), FFN_CONV ** -0.5),
        "ffn_conv_b": nrm(ks[20], (DEPTH, 2 * D_FF), 0.01),
        "ffn_w_out": nrm(ks[21], (DEPTH, D_FF, D_MODEL), D_FF ** -0.5),
    }

def first_block(x, norm_mix, norm_ffn, pa_w_in, pa_pool_w, pa_pool_scale, pa_q_gain, pa_k_gain,
              pa_w_out, rg_w_in, rg_conv_w, rg_conv_b, rg_w_a, rg_b_a, rg_w_x, rg_b_x, rg_lambda,
              rg_w_out, ffn_w_in, ffn_conv_w, ffn_conv_b, ffn_w_out):
    for l in range(DEPTH):
        j = l // 2
        h = rms_norm(x, norm_mix[l])
        if l % 2 == 0:
            x = x + pool_attn_mixer(h, pa_w_in[j], pa_pool_w[j], pa_pool_scale[j],
                                    pa_q_gain[j], pa_k_gain[j], pa_w_out[j])
        else:
            x = x + rglru_mixer(h, rg_w_in[j], rg_conv_w[j], rg_conv_b[j], rg_w_a[j], rg_b_a[j],
                                rg_w_x[j], rg_b_x[j], rg_lambda[j], rg_w_out[j])
        h = rms_norm(x, norm_ffn[l])
        x = x + conv_ffn(h, ffn_w_in[l], ffn_conv_w[l], ffn_conv_b[l], ffn_w_out[l])
    return x


N_MIXERS = 2
N_SSD_LAYERS = (DEPTH + N_MIXERS - 1) // N_MIXERS
N_MLA_LAYERS = DEPTH // N_MIXERS
N_SUBLAYERS = 3

FFN_RES_WEIGHT = 0.5
NORM_EPS = 1e-6

SSD_EXPAND = 2
D_INNER = SSD_EXPAND * D_MODEL
SSD_HEAD_DIM = 64
SSD_HEADS = D_INNER // SSD_HEAD_DIM
SSD_GROUPS = 8
SSD_HEADS_PER_GROUP = SSD_HEADS // SSD_GROUPS
SSD_STATE = 128
SSD_CONV = 5
SSD_CHUNK = 128
SSD_CONV_CH = D_INNER + 2 * SSD_GROUPS * SSD_STATE
SSD_IN = D_INNER + SSD_CONV_CH + 2 * SSD_HEADS
SSD_NORM_GROUP = D_INNER // SSD_GROUPS

MLA_HEADS = 16
MLA_Q_LORA = 384
MLA_KV_LORA = 256
MLA_NOPE = 64
MLA_ROPE = 32
MLA_V = 64
MLA_QK = MLA_NOPE + MLA_ROPE
MLA_IN = MLA_Q_LORA + MLA_KV_LORA + MLA_ROPE
ROPE_THETA = 10000.0
ATTN_Q_BLOCK = 128
MAX_POS_OFFSET = 1024


def rms_norm_2(x, g):
    xf = x.astype(jnp.float32)
    y = xf * lax.rsqrt(jnp.mean(xf * xf, axis=-1, keepdims=True) + NORM_EPS)
    return (y * g.astype(jnp.float32)).astype(x.dtype)

def modulate(x, g, shift, scale):
    return rms_norm_2(x, g) * (1.0 + scale[:, None, :]) + shift[:, None, :]

def swiglu(h, w_gate, w_up, w_down):
    return (jax.nn.silu(h @ w_gate) * (h @ w_up)) @ w_down

def depthwise_conv_centred(x, w, bias):
    ch = x.shape[-1]
    pad = SSD_CONV // 2
    out = lax.conv_general_dilated(
        x, w[:, None, :], window_strides=(1,), padding=[(pad, pad)],
        dimension_numbers=("NWC", "WIO", "NWC"), feature_group_count=ch)
    return out + bias

def ssd_chunked(x, dt, A, Bm, Cm):
    b, s, g, r, p = x.shape
    n = Bm.shape[-1]
    nc = s // SSD_CHUNK
    q = SSD_CHUNK
    x = x.reshape(b, nc, q, g, r, p)
    dt = dt.reshape(b, nc, q, g, r)
    Bm = Bm.reshape(b, nc, q, g, n)
    Cm = Cm.reshape(b, nc, q, g, n)
    a_cum = jnp.cumsum(dt * A, axis=2)
    xdt = x * dt[..., None]

    seg = a_cum[:, :, :, None] - a_cum[:, :, None, :]
    mask = jnp.tril(jnp.ones((q, q), dtype=bool))[:, :, None, None]
    decay = jnp.exp(jnp.where(mask, seg, -jnp.inf))
    cb = jnp.einsum("bcign,bcjgn->bcijg", Cm, Bm)
    y_diag = jnp.einsum("bcijgr,bcjgrp->bcigrp", cb[..., None] * decay, xdt)

    decay_to_end = jnp.exp(a_cum[:, :, -1:] - a_cum)
    states = jnp.einsum("bcjgn,bcjgrp->bcgrpn", Bm, xdt * decay_to_end[..., None])
    chunk_decay = jnp.exp(a_cum[:, :, -1])

    def step(h, inp):
        st, dec = inp
        return h * dec[..., None, None] + st, h

    h0 = jnp.zeros((b, g, r, p, n), dtype=states.dtype)
    _, h_prev = lax.scan(step, h0, (jnp.moveaxis(states, 1, 0), jnp.moveaxis(chunk_decay, 1, 0)))
    h_prev = jnp.moveaxis(h_prev, 0, 1)

    y_off = jnp.einsum("bcign,bcgrpn->bcigrp", Cm, h_prev) * jnp.exp(a_cum)[..., None]
    return (y_diag + y_off).reshape(b, s, g, r, p)

def ssd_mixer(h, w_in, conv_w, conv_b, dt_bias, a_log, d_skip, norm_g, w_out):
    b, s, _ = h.shape
    g, r = SSD_GROUPS, SSD_HEADS_PER_GROUP
    proj = h @ w_in
    z, xbc, dt_raw = jnp.split(proj, [D_INNER, D_INNER + SSD_CONV_CH], axis=-1)
    xbc = jax.nn.silu(depthwise_conv_centred(xbc, conv_w, conv_b))
    xs, Bm, Cm = jnp.split(xbc, [D_INNER, D_INNER + SSD_GROUPS * SSD_STATE], axis=-1)
    xs = xs.reshape(b, s, g, r, SSD_HEAD_DIM)
    Bm = Bm.reshape(b, s, g, SSD_STATE)
    Cm = Cm.reshape(b, s, g, SSD_STATE)
    dt = jax.nn.softplus(dt_raw.reshape(b, s, 2, g, r) + dt_bias.reshape(2, g, r))
    A = -jnp.exp(a_log).reshape(2, g, r)

    flip = lambda t: jnp.flip(t, axis=1)
    y_fwd = ssd_chunked(xs, dt[:, :, 0], A[0], Bm, Cm)
    y_bwd = flip(ssd_chunked(flip(xs), flip(dt[:, :, 1]), A[1], flip(Bm), flip(Cm)))
    y = y_fwd + y_bwd + xs * d_skip.reshape(g, r)[..., None]

    y = y.reshape(b, s, D_INNER) * jax.nn.silu(z)
    y = rms_norm_2(y.reshape(b, s, g, SSD_NORM_GROUP), norm_g.reshape(g, SSD_NORM_GROUP))
    return y.reshape(b, s, D_INNER) @ w_out

def rope_tables(positions):
    inv_freq = ROPE_THETA ** (-jnp.arange(0, MLA_ROPE, 2, dtype=jnp.float32) / MLA_ROPE)
    ang = positions.astype(jnp.float32)[..., None] * inv_freq
    return jnp.cos(ang)[:, :, None, :], jnp.sin(ang)[:, :, None, :]

def apply_rope_tail(t, cos, sin):
    t_nope, t_pe = t[..., :MLA_NOPE], t[..., MLA_NOPE:]
    x1, x2 = jnp.split(t_pe.astype(jnp.float32), 2, axis=-1)
    rot = jnp.concatenate([x1 * cos - x2 * sin, x2 * cos + x1 * sin], axis=-1).astype(t.dtype)
    return jnp.concatenate([t_nope, rot], axis=-1)

def blocked_attention(q, k, v):
    b, s, h, dq = q.shape
    nq = s // ATTN_Q_BLOCK
    scale = dq ** -0.5
    qb = jnp.moveaxis(q.reshape(b, nq, ATTN_Q_BLOCK, h, dq), 1, 0)

    def one_block(q_blk):
        logits = jnp.einsum("bqhd,bkhd->bhqk", q_blk, k).astype(jnp.float32) * scale
        p = jax.nn.softmax(logits, axis=-1).astype(v.dtype)
        return jnp.einsum("bhqk,bkhv->bqhv", p, v)

    o = lax.map(one_block, qb)
    return jnp.moveaxis(o, 0, 1).reshape(b, s, h, v.shape[-1])

def mla_mixer(h, positions, w_in, q_norm_g, kv_norm_g, w_uq, w_ukv, q_head_g, k_head_g, w_out):
    b, s, _ = h.shape
    q_lat, kv_lat, k_pe = jnp.split(h @ w_in, [MLA_Q_LORA, MLA_Q_LORA + MLA_KV_LORA], axis=-1)
    q = (rms_norm_2(q_lat, q_norm_g) @ w_uq).reshape(b, s, MLA_HEADS, MLA_QK)
    kv = (rms_norm_2(kv_lat, kv_norm_g) @ w_ukv).reshape(b, s, MLA_HEADS, MLA_NOPE + MLA_V)
    k_nope, v = jnp.split(kv, [MLA_NOPE], axis=-1)
    k_pe = jnp.broadcast_to(k_pe[:, :, None, :], (b, s, MLA_HEADS, MLA_ROPE))
    k = jnp.concatenate([k_nope, k_pe], axis=-1)
    q = rms_norm_2(q, q_head_g)
    k = rms_norm_2(k, k_head_g)
    cos, sin = rope_tables(positions)
    q = apply_rope_tail(q, cos, sin)
    k = apply_rope_tail(k, cos, sin)
    o = blocked_attention(q, k, v)
    return o.reshape(b, s, MLA_HEADS * MLA_V) @ w_out

def second_inputs(seed: int = 0) -> dict:
    key = jax.random.key(seed)
    ks = iter(jax.random.split(key, 40))

    def normal(shape, scale):
        return scale * jax.random.normal(next(ks), shape, jnp.float32)

    def gain(shape):
        return 1.0 + 0.05 * jax.random.normal(next(ks), shape, jnp.float32)

    na, nb = N_SSD_LAYERS, N_MLA_LAYERS
    x = normal((BATCH, SEQ, D_MODEL), 1.0)
    c = normal((BATCH, D_MODEL), 1.0)
    positions = (jax.random.randint(next(ks), (BATCH, 1), 0, MAX_POS_OFFSET, dtype=jnp.int32)
                 + jnp.arange(SEQ, dtype=jnp.int32)[None, :])
    norm_g = gain((DEPTH, N_SUBLAYERS, D_MODEL))
    w_mod = normal((DEPTH, D_MODEL, N_SUBLAYERS * 3 * D_MODEL), D_MODEL ** -0.5)
    b_mod = normal((DEPTH, N_SUBLAYERS * 3 * D_MODEL), 0.02)
    ffn_w_gate = normal((DEPTH, 2, D_MODEL, D_FF), D_MODEL ** -0.5)
    ffn_w_up = normal((DEPTH, 2, D_MODEL, D_FF), D_MODEL ** -0.5)
    ffn_w_down = normal((DEPTH, 2, D_FF, D_MODEL), D_FF ** -0.5)

    ssd_w_in = normal((na, D_MODEL, SSD_IN), D_MODEL ** -0.5)
    ssd_conv_w = normal((na, SSD_CONV, SSD_CONV_CH), SSD_CONV ** -0.5)
    ssd_conv_b = normal((na, SSD_CONV_CH), 0.02)
    dt0 = jnp.exp(jax.random.uniform(next(ks), (na, 2, SSD_HEADS), jnp.float32,
                                     math.log(1e-3), math.log(1e-1)))
    ssd_dt_bias = dt0 + jnp.log(-jnp.expm1(-dt0))
    ssd_a_log = jnp.log(jax.random.uniform(next(ks), (na, 2, SSD_HEADS), jnp.float32, 1.0, 16.0))
    ssd_d = gain((na, SSD_HEADS))
    ssd_norm_g = gain((na, D_INNER))
    ssd_w_out = normal((na, D_INNER, D_MODEL), D_INNER ** -0.5)

    mla_w_in = normal((nb, D_MODEL, MLA_IN), D_MODEL ** -0.5)
    mla_q_norm_g = gain((nb, MLA_Q_LORA))
    mla_kv_norm_g = gain((nb, MLA_KV_LORA))
    mla_w_uq = normal((nb, MLA_Q_LORA, MLA_HEADS * MLA_QK), MLA_Q_LORA ** -0.5)
    mla_w_ukv = normal((nb, MLA_KV_LORA, MLA_HEADS * (MLA_NOPE + MLA_V)), MLA_KV_LORA ** -0.5)
    mla_q_head_g = gain((nb, MLA_QK))
    mla_k_head_g = gain((nb, MLA_QK))
    mla_w_out = normal((nb, MLA_HEADS * MLA_V, D_MODEL), (MLA_HEADS * MLA_V) ** -0.5)

    return {
        "x": x, "c": c, "positions": positions,
        "norm_g": norm_g, "w_mod": w_mod, "b_mod": b_mod,
        "ffn_w_gate": ffn_w_gate, "ffn_w_up": ffn_w_up, "ffn_w_down": ffn_w_down,
        "ssd_w_in": ssd_w_in, "ssd_conv_w": ssd_conv_w, "ssd_conv_b": ssd_conv_b,
        "ssd_dt_bias": ssd_dt_bias, "ssd_a_log": ssd_a_log, "ssd_d": ssd_d,
        "ssd_norm_g": ssd_norm_g, "ssd_w_out": ssd_w_out,
        "mla_w_in": mla_w_in, "mla_q_norm_g": mla_q_norm_g, "mla_kv_norm_g": mla_kv_norm_g,
        "mla_w_uq": mla_w_uq, "mla_w_ukv": mla_w_ukv, "mla_q_head_g": mla_q_head_g,
        "mla_k_head_g": mla_k_head_g, "mla_w_out": mla_w_out,
    }

def second_block(x, c, positions, norm_g, w_mod, b_mod, ffn_w_gate, ffn_w_up, ffn_w_down,
              ssd_w_in, ssd_conv_w, ssd_conv_b, ssd_dt_bias, ssd_a_log, ssd_d,
              ssd_norm_g, ssd_w_out,
              mla_w_in, mla_q_norm_g, mla_kv_norm_g, mla_w_uq, mla_w_ukv,
              mla_q_head_g, mla_k_head_g, mla_w_out):
    cond = jax.nn.silu(c)
    for i in range(DEPTH):
        mod = (cond @ w_mod[i] + b_mod[i]).reshape(-1, N_SUBLAYERS, 3, D_MODEL)

        h = modulate(x, norm_g[i, 0], mod[:, 0, 0], mod[:, 0, 1])
        x = x + FFN_RES_WEIGHT * mod[:, 0, 2][:, None, :] * swiglu(
            h, ffn_w_gate[i, 0], ffn_w_up[i, 0], ffn_w_down[i, 0])

        h = modulate(x, norm_g[i, 1], mod[:, 1, 0], mod[:, 1, 1])
        j = i // N_MIXERS
        if i % N_MIXERS == 0:
            y = ssd_mixer(h, ssd_w_in[j], ssd_conv_w[j], ssd_conv_b[j], ssd_dt_bias[j],
                          ssd_a_log[j], ssd_d[j], ssd_norm_g[j], ssd_w_out[j])
        else:
            y = mla_mixer(h, positions, mla_w_in[j], mla_q_norm_g[j], mla_kv_norm_g[j],
                          mla_w_uq[j], mla_w_ukv[j], mla_q_head_g[j], mla_k_head_g[j],
                          mla_w_out[j])
        x = x + mod[:, 1, 2][:, None, :] * y

        h = modulate(x, norm_g[i, 2], mod[:, 2, 0], mod[:, 2, 1])
        x = x + FFN_RES_WEIGHT * mod[:, 2, 2][:, None, :] * swiglu(
            h, ffn_w_gate[i, 1], ffn_w_up[i, 1], ffn_w_down[i, 1])
    return x


def setup_inputs(seed=0):
    out = dict(first_inputs(seed))
    for name, value in second_inputs(seed + 1).items():
        if name != "x":
            out[name + "_2"] = value
    return out


def reference(
    x, norm_mix, norm_ffn, pa_w_in, pa_pool_w, pa_pool_scale, pa_q_gain, pa_k_gain, pa_w_out,
    rg_w_in, rg_conv_w, rg_conv_b, rg_w_a, rg_b_a, rg_w_x, rg_b_x, rg_lambda, rg_w_out,
    ffn_w_in, ffn_conv_w, ffn_conv_b, ffn_w_out, c_2, positions_2, norm_g_2, w_mod_2, b_mod_2,
    ffn_w_gate_2, ffn_w_up_2, ffn_w_down_2, ssd_w_in_2, ssd_conv_w_2, ssd_conv_b_2,
    ssd_dt_bias_2, ssd_a_log_2, ssd_d_2, ssd_norm_g_2, ssd_w_out_2, mla_w_in_2, mla_q_norm_g_2,
    mla_kv_norm_g_2, mla_w_uq_2, mla_w_ukv_2, mla_q_head_g_2, mla_k_head_g_2, mla_w_out_2,
):
    x = first_block(
        x, norm_mix, norm_ffn, pa_w_in, pa_pool_w, pa_pool_scale, pa_q_gain, pa_k_gain,
        pa_w_out, rg_w_in, rg_conv_w, rg_conv_b, rg_w_a, rg_b_a, rg_w_x, rg_b_x, rg_lambda,
        rg_w_out, ffn_w_in, ffn_conv_w, ffn_conv_b, ffn_w_out,
    )
    return second_block(
        x, c_2, positions_2, norm_g_2, w_mod_2, b_mod_2, ffn_w_gate_2, ffn_w_up_2, ffn_w_down_2,
        ssd_w_in_2, ssd_conv_w_2, ssd_conv_b_2, ssd_dt_bias_2, ssd_a_log_2, ssd_d_2,
        ssd_norm_g_2, ssd_w_out_2, mla_w_in_2, mla_q_norm_g_2, mla_kv_norm_g_2, mla_w_uq_2,
        mla_w_ukv_2, mla_q_head_g_2, mla_k_head_g_2, mla_w_out_2,
    )


_drawn_inputs = setup_inputs


def setup_inputs(seed=0):
    import zlib

    import numpy as np

    out = dict(_drawn_inputs(seed))
    spreads = {}
    factors = {'pa_q_gain': 4.872,
     'pa_k_gain': 5.288,
     'rg_conv_b': 2.82,
     'rg_b_a': 8.0,
     'rg_b_x': 8.0,
     'ffn_conv_b': 4.939,
     'ssd_conv_b_2': 7.462,
     'ssd_d_2': 8.0,
     'ssd_norm_g_2': 3.054,
     'mla_q_norm_g_2': 8.0,
     'mla_kv_norm_g_2': 7.453,
     'mla_q_head_g_2': 8.0,
     'mla_k_head_g_2': 8.0}
    for name, (base, spread) in spreads.items():
        noise = np.random.default_rng([zlib.crc32(name.encode()), seed]).standard_normal(out[name].shape)
        drawn = base * np.exp(spread * noise) if base else spread * noise
        out[name] = jnp.asarray(drawn.astype(out[name].dtype))
    for name, factor in factors.items():
        out[name] = (out[name] * factor).astype(out[name].dtype)
    return out
```

```python
from contextlib import ExitStack

import numpy as np

import concourse.bass as bass
from concourse import mybir

F32 = mybir.dt.float32
F32R = mybir.dt.float32r
I32 = mybir.dt.int32
BF16 = mybir.dt.bfloat16
ALU = mybir.AluOpType
ACT = mybir.ActivationFunctionType
AX = mybir.AxisListType

P = 128
T = 256
D = 1024
KD = D // P
FF = 2816
KF = FF // P
SLAB = 16 * P
RAW = 4
SPLIT = 2
HALF = SLAB // 2
RNN = 10
HEADS1, HD1 = 8, 64
SSD_H, SSD_G = 32, 8
MLA_H = 16
EPS = 1e-6
DMA_SCRATCH = 8192
MASKED = -(2.0 ** 100)

STAGES = [("pa_in", 8), ("pa_out", 4), ("f0_up", 22), ("f0_down", 11),
          ("rg_in", 10), ("rg_out", 5), ("f1_up", 22), ("f1_down", 11),
          ("g00_up", 22), ("g00_down", 11), ("ssd_in", 25), ("ssd_out", 8),
          ("g01_up", 22), ("g01_down", 11), ("g10_up", 22), ("g10_down", 11),
          ("mla_in", 3), ("mla_uq", 4), ("mla_ukv", 2), ("mla_out", 4),
          ("g11_up", 22), ("g11_down", 11)]
N0, _n = {}, 0
for _name, _s in STAGES:
    N0[_name] = _n
    _n += _s
NSLABS = _n
SLABS = dict(STAGES)
UPS = ["pa_in", "f0_up", "rg_in", "f1_up", "g00_up", "ssd_in", "g01_up", "g10_up",
       "mla_in", "g11_up"]
EV0, OD0, _e, _o = {}, {}, 0, 0
for _name in UPS:
    EV0[_name], OD0[_name] = _e, _o
    _e += (SLABS[_name] + 1) // 2
    _o += SLABS[_name] // 2

RESID, SUMS, HID, _h = {}, {}, {}, 0
for _name, _s in STAGES:
    if _name.endswith(("down", "out")):
        RESID[_name] = 8 * len(RESID)
        if _name not in ("pa_out", "mla_out"):
            HID[_name] = _h
            SUMS[_name] = 4 * len(SUMS)
            _h += _s
LIN, _l = {}, 0
for _name, _s in [("f0_up", 22), ("rg_in", 10), ("f1_up", 22), ("ssd_in", 16)]:
    LIN[_name] = _l
    _l += _s

COL, _c = {}, 0
for _name, _s in [("nmix0", 8), ("nmix1", 8), ("nffn0", 8), ("nffn1", 8), ("pool_scale", 4),
                  ("q_gain", 1), ("k_gain", 1),
                  ("fconv0", 3 * 44), ("fconvb0", 44), ("fconv1", 3 * 44), ("fconvb1", 44),
                  ("rconv", 40), ("rconvb", 10), ("rba", 10), ("rbx", 10), ("lam", 10),
                  ("ng", 48), ("bmod", 144),
                  ("sconv", 5 * 32), ("sconvb", 32), ("dt_bias", 1), ("a_log", 1), ("skip", 16),
                  ("snorm", 16), ("mqn", 3), ("mkn", 2), ("mqh", 1), ("mkh", 1), ("inv_freq", 1)]:
    COL[_name] = _c
    _c += _s
NPAR = _c
CON, _c = {}, 0
for _name, _s in [("ident", 128), ("ones", 128), ("pair64", 128), ("rows96", 128),
                  ("rope_rows", 128), ("rope_sum", 128), ("mask_f", 128), ("mask_b", 128),
                  ("cos_row", 1), ("phase", 1), ("sign", 1), ("nope", 1)]:
    CON[_name] = _c
    _c += _s
NCON = _c


TWO_PI = float(2 * np.pi)
ROUND = float(3 << 22)
_t1 = 6.28125
_t2 = float(np.float32(np.round((2 * np.pi - _t1) * 2 ** 22) / 2 ** 22))
TURN = (_t1, _t2, float(np.float32(2 * np.pi - _t1 - _t2)))
DOWN = {"f0_up": "f0_down", "f1_up": "f1_down", "g00_up": "g00_down", "g01_up": "g01_down",
        "g10_up": "g10_down", "g11_up": "g11_down"}


class Steps:

    def __init__(self, eng, sem):
        self.eng, self.sem, self.n, self.off = eng, sem, 0, None

    def put(self, ins):
        ins.then_inc(self.sem, 1)
        self.n += 1
        return self.n

    def wait(self, n):
        self.eng.wait_ge(self.sem, n if self.off is None else self.off + n)

    def link(self, ins):
        self.wait(self.put(ins))

    def enter(self, i, per):
        self.start, self.per, self.off = self.n, per, i * per

    def leave(self, times):
        assert self.n - self.start == self.per, (self.n - self.start, self.per)
        self.n, self.off = self.start + times * self.per, None


def plus(a, i, k):
    return a if i is None else i * k + a


def build(nc, x, slabs, par, con, tab, small, cvec, pos, wmod, out):
    with ExitStack() as ctx:
        def sb(name, shape, dt=F32):
            return ctx.enter_context(nc.sbuf_tensor(name, shape, dt))

        def sem(name):
            return ctx.enter_context(nc.semaphore(name))

        def over(name, shape, dt, at):
            return nc.alloc_sbuf_tensor_at(name, shape, dt, offset=at)

        raw = sb("raw", [P, RAW, SLAB])
        hi = sb("hi", [P, SPLIT, SLAB], F32R)
        lo = sb("lo", [P, SPLIT, SLAB], F32R)
        X = sb("X", [P, KD, T])
        XH = sb("XH", [P, KD, T], F32R)
        XL = sb("XL", [P, KD, T], F32R)
        hh_at = (nc.sbuf_base + 31) // 32 * 32
        HH = sb("HH", [P, KF, T], F32R)
        hl_at = (nc.sbuf_base + 31) // 32 * 32
        HL = sb("HL", [P, KF, T], F32R)
        A1 = sb("A1", [P, 16, T])
        A2 = sb("A2", [P, 16, T])
        S = sb("S", [P, 4096])
        PAR = sb("PAR", [P, NPAR])
        CN = sb("CN", [P, NCON])
        modw = sb("modw", [P, 2, D])
        cond = sb("cond", [P, D])
        posi = sb("posi", [P, T], I32)
        modp = sb("modp", [P, 72, 16])
        MOD = sb("MOD", [P, 2 * 72])
        MG = sb("MG", [P, 2 * 24])
        GT = sb("GT", [P, 2 * 24])
        R = sb("R", [P, 2 * T])
        c4 = sb("c4", [P, 4 * RNN])
        tiny = sb("tiny", [P, 256])
        zero = sb("zero", [1, P], BF16)
        CS = sb("CS", [P, T])
        acr = sb("acr", [64, 2, T], F32R)
        cols = sb("cols", [P, 4, 64])
        identr = sb("identr", [P, P], F32R)
        maskr = sb("maskr", [P, 2 * P], F32R)
        TAIL = 12 * T * 4
        GG = over("GG", [P, RNN, T], F32, hh_at + TAIL)
        IX = over("IX", [P, RNN, T], F32, hl_at + TAIL)
        XS = over("XS", [P, 16, T], F32, hh_at)
        XST = over("XST", [P, 2, 16, P], F32, hl_at)
        EX = over("EX", [P, 2, 6, P], F32, hh_at + 16 * T * 4)
        MT = over("MT", [P, 2, 2, T], F32, hl_at + 16 * T * 4)
        QH = over("QH", [P, MLA_H, T], F32, hh_at)
        KH = over("KH", [P, MLA_H, T], F32, hl_at)
        SW = A2[:, 0:12, :].rearrange("p a (b c) -> p (a b) c", c=P)
        INV = A2[:, 12:16, :]
        DIST = A1[:, 8:10, :].rearrange("p a t -> p (a t)")
        VT1 = A1[:, 10:14, :].rearrange("p (k a) t -> p k (a t)", k=2)
        VT2 = A2[:, 0:8, :].rearrange("p (k a) t -> p k (a t)", k=2)
        KPS, KR = A2[:, 8, :], A2[:, 9, :]
        PAD = 16
        UP = over("UP", [P, 3, 4, PAD + T], F32, hh_at)
        VRAW = over("VRAW", [P, 4, T], F32, hl_at)
        CAT1 = over("CAT1", [P, KD, T], F32, hl_at + 4 * T * 4)

        bank = [ctx.enter_context(nc.psum_tensor(f"bank{b}", [P, 512], F32)) for b in range(8)]


        names = """par_loaded late_loaded hi_ready lo_ready slab_used even_evacuated odd_evacuated
            x_ready h_ready pair_summed resid_ready squares_ready squares_folded sum_ready norm_ready
            diag_ready spread_ready scaled_ready xh_ready lin_ready gelu_ready first_queries vec_steps act_steps pool_steps
            identr_ready cond_ready cond_loaded mod_summed mod_taken mod_ready zero_ready
            angle_ready table_ready decay_z decay_u decay_l c4_ready
            qk_squares qk_sum qk_var qk_norm v_kept v_turned vt_ready pooled pool_mixed pool_kept
            cat_hi scores_ready shift_ready exp_ready prob_ready turn_ready turned_ready
            head_ready head_kept
            ri_ready it_ready ix_ready rg_exp rg_arg rg_root
            silu_ready dt_kept dt_z dt_u dt_log exponents_ready xs_turn xs_turned
            col_turn cols_ready cb_ready expo_ready decay_ready mt_ready y_ready yz_ready
            ysq_ready ysum_ready yvar_ready yroot_ready yn_ready yh_ready
            lat_kept lat_sum lat_var lat_root lat_scaled lat_hi pe_scaled rope_summed rope_kept
            mq_kept mq_sum mq_var mq_root mq_ready mk_kept mk_sum mk_var mk_root mk_ready
            mv_turn mv_turned out_stored""".split()
        q = {name: sem(name) for name in names}
        raw_loaded = [sem(f"raw_loaded{k}") for k in range(RAW)]
        mod_loaded = [sem(f"mod_loaded{k}") for k in range(2)]
        evacuated = (q["even_evacuated"], q["odd_evacuated"])

        block = ctx.enter_context(nc.Block())

        def col(name, k=0, i=None, step=0):
            at = COL[name] + k
            return PAR[:, at:at + 1] if i is None else PAR[:, bass.ds(i * step + at, 1)]

        def col_span(name, w, k=0):
            return PAR[:, COL[name] + k:COL[name] + k + w]

        def con_mat(name, w=P):
            return CN[:, CON[name]:CON[name] + w]

        ident, ones = con_mat("ident"), con_mat("ones")

        def up_count(name, s):
            return evacuated[s % 2], (EV0, OD0)[s % 2][name] + s // 2 + 1

        @block.sync
        def _(sp):
            sp.dma_start(X[:], x).then_inc(q["par_loaded"], 16)
            sp.dma_start(CN[:], con).then_inc(q["par_loaded"], 16)
            sp.dma_start(PAR[:], par).then_inc(q["par_loaded"], 16)

            def load(k, n, i=None):
                sp.wait_ge(q["lo_ready"], plus(2 * (n - RAW + 1), i, 2 * RAW))
                src = slabs[n] if i is None else slabs[i * RAW + n]
                sp.dma_start(raw[:, k, :], src).then_inc(raw_loaded[k], 16)

            for n in range(RAW):
                sp.dma_start(raw[:, n, :], slabs[n]).then_inc(raw_loaded[n], 16)
            loops = (NSLABS - RAW) // RAW
            with sp.Fori(0, loops) as i:
                for k in range(RAW):
                    load(k, RAW + k, i)
            for n in range(RAW + loops * RAW, NSLABS):
                load(n % RAW, n)
            for k in range(4):
                sp.wait_ge(q["resid_ready"], RESID["g11_down"] + 2 * k + 2)
                sp.dma_start(out[:, 2 * k:2 * k + 2, :], X[:, 2 * k:2 * k + 2, :]).then_inc(q["out_stored"], 16)
            sp.wait_ge(q["out_stored"], 64)

        @block.tensor
        def _(pe):
            mm = nc.tensor.matmul

            def three(dst, n, j, xh, xl, start):
                k = n % SPLIT
                wh, wl = hi[:, k, j * P:(j + 1) * P], lo[:, k, j * P:(j + 1) * P]
                mm(dst, wh, xh, start=start, stop=False, skip_group_check=True)
                mm(dst, wh, xl, start=False, stop=False, skip_group_check=True)
                return mm(dst, wl, xh, start=False, stop=False, skip_group_check=True)

            def up_slab(stage, s, i=None):
                n = N0[stage] + s
                if s >= 4 or i is not None:
                    e, v = up_count(stage, s)
                    pe.wait_ge(e, plus(v - 2, i, 2))
                for m in range(2):
                    pe.wait_ge(q["lo_ready"], plus(2 * n + m + 1, i, 8))
                    for kt in range(KD):
                        last = three(bank[n % 4][:, m * T:(m + 1) * T], n, m * KD + kt,
                                     XH[:, kt, :], XL[:, kt, :], start=(m == 0 and kt == 0))
                last.then_inc(q["slab_used"], 1)

            def first_up_slab(stage, preps):
                n = N0[stage]
                pe.wait_ge(q["lo_ready"], 2 * n + 2)
                for kt in range(KD):
                    pe.wait_ge(q["x_ready"], KD * (preps - 1) + kt + 1)
                    for m in range(2):
                        last = three(bank[n % 4][:, m * T:(m + 1) * T], n, m * KD + kt,
                                     XH[:, kt, :], XL[:, kt, :], start=(m == 0 and kt == 0))
                last.then_inc(q["slab_used"], 1)

            def up_stage(stage, preps, between=None):
                loops = SLABS[stage] // 4 - 1 if SLABS[stage] >= 16 and between is None else 0
                first_up_slab(stage, preps)
                for s in range(1, 4 if loops else SLABS[stage]):
                    up_slab(stage, s)
                    if between is not None:
                        between(s)
                if loops:
                    with pe.Fori(0, loops) as i:
                        for s in range(4, 8):
                            up_slab(stage, s, i)
                    for s in range(4 + 4 * loops, SLABS[stage]):
                        up_slab(stage, s)

            def down_slab(stage, s, i=None):
                n = N0[stage] + s
                pe.wait_ge(q["h_ready"], plus(HID[stage] + s + 1, i, 4))
                for kk in range(2):
                    pe.wait_ge(q["lo_ready"], plus(2 * n + kk + 1, i, 8))
                    for m in range(KD):
                        if i is None:
                            xh, xl = HH[:, 2 * s + kk, :], HL[:, 2 * s + kk, :]
                        else:
                            xh = HH[:, bass.ds(i * 8 + 2 * s + kk, 1), :].rearrange("p a t -> p (a t)")
                            xl = HL[:, bass.ds(i * 8 + 2 * s + kk, 1), :].rearrange("p a t -> p (a t)")
                        last = three(bank[4 + m // 2][:, m % 2 * T:(m % 2 + 1) * T], n, kk * KD + m,
                                     xh, xl, start=False)
                return last.then_inc(q["slab_used"], 1)

            def down_stage(stage):
                pe.wait_ge(q["h_ready"], HID[stage] + 1)
                for b in range(4, 8):
                    mm(bank[b][:, 0:2], zero[:, :], zero[:, 0:2], start=True, stop=False,
                       skip_group_check=True)
                loops = SLABS[stage] // 4 if SLABS[stage] > 8 else 0
                if loops:
                    with pe.Fori(0, loops) as i:
                        for s in range(4):
                            down_slab(stage, s, i)
                for s in range(4 * loops, SLABS[stage] - 1):
                    down_slab(stage, s)
                s = SLABS[stage] - 1
                n = N0[stage] + s
                pe.wait_ge(q["h_ready"], HID[stage] + s + 1)
                pe.wait_ge(q["lo_ready"], 2 * n + 2)
                for m in range(KD):
                    for kk in range(2):
                        last = three(bank[4 + m // 2][:, m % 2 * T:(m % 2 + 1) * T], n, kk * KD + m,
                                     HH[:, 2 * s + kk, :], HL[:, 2 * s + kk, :], start=False)
                    if m % 2 and m < KD - 1:
                        last.then_inc(q["pair_summed"], 1)
                last.then_inc(q["slab_used"], 1)

            norms = [0]

            def norm(bank_of_sums=3):
                k = norms[0]
                norms[0] += 1
                sums = bank[bank_of_sums]
                pe.wait_ge(q["squares_folded"], k + 1)
                for m in (0, 1, 6, 7):
                    if m >= 6:
                        pe.wait_ge(q["squares_ready"], 8 * k + m + 1)
                    for j in range(2):
                        last = mm(sums[:, j:j + 1], S[:, m * T + j * P:m * T + (j + 1) * P], ones[:, 0:1],
                                  start=(m == 0 and j == 0), stop=False, skip_group_check=True)
                last.then_inc(q["sum_ready"], 1)
                pe.wait_ge(q["diag_ready"], k + 1)
                mm(bank[4][:, 0:T], ones, R[:, 0:T], start=True, stop=True).then_inc(q["spread_ready"], 1)

            def attention(done, heads, query, key, value, pairs):
                def scores(h):
                    if h >= 2:
                        pe.wait_ge(q["exp_ready"], done + h - 1)
                    for j in range(2):
                        last = mm(bank[h % 2][:, j * T:(j + 1) * T], query(h, j), key(h),
                                  start=(j == 0), stop=(j == 1), skip_group_check=True)
                    last.then_inc(q["scores_ready"], 1)

                def turn(h):
                    pe.wait_ge(q["prob_ready"], done + h + 1)
                    if h >= 2:
                        pe.wait_ge(q["turned_ready"], done + h - 1)
                    for k in range(2):
                        for j in range(2):
                            at = (h % 2) * 512 + j * T + k * P
                            last = nc.tensor.transpose(bank[2 + h % 2][:, k * T + j * P:k * T + (j + 1) * P],
                                                       S[:, at:at + P], ident)
                    last.then_inc(q["turn_ready"], 1)

                def output(h):
                    pe.wait_ge(q["turned_ready"], done + h + 1)
                    pair, row = h // 2, h % 2 * 64
                    if row == 0 and pair >= 2:
                        pe.wait_ge(q["head_kept"], pairs + pair - 1)
                    for k in range(2):
                        at = 1024 + (h % 2) * 512 + k * T
                        last = mm(bank[4 + pair % 2][row:row + 64, 0:T], value(h, k),
                                  S[:, at:at + T], start=(k == 0), stop=(k == 1), skip_group_check=True)
                    last.then_inc(q["head_ready"], 1)

                scores(0)
                for h in range(heads):
                    if h + 1 < heads:
                        scores(h + 1)
                    turn(h)
                    if h:
                        output(h - 1)
                output(heads - 1)

            pe.wait_ge(q["par_loaded"], 48)
            pe.wait_ge(q["zero_ready"], 1)
            norm()

            def qk_sum(s):
                pe.wait_ge(q["qk_squares"], s - 1)
                mm(bank[2 + s][:, :], con_mat("pair64"), S[:, (s - 2) * 512:(s - 1) * 512],
                   start=True, stop=True).then_inc(q["qk_sum"], 1)

            up_stage("pa_in", 1, lambda s: qk_sum(s - 1) if 3 <= s <= 6 else None)
            pe.wait_ge(q["even_evacuated"], 4)
            pe.wait_ge(q["odd_evacuated"], 4)
            for j in range(2):
                for v in range(4):
                    last = nc.tensor.transpose(bank[2 + j][:, v * P:(v + 1) * P],
                                               VRAW[:, v, j * P:(j + 1) * P], ident)
            last.then_inc(q["v_turned"], 1)
            pe.wait_ge(q["vt_ready"], 1)
            attention(0, HEADS1,
                      lambda h, j: A1[h % 2 * 64:h % 2 * 64 + 64, h // 2, j * P:(j + 1) * P],
                      lambda h: A1[h % 2 * 64:h % 2 * 64 + 64, 4 + h // 2, :],
                      lambda h, k: VT1[:, k, h * HD1:(h + 1) * HD1], 0)
            pe.wait_ge(q["pooled"], 1)
            pe.wait_ge(q["late_loaded"], 16 * 4)
            for g in range(4):
                last = mm(bank[6 + g // 2][:, g % 2 * T:(g % 2 + 1) * T], SW[:, g, :],
                          UP[:, 0, g, PAD:PAD + T], start=(g % 2 == 0), stop=(g % 2 == 1),
                          skip_group_check=True)
            last.then_inc(q["pool_mixed"], 1)
            up_stage("pa_out", 2)

            norm(6)
            up_stage("f0_up", 3)
            down_stage("f0_down")

            norm()

            def gates(s):
                pe.wait_ge(*up_count("rg_in", s))
                if s >= 2:
                    pe.wait_ge(q["it_ready"], s - 1)
                at = s % 2 * T
                mm(bank[4 + s % 2][:, 0:T], SW[:, 4 + s, :], S[:, at:at + T], start=True, stop=False,
                   skip_group_check=True)
                mm(bank[4 + s % 2][:, T:2 * T], SW[:, 14 + s, :], S[:, at:at + T], start=False,
                   stop=True, skip_group_check=True).then_inc(q["ri_ready"], 1)

            up_stage("rg_in", 4, lambda s: gates(s - 1) if s >= 1 else None)
            gates(RNN - 1)
            down_stage("rg_out")

            norm()
            up_stage("f1_up", 5)
            down_stage("f1_down")

            norm()
            up_stage("g00_up", 6)
            down_stage("g00_down")

            norm()

            def turn_x(r):
                if r >= 4:
                    pe.wait_ge(q["xs_turned"], r - 3)
                for v in range(4):
                    last = nc.tensor.transpose(bank[4 + r % 4][:, v * P:(v + 1) * P],
                                               XS[:, r // 2 * 4 + v, r % 2 * P:(r % 2 + 1) * P], ident)
                last.then_inc(q["xs_turn"], 1)

            def ssd_between(s):
                if s == 18:
                    pe.wait_ge(q["silu_ready"], 16)
                if s in (18, 19):
                    for r in range(4):
                        turn_x(4 * (s - 18) + r)
                if s == 22:
                    pe.wait_ge(q["exponents_ready"], 1)
                    pe.wait_ge(q["xs_turned"], 8)
                    for v in range(4):
                        src = S[0:64, 2048 + (v // 2) * T + v % 2 * P:2048 + (v // 2) * T + v % 2 * P + P]
                        last = nc.tensor.transpose(bank[4][:, v * 64:(v + 1) * 64], src,
                                                   CN[0:64, CON["ident"]:CON["ident"] + 64])
                    last.then_inc(q["col_turn"], 1)

            up_stage("ssd_in", 7, ssd_between)

            def expo(h):
                if h >= 2:
                    pe.wait_ge(q["decay_ready"], h - 1)
                b = 2 + 2 * (h % 2)
                for d, (spans, mask) in enumerate([(((0, 0, T), (T, P, P)), 0), (((0, 0, P), (P, 0, T)), 1)]):
                    sel = identr[0:64, 32 * d + h:32 * d + h + 1].to_broadcast([64, P])
                    first = True
                    for at, t0, w in spans:
                        for part in range(2):
                            mm(bank[b + d][:, at:at + w], sel, acr[:, part, t0:t0 + w], start=first,
                               stop=False, skip_group_check=True)
                            first = False
                    for at in (0, T):
                        last = mm(bank[b + d][:, at:at + P], identr[:, :], maskr[:, mask * P:(mask + 1) * P],
                                  start=False, stop=False, skip_group_check=True)
                last.then_inc(q["expo_ready"], 1)

            def cb(g):
                if g >= 2:
                    pe.wait_ge(q["mt_ready"], 4 * (g - 1))
                for j in range(2):
                    last = mm(bank[g % 2][:, j * T:(j + 1) * T], A2[:, g, j * P:(j + 1) * P], A2[:, 8 + g, :],
                              start=(j == 0), stop=(j == 1), skip_group_check=True)
                last.then_inc(q["cb_ready"], 1)

            pe.wait_ge(q["even_evacuated"], EV0["ssd_in"] + 13)
            pe.wait_ge(q["odd_evacuated"], OD0["ssd_in"] + 12)
            pe.wait_ge(q["cols_ready"], 1)
            pe.wait_ge(q["identr_ready"], 1)
            cb(0)
            expo(0)
            for h in range(SSD_H):
                if h + 1 < SSD_H:
                    expo(h + 1)
                if h % 4 == 0 and h // 4 + 1 < SSD_G:
                    cb(h // 4 + 1)
                pe.wait_ge(q["mt_ready"], h + 1)
                pair, row = h // 2, h % 2 * 64
                if row == 0 and pair >= 2:
                    pe.wait_ge(q["yz_ready"], pair - 1)
                for j in range(2):
                    last = mm(bank[6 + pair % 2][row:row + 64, 0:T], XST[:, j, pair, row:row + 64],
                              MT[:, h % 2, j, :], start=(j == 0), stop=(j == 1), skip_group_check=True)
                last.then_inc(q["y_ready"], 1)
            for g in range(SSD_G):
                pe.wait_ge(q["ysq_ready"], g + 1)
                for k in range(2):
                    last = mm(bank[g // 2][:, g % 2 * T:(g % 2 + 1) * T], ones,
                              S[:, (2 * g + k) * T:(2 * g + k + 1) * T], start=(g % 2 == 0 and k == 0),
                              stop=(k == 1), skip_group_check=True)
                if g % 2:
                    last.then_inc(q["ysum_ready"], 1)
            down_stage("ssd_out")

            norm()
            up_stage("g01_up", 8)
            down_stage("g01_down")
            norm()
            up_stage("g10_up", 9)
            down_stage("g10_down")

            norm()
            up_stage("mla_in", 10)
            pe.wait_ge(q["lat_kept"], 3)
            for k in range(3):
                mm(bank[4][:, 0:T], ones, S[:, k * T:(k + 1) * T], start=(k == 0), stop=False,
                   skip_group_check=True)
            for k in range(3, 5):
                mm(bank[4][:, T:2 * T], ones, S[:, k * T:(k + 1) * T], start=False, stop=False,
                   skip_group_check=True)
            mm(bank[5][:, 0:T], con_mat("rope_rows"), S[:, 5 * T:6 * T], start=True,
               stop=True).then_inc(q["lat_sum"], 1)
            pe.wait_ge(q["pe_scaled"], 1)
            mm(bank[6][:, 0:T], con_mat("rope_sum"), A1[:, 5, :], start=True,
               stop=True).then_inc(q["rope_summed"], 1)
            pe.wait_ge(q["x_ready"], 88)

            def mq_sum(u):
                pe.wait_ge(q["mq_kept"], u + 1)
                if u >= 2:
                    pe.wait_ge(q["mq_ready"], u - 1)
                mm(bank[4 + u % 2][:, :], con_mat("rows96"), S[:, u % 2 * 512:u % 2 * 512 + 512],
                   start=True, stop=True).then_inc(q["mq_sum"], 1)

            for s in range(4):
                n = N0["mla_uq"] + s
                for m in range(4):
                    if m % 2 == 0:
                        pe.wait_ge(q["lo_ready"], 2 * n + m // 2 + 1)
                        if s >= 2:
                            pe.wait_ge(q["mq_kept"], 2 * s + m // 2 - 3)
                    for kt in range(3):
                        last = three(bank[s % 2 * 2 + m // 2][:, m % 2 * T:(m % 2 + 1) * T], n, 4 * m + kt,
                                     XH[:, kt, :], XL[:, kt, :], start=(m % 2 == 0 and kt == 0))
                    if m == 1:
                        last.then_inc(q["first_queries"], 1)
                last.then_inc(q["slab_used"], 1)
                if s:
                    mq_sum(2 * s - 2)
                    mq_sum(2 * s - 1)
            mq_sum(6)
            mq_sum(7)

            def mk_sum(u):
                pe.wait_ge(q["mk_kept"], u + 1)
                if u >= 2:
                    pe.wait_ge(q["mk_var"], u - 1)
                else:
                    pe.wait_ge(q["mq_ready"], 8)
                mm(bank[4 + u % 2][:, :], CN[0:64, CON["ones"]:CON["ones"] + P],
                   S[0:64, u % 2 * 512:u % 2 * 512 + 512], start=True, stop=True).then_inc(q["mk_sum"], 1)

            for s in range(2):
                n = N0["mla_ukv"] + s
                for m in range(8):
                    if m % 4 == 0:
                        pe.wait_ge(q["lo_ready"], 2 * n + m // 4 + 1)
                    if m % 2 == 0:
                        if s == 0:
                            pe.wait_ge(q["mq_kept"], 5 + m // 2)
                        else:
                            pe.wait_ge(q["mk_ready"], m // 2 + 1)
                    for kt in range(2):
                        last = three(bank[m // 2][:, m % 2 * T:(m % 2 + 1) * T], n, 2 * m + kt,
                                     XH[:, 3 + kt, :], XL[:, 3 + kt, :], start=(m % 2 == 0 and kt == 0))
                last.then_inc(q["slab_used"], 1)
                for u in range(4):
                    mk_sum(4 * s + u)
            for r in range(4):
                j, half = r % 2, r // 2
                if r >= 2:
                    pe.wait_ge(q["mv_turned"], r - 1)
                pe.wait_ge(q["mk_kept"], 4 * half + 4)
                for v in range(8):
                    last = nc.tensor.transpose(bank[6 + r % 2][:, v * 64:(v + 1) * 64],
                                               A1[64:P, 8 * half + v, j * P:(j + 1) * P],
                                               CN[64:P, CON["ident"] + 64:CON["ident"] + P])
                last.then_inc(q["mv_turn"], 1)
            pe.wait_ge(q["mv_turned"], 4)
            pe.wait_ge(q["mk_ready"], 8)
            attention(HEADS1, MLA_H,
                      lambda h, j: QH[:, h, j * P:(j + 1) * P],
                      lambda h: KH[:, h, :],
                      lambda h, k: VT2[:, k, h * 64:(h + 1) * 64], HEADS1 // 2)
            up_stage("mla_out", 12)

            norm(6)
            up_stage("g11_up", 13)
            down_stage("g11_down")

        @block.scalar
        def _(act):
            f = nc.scalar.activation

            def split_hi(n, i=None):
                if n >= NSLABS:
                    return
                act.wait_ge(raw_loaded[n % RAW], plus(16 * (n // RAW + 1), i, 16))
                if n >= SPLIT:
                    act.wait_ge(q["slab_used"], plus(n - SPLIT + 1, i, 4))
                for h in range(2):
                    at = slice(h * HALF, (h + 1) * HALF)
                    f(hi[:, n % SPLIT, at], raw[:, n % RAW, at], ACT.Copy).then_inc(q["hi_ready"], 1)

            def down_stage(stage, between={}):
                loops = SLABS[stage] // 4 if SLABS[stage] > 8 and not between else 0
                if loops:
                    with act.Fori(0, loops) as i:
                        for s in range(4):
                            split_hi(N0[stage] + s + 2, i)
                for s in range(4 * loops, SLABS[stage] - 1):
                    split_hi(N0[stage] + s + 2)
                    if s in between:
                        between[s]()

            norms = [0]

            def norm(stage, layer=0, shift=None, bank_of_sums=3, then=None):
                k = norms[0]
                norms[0] += 1
                f(tiny[:, 61:62], tiny[:, 60:61], ACT.Sqrt)
                for m, w in ((0, 2), (2, 2), (4, 2), (6, 1), (7, 1)):
                    if k:
                        act.wait_ge(q["resid_ready"], 8 * (k - 1) + m + w)
                    f(S[:, m * T:(m + w) * T], X[:, m:m + w, :].rearrange("p a t -> p (a t)"),
                      ACT.Square).then_inc(q["squares_ready"], w)
                act.wait_ge(q["sum_ready"], k + 1)
                f(tiny[:, 52:54], bank[bank_of_sums][:, 0:2], ACT.Sqrt, scale=1.0 / D,
                  bias=tiny[:, 59:60]).then_inc(q["norm_ready"], 1)
                split_hi(N0[stage] + 1)
                for kt in range(KD):
                    act.wait_ge(q["scaled_ready"], 8 * k + kt + 1)
                    if shift is None:
                        f(XH[:, kt, :], S[:, kt * T:(kt + 1) * T], ACT.Copy).then_inc(q["xh_ready"], 1)
                    else:
                        f(XH[:, kt, :], S[:, kt * T:(kt + 1) * T], ACT.Identity,
                          bias=MOD[:, 72 * layer + shift + kt:72 * layer + shift + kt + 1]).then_inc(q["xh_ready"], 1)
                if then is not None:
                    f(tiny[:, 61:62], tiny[:, 60:61], then)

            def conv_ffn(stage, layer):
                def pair(p, i=None):
                    b = p % 2
                    for side in range(2):
                        n = N0[stage] + 2 * p + side
                        split_hi(n + 2, i)
                        act.wait_ge(q["slab_used"], plus(n + 1, i, 4))
                        if side == 0 and p >= 2:
                            act.wait_ge(q["h_ready"], plus(HID[DOWN[stage]] + p - 1, i, 2))
                        for m in range(2):
                            k = 2 * p + m + 22 * side
                            last = f(S[:, b * 1024 + side * 512 + m * T:b * 1024 + side * 512 + (m + 1) * T],
                                     bank[n % 4][:, m * T:(m + 1) * T], ACT.Identity,
                                     scale=col(f"fconv{layer}", 88 + k, i, 4),
                                     bias=col(f"fconvb{layer}", k, i, 4))
                        last.then_inc(q["lin_ready"], 1)
                    e, v = up_count(stage, 2 * p + 1)
                    act.wait_ge(e, plus(v, i, 2))
                    f(S[:, 2048 + b * 512:2560 + b * 512], S[:, b * 1024 + 512:b * 1024 + 1024],
                      ACT.Gelu_apprx_tanh).then_inc(q["gelu_ready"], 1)

                pair(0)
                pair(1)
                with act.Fori(0, 4) as i:
                    pair(2, i)
                    pair(3, i)
                pair(10)

            def gated_ffn(stage):
                def pair(p, i=None):
                    b = p % 2
                    n = N0[stage] + 2 * p
                    split_hi(n + 2, i)
                    act.wait_ge(q["slab_used"], plus(n + 1, i, 4))
                    if p >= 2:
                        act.wait_ge(q["h_ready"], plus(HID[DOWN[stage]] + p - 1, i, 2))
                    f(S[:, 2048 + b * 512:2560 + b * 512], bank[n % 4][:, :],
                      ACT.Silu).then_inc(evacuated[0], 1)
                    split_hi(n + 3, i)

                pair(0)
                pair(1)
                with act.Fori(0, 4) as i:
                    pair(2, i)
                    pair(3, i)
                pair(10)

            def attention(done, heads, scale, scores, cat, pairs):
                def exps(h):
                    act.wait_ge(q["shift_ready"], done + h + 1)
                    if h >= 2:
                        act.wait_ge(q["turn_ready"], done + h - 1)
                    for j in range(2):
                        at = h % 2 * 512 + j * T
                        last = f(S[:, at:at + T], scores(h, j), ACT.Exp, scale=scale,
                                 bias=tiny[:, h % 2 * 8 + 2 + j:h % 2 * 8 + 3 + j],
                                 accum_out=tiny[:, h % 2 * 8 + 4 + j:h % 2 * 8 + 5 + j])
                    last.then_inc(q["exp_ready"], 1)

                def keep_pair(p):
                    act.wait_ge(q["head_ready"], done + 2 * p + 2)
                    f(cat(p), bank[4 + p % 2][:, 0:T], ACT.Copy).then_inc(q["head_kept"], 1)

                exps(0)
                for h in range(heads):
                    if h + 1 < heads:
                        exps(h + 1)
                    act.wait_ge(q["turn_ready"], done + h + 1)
                    if h >= 2:
                        act.wait_ge(q["head_ready"], done + h - 1)
                    at = 1024 + h % 2 * 512
                    f(S[:, at:at + 512], bank[2 + h % 2][:, :], ACT.Copy).then_inc(q["turned_ready"], 1)
                    if h % 2 and h >= 3:
                        keep_pair((h - 3) // 2)
                keep_pair(heads // 2 - 1)

            cats = [0]

            def cat_hi(cat):
                cats[0] += 1
                for k in range(4):
                    last = f(XH[:, 2 * k:2 * k + 2, :], cat[:, 2 * k:2 * k + 2, :], ACT.Copy)
                    last.then_inc(q["cat_hi"], 1)

            split_hi(0)
            act.wait_ge(q["zero_ready"], 1)
            act.wait_ge(q["par_loaded"], 48)
            norm("pa_in", then=ACT.Silu)
            act.wait_ge(q["cond_loaded"], 16)
            f(cond[:, :], cond[:, :], ACT.Silu).then_inc(q["cond_ready"], 1)

            for s in range(8):
                split_hi(s + 2)
                act.wait_ge(q["slab_used"], s + 1)
                if s < 2:
                    if s == 0:
                        act.wait_ge(q["pool_steps"], 1)
                    f(UP[:, 0, 2 * s:2 * s + 2, PAD:PAD + T],
                      bank[s % 4][:, :].rearrange("p (a t) -> p a t", a=2), ACT.Copy).then_inc(evacuated[s % 2], 1)
                elif s < 6:
                    f(S[:, (s - 2) * 512:(s - 1) * 512], bank[s % 4][:, :],
                      ACT.Square).then_inc(q["qk_squares"], 1)
                else:
                    f(VRAW[:, 2 * (s - 6):2 * (s - 5), :],
                      bank[s % 4][:, :].rearrange("p (a t) -> p a t", a=2), ACT.Copy).then_inc(evacuated[s % 2], 1)
                if 3 <= s <= 6:
                    at = 2048 + (s - 3) * 512
                    act.wait_ge(q["qk_var"], s - 2)
                    f(S[:, at:at + 512], S[:, at:at + 512], ACT.Sqrt).then_inc(q["qk_norm"], 1)
            act.wait_ge(q["v_turned"], 1)
            for j in range(2):
                last = f(VT1[:, j, :], bank[2 + j][:, :], ACT.Copy)
            last.then_inc(q["vt_ready"], 1)
            attention(0, HEADS1, HD1 ** -0.5,
                      lambda h, j: S[:, h % 2 * 512 + j * T:h % 2 * 512 + (j + 1) * T],
                      lambda p: CAT1[:, 4 + p, :], 0)
            act.wait_ge(q["pool_mixed"], 1)
            for g in range(4):
                last = f(CAT1[:, g, :], bank[6 + g // 2][:, g % 2 * T:(g % 2 + 1) * T], ACT.Copy,
                         scale=col("pool_scale", g))
            last.then_inc(q["act_steps"], 1)
            act.wait_ge(q["act_steps"], 1)
            act.wait_ge(q["head_kept"], 4)
            cat_hi(CAT1)
            for s in range(3):
                split_hi(N0["pa_out"] + s + 2)


            norm("f0_up", bank_of_sums=6, then=ACT.Gelu_apprx_tanh)
            conv_ffn("f0_up", 0)
            def softplus_1():
                f(tiny[:, 20:30], col_span("lam", 10), ACT.Abs).then_inc(q["act_steps"], 1)
                act.wait_ge(q["act_steps"], 2)
                f(tiny[:, 20:30], tiny[:, 20:30], ACT.Exp, scale=-1.0).then_inc(q["decay_z"], 1)
                f(tiny[:, 50:51], col("a_log"), ACT.Exp).then_inc(q["decay_z"], 1)

            def softplus_2():
                act.wait_ge(q["decay_u"], 1)
                f(tiny[:, 40:50], tiny[:, 30:40], ACT.Ln).then_inc(q["decay_l"], 1)

            down_stage("f0_down", {3: softplus_1, 4: softplus_2})

            norm("rg_in", then=ACT.Gelu_apprx_tanh)

            def gate_tanhs(s):
                act.wait_ge(q["ri_ready"], s + 1)
                f(A1[:, s, :], bank[4 + s % 2][:, 0:T], ACT.Tanh, scale=0.5,
                  bias=c4[:, 2 * RNN + s:2 * RNN + s + 1])
                f(S[:, 512 + s % 2 * T:512 + (s % 2 + 1) * T], bank[4 + s % 2][:, T:2 * T], ACT.Tanh,
                  scale=0.5, bias=c4[:, 3 * RNN + s:3 * RNN + s + 1]).then_inc(q["it_ready"], 1)

            act.wait_ge(q["c4_ready"], 1)
            for s in range(RNN):
                n = N0["rg_in"] + s
                split_hi(n + 2)
                act.wait_ge(q["slab_used"], n + 1)
                f(GG[:, s, :], bank[n % 4][:, 0:T], ACT.Gelu_apprx_tanh).then_inc(q["act_steps"], 1)
                if s >= 2:
                    act.wait_ge(q["ix_ready"], s - 1)
                f(S[:, s % 2 * T:(s % 2 + 1) * T], bank[n % 4][:, T:2 * T], ACT.Identity,
                  scale=col("rconv", 30 + s), bias=col("rconvb", s)).then_inc(q["lin_ready"], 1)
                if s:
                    gate_tanhs(s - 1)
            gate_tanhs(RNN - 1)
            act.wait_ge(q["it_ready"], RNN)
            for s in range(RNN):
                at = 1024 + s * T
                f(S[:, at:at + T], A1[:, s, :], ACT.Tanh, scale=c4[:, s:s + 1],
                  bias=c4[:, s:s + 1]).then_inc(q["act_steps"], 1)
                act.wait_ge(q["act_steps"], 2 + RNN + s + 1)
                f(A1[:, s, :], A1[:, s, :], ACT.Exp, scale=c4[:, RNN + s:RNN + s + 1],
                  bias=c4[:, RNN + s:RNN + s + 1]).then_inc(q["rg_exp"], 1)
            for s in range(RNN):
                at = 1024 + s * T
                act.wait_ge(q["rg_arg"], s + 1)
                f(S[:, at:at + T], S[:, at:at + T], ACT.Sqrt).then_inc(q["rg_root"], 1)
            down_stage("rg_out")

            norm("f1_up", then=ACT.Gelu_apprx_tanh)
            conv_ffn("f1_up", 1)
            down_stage("f1_down")

            act.wait_ge(q["mod_ready"], 1)
            norm("g00_up", 0, 0, then=ACT.Silu)
            gated_ffn("g00_up")

            def rope_table():
                act.wait_ge(q["angle_ready"], 1)
                f(CS[:, :], CS[:, :], ACT.Sin).then_inc(q["table_ready"], 1)

            down_stage("g00_down", {4: rope_table})

            norm("ssd_in", 0, 24, then=ACT.Silu)

            def ssd_silu(s):
                e, v = up_count("ssd_in", s)
                act.wait_ge(e, v)
                dst = (A2 if s < 8 else XS)[:, 2 * (s % 8):2 * (s % 8) + 2, :]
                f(dst, S[:, s % 2 * 512:(s % 2 + 1) * 512].rearrange("p (a t) -> p a t", a=2),
                  ACT.Silu).then_inc(q["silu_ready"], 1)

            for s in range(25):
                n = N0["ssd_in"] + s
                split_hi(n + 2)
                act.wait_ge(q["slab_used"], n + 1)
                if s < 16:
                    if s >= 2:
                        act.wait_ge(q["silu_ready"], s - 1)
                    for m in range(2):
                        last = f(S[:, s % 2 * 512 + m * T:s % 2 * 512 + (m + 1) * T],
                                 bank[n % 4][:, m * T:(m + 1) * T], ACT.Identity,
                                 scale=col("sconv", 64 + 2 * s + m), bias=col("sconvb", 2 * s + m))
                    last.then_inc(q["lin_ready"], 1)
                    if s:
                        ssd_silu(s - 1)
                elif s == 16:
                    ssd_silu(15)
                    f(S[0:64, 2048:2304], bank[n % 4][0:64, 0:T], ACT.Identity,
                      bias=PAR[0:64, COL["dt_bias"]:COL["dt_bias"] + 1]).then_inc(evacuated[0], 1)
                else:
                    f(A1[:, 2 * (s - 17):2 * (s - 16), :],
                      bank[n % 4][:, :].rearrange("p (a t) -> p a t", a=2), ACT.Silu).then_inc(evacuated[s % 2], 1)
                if s == 17:
                    act.wait_ge(evacuated[0], EV0["ssd_in"] + 9)
                    f(S[0:64, 2304:2560], S[0:64, 2048:2304], ACT.Abs).then_inc(q["act_steps"], 1)
                    act.wait_ge(q["act_steps"], 2 + 2 * RNN + 1)
                    f(S[0:64, 2304:2560], S[0:64, 2304:2560], ACT.Exp, scale=-1.0).then_inc(q["dt_z"], 1)
                if s == 18:
                    act.wait_ge(q["dt_u"], 1)
                    f(S[0:64, 2816:3072], S[0:64, 2560:2816], ACT.Ln).then_inc(q["dt_log"], 1)
            act.wait_ge(q["cols_ready"], 1)
            for h in range(SSD_H):
                act.wait_ge(q["expo_ready"], h + 1)
                if h >= 2:
                    act.wait_ge(q["mt_ready"], h - 1)
                b, E = 2 + 2 * (h % 2), EX[:, h % 2]
                f(E[:, 0:2, :].rearrange("p a t -> p (a t)"), bank[b][:, 0:T], ACT.Exp, bias=cols[:, 2, h:h + 1])
                f(E[:, 3, :], bank[b][:, T:T + P], ACT.Exp, bias=cols[:, 3, h:h + 1])
                f(E[:, 4, :], bank[b + 1][:, 0:P], ACT.Exp, bias=cols[:, 2, 32 + h:33 + h])
                f(E[:, 2:6:3, :], bank[b + 1][:, P:3 * P].rearrange("p (a t) -> p a t", a=2), ACT.Exp,
                  bias=cols[:, 3, 32 + h:33 + h]).then_inc(q["decay_ready"], 1)
            for g in range(SSD_G):
                act.wait_ge(q["yz_ready"], 2 * g + 2)
                if g == 0:
                    act.wait_ge(q["yz_ready"], 16)
                f(S[:, 2 * g * T:2 * (g + 1) * T].rearrange("p (a t) -> p a t", a=2),
                  A1[:, 2 * g:2 * g + 2, :], ACT.Square).then_inc(q["ysq_ready"], 1)
            for b in range(4):
                act.wait_ge(q["yvar_ready"], b + 1)
                v = A2[:, 2 * b:2 * b + 2, :]
                f(v, v, ACT.Sqrt).then_inc(q["yroot_ready"], 1)
            for g in range(SSD_G):
                act.wait_ge(q["yn_ready"], g + 1)
                f(HH[:, 2 * g:2 * g + 2, :], A1[:, 2 * g:2 * g + 2, :], ACT.Copy).then_inc(q["yh_ready"], 1)
            down_stage("ssd_out")

            norm("g01_up", 0, 48, then=ACT.Silu)
            gated_ffn("g01_up")
            down_stage("g01_down")
            act.wait_ge(q["mod_ready"], 2)
            norm("g10_up", 1, 0, then=ACT.Silu)
            gated_ffn("g10_up")
            down_stage("g10_down")

            norm("mla_in", 1, 24)
            for s in range(3):
                n = N0["mla_in"] + s
                split_hi(n + 2)
                act.wait_ge(q["slab_used"], n + 1)
                two = bank[n % 4][:, :].rearrange("p (a t) -> p a t", a=2)
                f(A1[:, 2 * s:2 * s + 2, :], two, ACT.Copy).then_inc(evacuated[s % 2], 1)
                f(S[:, 2 * s * T:2 * (s + 1) * T].rearrange("p (a t) -> p a t", a=2), two,
                  ACT.Square).then_inc(q["lat_kept"], 1)
            act.wait_ge(q["lat_var"], 1)
            f(R[:, :], R[:, :], ACT.Sqrt).then_inc(q["lat_root"], 1)
            for k in range(5):
                act.wait_ge(q["lat_scaled"], k + 1)
                f(XH[:, k, :], A1[:, k, :], ACT.Copy).then_inc(q["lat_hi"], 1)

            def mq_root(u):
                act.wait_ge(q["mq_var"], u + 1)
                at = 2048 + u % 2 * 512
                f(S[:, at:at + 512], S[:, at:at + 512], ACT.Sqrt).then_inc(q["mq_root"], 1)

            for u in range(8):
                n = N0["mla_uq"] + u // 2
                if u % 2 == 0:
                    split_hi(n + 2)
                    act.wait_ge(q["first_queries"], u // 2 + 1)
                else:
                    act.wait_ge(q["slab_used"], n + 1)
                if u >= 2:
                    mq_root(u - 2)
                    act.wait_ge(q["mq_ready"], u - 1)
                src = bank[u // 2 % 2 * 2 + u % 2]
                f(S[:, u % 2 * 512:u % 2 * 512 + 512], src[:, :], ACT.Square)
                f(S[:, 1024 + u % 2 * 512:1536 + u % 2 * 512], src[:, :], ACT.Copy,
                  scale=col("mqh")).then_inc(q["mq_kept"], 1)
            mq_root(6)
            mq_root(7)

            def mk_root(u):
                act.wait_ge(q["mk_var"], u + 1)
                at = 2048 + u % 2 * 512
                f(S[:, at:at + 512], S[:, at:at + 512], ACT.Sqrt).then_inc(q["mk_root"], 1)

            for u in range(8):
                n = N0["mla_ukv"] + u // 4
                if u:
                    mk_root(u - 1)
                if u % 4 == 0:
                    split_hi(n + 2)
                    act.wait_ge(q["slab_used"], n + 1)
                if u == 0:
                    act.wait_ge(q["mq_sum"], 8)
                if u >= 2:
                    act.wait_ge(q["mk_sum"], u - 1)
                src = bank[u % 4]
                f(S[0:64, u % 2 * 512:u % 2 * 512 + 512], src[0:64, :], ACT.Square)
                f(A1[64:P, 2 * u:2 * u + 2, :], src[64:P, :].rearrange("p (a t) -> p a t", a=2),
                  ACT.Copy).then_inc(q["mk_kept"], 1)
            mk_root(7)
            act.wait_ge(q["mk_ready"], 8)
            attention(HEADS1, MLA_H, 96 ** -0.5,
                      lambda h, j: bank[h % 2][:, j * T:(j + 1) * T],
                      lambda p: A1[:, p, :], HEADS1 // 2)
            act.wait_ge(q["head_kept"], 12)
            cat_hi(A1)
            for s in range(3):
                split_hi(N0["mla_out"] + s + 2)

            norm("g11_up", 1, 48, 6, ACT.Silu)
            gated_ffn("g11_up")
            down_stage("g11_down")

        @block.vector
        def _(dve):
            v = nc.vector
            step = Steps(dve, q["vec_steps"])
            stt = v.scalar_tensor_tensor

            def two(ap, a=2):
                return ap.rearrange("p (a t) -> p a t", a=a)

            def split_lo(n, i=None, halves=(0, 1)):
                if n >= NSLABS:
                    return
                for h in halves:
                    dve.wait_ge(q["hi_ready"], plus(2 * n + h + 1, i, 8))
                    at = slice(h * HALF, (h + 1) * HALF)
                    v.tensor_tensor(lo[:, n % SPLIT, at], raw[:, n % RAW, at],
                                    hi[:, n % SPLIT, at].bitcast(F32), ALU.subtract).then_inc(q["lo_ready"], 1)

            def down_stage(stage, between={}):
                loops = SLABS[stage] // 4 if SLABS[stage] > 8 and not between else 0
                if loops:
                    with dve.Fori(0, loops) as i:
                        for s in range(4):
                            split_lo(N0[stage] + s + 2, i)
                for s in range(4 * loops, SLABS[stage] - 2):
                    split_lo(N0[stage] + s + 2)
                    if s in between:
                        between[s]()

            def fold_squares(k):
                for pair in (1, 2):
                    dve.wait_ge(q["squares_ready"], 8 * k + 2 * pair + 2)
                    last = v.tensor_tensor(S[:, 0:2 * T], S[:, 0:2 * T], S[:, 2 * pair * T:2 * (pair + 1) * T],
                                           ALU.add)
                    if pair == 1:
                        step.link(last)
                last.then_inc(q["squares_folded"], 1)

            def residual(stage, gate=None, more=True):
                following = N0[stage] + SLABS[stage]
                if stage in HID:
                    split_lo(following, halves=(0,))
                for k in range(4):
                    if k == 3 and more:
                        fold_squares(norms[0])
                    if stage in HID:
                        b = 4 + k
                        if k < 3:
                            dve.wait_ge(q["pair_summed"], 3 * SUMS[stage] // 4 + k + 1)
                        else:
                            dve.wait_ge(q["slab_used"], N0[stage] + SLABS[stage])
                    else:
                        n = N0[stage] + k
                        b = n % 4
                        if k < 3:
                            split_lo(n + 2, halves=(0, 1) if k < 2 else (0,))
                        dve.wait_ge(q["slab_used"], n + 1)
                    if gate is None and k < 3:
                        v.tensor_tensor(X[:, 2 * k:2 * k + 2, :], two(bank[b][:, :]), X[:, 2 * k:2 * k + 2, :],
                                        ALU.add).then_inc(q["resid_ready"], 2)
                    elif gate is None:
                        for m in (6, 7):
                            v.tensor_tensor(X[:, m, :], bank[b][:, m % 2 * T:(m % 2 + 1) * T], X[:, m, :],
                                            ALU.add).then_inc(q["resid_ready"], 1)
                    else:
                        for m in (2 * k, 2 * k + 1):
                            stt(out=X[:, m, :], in0=bank[b][:, m % 2 * T:(m % 2 + 1) * T],
                                scalar=GT[:, gate + m:gate + m + 1], in1=X[:, m, :],
                                op0=ALU.mult, op1=ALU.add).then_inc(q["resid_ready"], 1)
                split_lo(following, halves=(1,))

            norms = [0]

            def norm(stage, gain=None, shift=None):
                k = norms[0]
                norms[0] += 1
                dve.wait_ge(q["norm_ready"], k + 1)
                step.link(v.reciprocal(tiny[:, 54:56], tiny[:, 52:54]))
                for j in range(2):
                    last = v.tensor_scalar(R[:, j * P:(j + 1) * P], ident, tiny[:, 54 + j:55 + j], None, ALU.mult)
                last.then_inc(q["diag_ready"], 1)
                dve.wait_ge(q["spread_ready"], k + 1)

                def rest(kt):
                    dve.wait_ge(q["xh_ready"], 8 * k + kt + 1)
                    high = XH[:, kt, :].bitcast(F32)
                    if shift is None:
                        last = v.tensor_tensor(XL[:, kt, :], S[:, kt * T:(kt + 1) * T], high, ALU.subtract)
                    else:
                        last = stt(out=XL[:, kt, :], in0=S[:, kt * T:(kt + 1) * T],
                                   scalar=MOD[:, shift + kt:shift + kt + 1], in1=high,
                                   op0=ALU.add, op1=ALU.subtract)
                    last.then_inc(q["x_ready"], 1)

                for kt in range(KD):
                    g = col(gain, kt) if shift is None else MG[:, gain + kt:gain + kt + 1]
                    stt(out=S[:, kt * T:(kt + 1) * T], in0=X[:, kt, :], scalar=g, in1=bank[4][:, 0:T],
                        op0=ALU.mult, op1=ALU.mult).then_inc(q["scaled_ready"], 1)
                    if kt >= 2:
                        rest(kt - 2)
                rest(KD - 2)
                rest(KD - 1)
                split_lo(N0[stage] + 1)

            def modulation(layer):
                dve.wait_ge(q["mod_summed"], 72 * (layer + 1))
                M = MOD[:, 72 * layer:72 * layer + 72]
                step.link(v.tensor_reduce(M, modp[:, :, :], AX.X, ALU.add))
                v.tensor_tensor(M, M, col_span("bmod", 72, 72 * layer), ALU.add).then_inc(q["mod_taken"], 1)
                dve.wait_ge(q["mod_taken"], layer + 1)
                for sub in range(3):
                    at = 24 * layer + 8 * sub
                    stt(out=MG[:, at:at + 8], in0=M[:, 24 * sub + 8:24 * sub + 16], scalar=1.0,
                        in1=col_span("ng", 8, at), op0=ALU.add, op1=ALU.mult)
                    last = v.tensor_scalar(GT[:, at:at + 8], M[:, 24 * sub + 16:24 * sub + 24],
                                           1.0 if sub == 1 else 0.5, None, ALU.mult)
                last.then_inc(q["mod_ready"], 1)
                dve.wait_ge(q["mod_ready"], layer + 1)

            def hidden(buf, stage, p, i=None, made=None):
                at = 2 * p
                hh, hl = ((HH[:, at:at + 2, :], HL[:, at:at + 2, :]) if i is None else
                          (HH[:, bass.ds(i * 4 + at, 2), :], HL[:, bass.ds(i * 4 + at, 2), :]))
                step.link(made)
                step.link(v.tensor_copy(hh, two(buf)))
                v.tensor_tensor(hl, two(buf), hh.bitcast(F32), ALU.subtract).then_inc(q["h_ready"], 1)

            def conv_ffn(stage, layer, gelus):
                def pair(p, i=None):
                    b = p % 2
                    for side in range(2):
                        n = N0[stage] + 2 * p + side
                        split_lo(n + 2, i)
                        dve.wait_ge(q["lin_ready"], plus(LIN[stage] + 2 * p + side + 1, i, 4))
                        marks = []
                        for tap in (1, 2):
                            for m in range(2):
                                k = 2 * p + m + 22 * side
                                at = b * 1024 + side * 512 + m * T
                                z = S[:, at + tap:at + T]
                                if tap == 2:
                                    step.wait(marks[m])
                                last = stt(out=z, in0=bank[n % 4][:, m * T:(m + 1) * T - tap],
                                           scalar=col(f"fconv{layer}", (2 - tap) * 44 + k, i, 4), in1=z,
                                           op0=ALU.mult, op1=ALU.add)
                                if tap == 1:
                                    marks.append(step.put(last))
                        last.then_inc(evacuated[side], 1)
                    dve.wait_ge(q["gelu_ready"], plus(gelus + p + 1, i, 2))
                    e, val = up_count(stage, 2 * p)
                    dve.wait_ge(e, plus(val, i, 2))
                    buf = S[:, 3072 + b * 512:3584 + b * 512]
                    hidden(buf, stage, p, i, v.tensor_tensor(
                        buf, S[:, 2048 + b * 512:2560 + b * 512], S[:, b * 1024:b * 1024 + 512], ALU.mult))

                pair(0)
                pair(1)
                with dve.Fori(0, 4) as i:
                    step.enter(i, 12)
                    pair(2, i)
                    pair(3, i)
                    step.leave(4)
                pair(10)

            def gated_ffn(stage):
                def gated_pair(p, i=None):
                    b = p % 2
                    n = N0[stage] + 2 * p
                    split_lo(n + 2, i)
                    split_lo(n + 3, i)
                    e, val = up_count(stage, 2 * p)
                    dve.wait_ge(e, plus(val, i, 2))
                    dve.wait_ge(q["slab_used"], plus(n + 2, i, 4))
                    buf = S[:, 3072 + b * 512:3584 + b * 512]
                    made = v.tensor_tensor(buf, S[:, 2048 + b * 512:2560 + b * 512], bank[(n + 1) % 4][:, :],
                                           ALU.mult)
                    step.link(made)
                    at = 2 * p
                    hh, hl = ((HH[:, at:at + 2, :], HL[:, at:at + 2, :]) if i is None else
                              (HH[:, bass.ds(i * 4 + at, 2), :], HL[:, bass.ds(i * 4 + at, 2), :]))
                    v.tensor_copy(hh, two(buf)).then_inc(evacuated[1], 1)
                    e, val = up_count(stage, 2 * p + 1)
                    dve.wait_ge(e, plus(val, i, 2))
                    v.tensor_tensor(hl, two(buf), hh.bitcast(F32), ALU.subtract).then_inc(q["h_ready"], 1)

                gated_pair(0)
                gated_pair(1)
                with dve.Fori(0, 4) as i:
                    step.enter(i, 2)
                    gated_pair(2, i)
                    gated_pair(3, i)
                    step.leave(4)
                gated_pair(10)

            def attention(done, heads, scale, slopes=None):
                def maxima(h):
                    dve.wait_ge(q["scores_ready"], done + h + 1)
                    if slopes is None:
                        s = two(bank[h % 2][:, :])
                    else:
                        if h >= 2:
                            dve.wait_ge(q["turn_ready"], done + h - 1)
                        buf = S[:, h % 2 * 512:h % 2 * 512 + 512]
                        step.link(stt(out=buf, in0=DIST, scalar=slopes[h] / scale, in1=bank[h % 2][:, :],
                                      op0=ALU.mult, op1=ALU.add))
                        s = two(buf)
                    t = tiny[:, h % 2 * 8:h % 2 * 8 + 8]
                    step.link(v.tensor_reduce(t[:, 0:2], s, AX.X, ALU.max))
                    v.tensor_scalar(t[:, 2:4], t[:, 0:2], -scale, None, ALU.mult).then_inc(q["shift_ready"], 1)

                maxima(0)
                for h in range(heads):
                    if h + 1 < heads:
                        maxima(h + 1)
                    t = tiny[:, h % 2 * 8:h % 2 * 8 + 8]
                    dve.wait_ge(q["exp_ready"], done + h + 1)
                    step.link(v.reciprocal(t[:, 6:8], t[:, 4:6]))
                    for j in range(2):
                        at = h % 2 * 512 + j * T
                        last = v.tensor_scalar(S[:, at:at + T], S[:, at:at + T], t[:, 6 + j:7 + j], None,
                                               ALU.mult)
                    last.then_inc(q["prob_ready"], 1)

            cats = [0]

            def cat_lo(cat):
                for k in range(4):
                    dve.wait_ge(q["cat_hi"], 4 * cats[0] + k + 1)
                    v.tensor_tensor(XL[:, 2 * k:2 * k + 2, :], cat[:, 2 * k:2 * k + 2, :],
                                    XH[:, 2 * k:2 * k + 2, :].bitcast(F32), ALU.subtract).then_inc(q["x_ready"], 2)
                cats[0] += 1

            def log1p_rest(z, u, lg, tmp, y, out_):
                step.link(v.tensor_scalar(tmp, u, 1.0, None, ALU.is_equal))
                step.link(stt(out=u, in0=u, scalar=-1.0, in1=tmp, op0=ALU.add, op1=ALU.add))
                step.link(v.reciprocal(u, u))
                step.link(v.tensor_tensor(lg, lg, u, ALU.mult))
                step.link(v.tensor_tensor(lg, lg, tmp, ALU.add))
                step.link(v.tensor_tensor(lg, lg, z, ALU.mult))
                return stt(out=out_, in0=y, scalar=0.0, in1=lg, op0=ALU.max, op1=ALU.add)

            v.memset(tiny[:, 60:61], 1.0)
            v.memset(tiny[:, 59:60], EPS)
            v.memset(zero[:, :], 0.0).then_inc(q["zero_ready"], 1)
            dve.wait_ge(q["par_loaded"], 48)
            v.tensor_copy(identr[:, :], ident)
            v.tensor_copy(maskr[:, :], CN[:, CON["mask_f"]:CON["mask_f"] + 2 * P]).then_inc(q["identr_ready"], 1)
            split_lo(0)
            fold_squares(0)
            norm("pa_in", "nmix0")

            def head_norm(s):
                at = 2048 + (s - 2) * 512
                dve.wait_ge(q["qk_norm"], s - 1)
                stt(out=A1[:, 2 * (s - 2):2 * (s - 1), :], in0=two(bank[s][:, :] if s < 4 else bank[s - 4][:, :]),
                    scalar=col("q_gain" if s < 4 else "k_gain"), in1=two(S[:, at:at + 512]),
                    op0=ALU.mult, op1=ALU.mult).then_inc(evacuated[s % 2], 1)

            for s in range(8):
                split_lo(s + 2)
                if 3 <= s <= 6:
                    dve.wait_ge(q["qk_sum"], s - 2)
                    at = 2048 + (s - 3) * 512
                    step.link(v.tensor_scalar(S[:, at:at + 512], bank[1 + s][:, :], 1.0 / HD1, EPS,
                                              ALU.mult, ALU.add))
                    v.reciprocal(S[:, at:at + 512], S[:, at:at + 512]).then_inc(q["qk_var"], 1)
                    head_norm(s - 1)
            dve.wait_ge(q["late_loaded"], 16 * 4)
            attention(0, HEADS1, HD1 ** -0.5, [2.0 ** -(h + 1) for h in range(HEADS1)])
            cat_lo(CAT1)
            residual("pa_out")

            norm("f0_up", "nffn0")
            conv_ffn("f0_up", 0, 0)
            z, u, lg = tiny[:, 20:30], tiny[:, 30:40], tiny[:, 40:50]

            def softplus_1():
                dve.wait_ge(q["decay_z"], 2)
                v.tensor_scalar(u, z, 1.0, None, ALU.add).then_inc(q["decay_u"], 1)

            def softplus_2():
                dve.wait_ge(q["decay_l"], 1)
                step.link(v.tensor_scalar(c4[:, 30:40], col_span("lam", 10), -1.0, None, ALU.mult))
                step.link(log1p_rest(z, u, lg, c4[:, 0:10], c4[:, 30:40], c4[:, 20:30]))
                v.tensor_scalar(c4[:, 10:20], c4[:, 20:30], -4.0, None, ALU.mult)
                step.link(v.tensor_scalar(c4[:, 0:10], c4[:, 20:30], 4.0, None, ALU.mult))
                v.tensor_scalar(c4[:, 20:30], col_span("rba", 10), 0.5, None, ALU.mult)
                v.tensor_scalar(c4[:, 30:40], col_span("rbx", 10), 0.5, None, ALU.mult).then_inc(q["c4_ready"], 1)

            down_stage("f0_down", {3: softplus_1, 4: softplus_2})
            residual("f0_down")

            norm("rg_in", "nmix1")

            def gated_input(s):
                t = S[:, 512 + s % 2 * T:512 + (s % 2 + 1) * T]
                dve.wait_ge(q["it_ready"], s + 1)
                step.link(v.tensor_scalar(t, t, 0.5, 0.5, ALU.mult, ALU.add))
                v.tensor_tensor(IX[:, s, :], t, S[:, s % 2 * T:(s % 2 + 1) * T], ALU.mult).then_inc(q["ix_ready"], 1)

            for s in range(RNN):
                n = N0["rg_in"] + s
                split_lo(n + 2)
                dve.wait_ge(q["lin_ready"], LIN["rg_in"] + s + 1)
                for tap in (1, 2, 3):
                    zt = S[:, s % 2 * T + tap:(s % 2 + 1) * T]
                    last = stt(out=zt, in0=bank[n % 4][:, T:2 * T - tap], scalar=col("rconv", (3 - tap) * 10 + s),
                               in1=zt, op0=ALU.mult, op1=ALU.add)
                    if tap < 3:
                        step.link(last)
                last.then_inc(evacuated[s % 2], 1)
                if s:
                    gated_input(s - 1)
            gated_input(RNN - 1)
            for s in range(RNN):
                a, th, sq = A1[:, s, :], S[:, 1024 + s * T:1280 + s * T], S[:, 3584 + s % 2 * T:3840 + s % 2 * T]
                dve.wait_ge(q["rg_exp"], s + 1)
                step.link(v.tensor_tensor(sq, a, a, ALU.mult))
                stt(out=th, in0=sq, scalar=1.0, in1=th, op0=ALU.add, op1=ALU.mult).then_inc(q["rg_arg"], 1)
            dve.wait_ge(q["ix_ready"], RNN)
            for s in range(RNN):
                a, th = A1[:, s, :], S[:, 1024 + s * T:1280 + s * T]
                dve.wait_ge(q["rg_root"], s + 1)
                step.link(v.tensor_tensor(th, th, IX[:, s, :], ALU.mult))
                step.link(v.tensor_tensor_scan(IX[:, s, :], a, th, 0.0, ALU.mult, ALU.add))
                step.link(v.tensor_tensor(GG[:, s, :], GG[:, s, :], IX[:, s, :], ALU.mult))
                step.link(v.tensor_copy(HH[:, s, :], GG[:, s, :]))
                last = v.tensor_tensor(HL[:, s, :], GG[:, s, :], HH[:, s, :].bitcast(F32), ALU.subtract)
                if s % 2:
                    last.then_inc(q["h_ready"], 1)
            down_stage("rg_out")
            residual("rg_out")

            norm("f1_up", "nffn1")
            conv_ffn("f1_up", 1, 11)
            modulation(0)
            down_stage("f1_down")
            residual("f1_down")

            norm("g00_up", 0, 0)
            gated_ffn("g00_up")

            def angles_1():
                step.link(v.tensor_copy(CS[:, :], posi[:, :]))
                step.link(v.tensor_scalar(CS[:, :], CS[:, :], col("inv_freq"), None, ALU.mult))
                step.link(v.tensor_scalar(R[:, 0:T], CS[:, :], con_mat("phase", 1), 1.0 / TWO_PI, ALU.add, ALU.mult))
                step.link(v.tensor_scalar(R[:, 0:T], R[:, 0:T], ROUND, None, ALU.add))
                step.link(v.tensor_scalar(R[:, 0:T], R[:, 0:T], -ROUND, None, ALU.add))

            def angles_2():
                for part in TURN:
                    step.link(stt(out=CS[:, :], in0=R[:, 0:T], scalar=-part, in1=CS[:, :], op0=ALU.mult, op1=ALU.add))
                step.link(v.tensor_scalar(CS[:, :], CS[:, :], con_mat("phase", 1), None, ALU.add))
                v.tensor_scalar(CS[:, :], CS[:, :], 3.1415925, -3.1415925, ALU.min, ALU.max).then_inc(q["angle_ready"], 1)

            def rope_table():
                dve.wait_ge(q["table_ready"], 1)
                step.link(v.tensor_scalar(CS[:, :], CS[:, :], con_mat("sign", 1), con_mat("nope", 1),
                                          ALU.mult, ALU.add))

            down_stage("g00_down", {1: angles_1, 3: angles_2, 5: rope_table})
            residual("g00_down", 0)

            norm("ssd_in", 8, 24)
            for s in range(25):
                n = N0["ssd_in"] + s
                split_lo(n + 2)
                if s < 16:
                    dve.wait_ge(q["lin_ready"], LIN["ssd_in"] + s + 1)
                    marks = [0, 0]
                    for k, d in ((0, 2), (1, 1), (3, -1), (4, -2)):
                        for m in range(2):
                            base = s % 2 * 512 + m * T
                            src = bank[n % 4][:, m * T:(m + 1) * T]
                            if d > 0:
                                zt, src = S[:, base + d:base + T], src[:, 0:T - d]
                            else:
                                zt, src = S[:, base:base + T + d], src[:, -d:T]
                            if k:
                                step.wait(marks[m])
                            last = stt(out=zt, in0=src, scalar=col("sconv", 32 * k + 2 * s + m), in1=zt,
                                       op0=ALU.mult, op1=ALU.add)
                            if k < 4:
                                marks[m] = step.put(last)
                    last.then_inc(evacuated[s % 2], 1)
                if s in (18, 19):
                    for r in range(4 * (s - 18), 4 * (s - 17)):
                        dve.wait_ge(q["xs_turn"], r + 1)
                        v.tensor_copy(XST[:, r % 2, r // 2 * 4:r // 2 * 4 + 4, :],
                                      bank[4 + r % 4][:, :].rearrange("p (a t) -> p a t", a=4)).then_inc(q["xs_turned"], 1)
                if s == 17:
                    dve.wait_ge(q["dt_z"], 1)
                    v.tensor_scalar(S[0:64, 2560:2816], S[0:64, 2304:2560], 1.0, None,
                                    ALU.add).then_inc(q["dt_u"], 1)
                if s == 20:
                    dve.wait_ge(q["dt_log"], 1)
                    y, z2, u2, l2, t2, o2 = (S[0:64, at:at + T] for at in (2048, 2304, 2560, 2816, 3072, 3328))
                    step.link(log1p_rest(z2, u2, l2, t2, y, o2))
                    step.link(v.tensor_copy(y, o2))
                    step.link(v.tensor_scalar(t2, y, tiny[0:64, 50:51], -1.0, ALU.mult, ALU.mult))
                    step.link(v.memset(u2, 1.0))
                    v.tensor_tensor_scan(z2[0:32, :], u2[0:32, :], t2[0:32, :], 0.0, ALU.mult, ALU.add)
                    step.link(v.tensor_tensor_scan(z2[32:64, ::-1], u2[32:64, :], t2[32:64, ::-1], 0.0,
                                                   ALU.mult, ALU.add))
                    step.link(v.tensor_copy(acr[:, 0, :], z2))
                    v.tensor_tensor(acr[:, 1, :], z2, acr[:, 0, :].bitcast(F32),
                                    ALU.subtract).then_inc(q["exponents_ready"], 1)
            dve.wait_ge(q["col_turn"], 1)
            v.tensor_copy(cols[:, 0:2, :], bank[4][:, 0:128].rearrange("p (a t) -> p a t", a=2))
            v.tensor_scalar(cols[:, 2:4, :], bank[4][:, 128:256].rearrange("p (a t) -> p a t", a=2), -1.0, None,
                            ALU.mult).then_inc(q["cols_ready"], 1)
            dve.wait_ge(q["cols_ready"], 1)

            def gate_y(pair):
                t = S[:, 2048 + pair % 2 * T:2048 + (pair % 2 + 1) * T]
                dve.wait_ge(q["y_ready"], 2 * pair + 2)
                step.link(stt(out=t, in0=XS[:, pair, :], scalar=col("skip", pair),
                              in1=bank[6 + pair % 2][:, 0:T], op0=ALU.mult, op1=ALU.add))
                v.tensor_tensor(A1[:, pair, :], A1[:, pair, :], t, ALU.mult).then_inc(q["yz_ready"], 1)

            for h in range(SSD_H):
                E, g = EX[:, h % 2], h // 4
                dve.wait_ge(q["decay_ready"], h + 1)
                a = v.tensor_scalar(E[:, 4, :], E[:, 4, :], cols[:, 0, 32 + h:33 + h], None, ALU.mult)
                m4 = step.put(a)
                m5 = step.put(v.tensor_scalar(E[:, 5, :], E[:, 5, :], cols[:, 1, 32 + h:33 + h], None, ALU.mult))
                v.tensor_scalar(E[:, 1, :], E[:, 1, :], cols[:, 0, h:h + 1], None, ALU.mult)
                v.tensor_scalar(E[:, 2, :], E[:, 2, :], cols[:, 1, 32 + h:33 + h], None, ALU.mult)
                step.wait(m4)
                stt(out=E[:, 0, :], in0=E[:, 0, :], scalar=cols[:, 0, h:h + 1], in1=E[:, 4, :],
                    op0=ALU.mult, op1=ALU.add)
                step.wait(m5)
                step.link(stt(out=E[:, 3, :], in0=E[:, 3, :], scalar=cols[:, 1, h:h + 1], in1=E[:, 5, :],
                              op0=ALU.mult, op1=ALU.add))
                if h % 4 == 0:
                    dve.wait_ge(q["cb_ready"], g + 1)
                if h >= 2:
                    dve.wait_ge(q["y_ready"], h - 1)
                v.tensor_tensor(MT[:, h % 2], E[:, 0:4, :].rearrange("p (j a) t -> p j (a t)", j=2),
                                two(bank[g % 2][:, :]), ALU.mult).then_inc(q["mt_ready"], 1)
                if h % 2 == 0 and h:
                    gate_y(h // 2 - 1)
            gate_y(15)
            for b in range(4):
                r = A2[:, 2 * b:2 * b + 2, :]
                dve.wait_ge(q["ysum_ready"], b + 1)
                step.link(v.tensor_scalar(r, two(bank[b][:, :]), 1.0 / 256, EPS, ALU.mult, ALU.add))
                v.reciprocal(r, r).then_inc(q["yvar_ready"], 1)
            for g in range(SSD_G):
                dve.wait_ge(q["yroot_ready"], g // 2 + 1)
                for k in (2 * g, 2 * g + 1):
                    last = stt(out=A1[:, k, :], in0=A1[:, k, :], scalar=col("snorm", k), in1=A2[:, g, :],
                               op0=ALU.mult, op1=ALU.mult)
                last.then_inc(q["yn_ready"], 1)
            for g in range(SSD_G):
                dve.wait_ge(q["yh_ready"], g + 1)
                v.tensor_tensor(HL[:, 2 * g:2 * g + 2, :], A1[:, 2 * g:2 * g + 2, :],
                                HH[:, 2 * g:2 * g + 2, :].bitcast(F32), ALU.subtract).then_inc(q["h_ready"], 1)
            down_stage("ssd_out")
            residual("ssd_out", 8)

            norm("g01_up", 16, 48)
            gated_ffn("g01_up")
            modulation(1)
            down_stage("g01_down")
            residual("g01_down", 16)
            norm("g10_up", 24, 72)
            gated_ffn("g10_up")
            down_stage("g10_down")
            residual("g10_down", 24)

            norm("mla_in", 32, 96)
            for s in range(3):
                split_lo(N0["mla_in"] + s + 2)
            dve.wait_ge(q["lat_sum"], 1)
            v.tensor_scalar(R[:, 0:T], bank[4][:, 0:T], 1.0 / 384, EPS, ALU.mult, ALU.add)
            step.link(v.tensor_scalar(R[:, T:2 * T], bank[4][:, T:2 * T], 1.0 / 256, EPS, ALU.mult, ALU.add))
            v.reciprocal(R[:, :], R[:, :]).then_inc(q["lat_var"], 1)
            step.link(v.tensor_copy(KPS, bank[5][:, 0:T]))
            v5 = A1[:, 5, :]
            step.link(v.tensor_scalar(v5, v5, col("mkh"), None, ALU.mult))
            v.tensor_tensor(v5, v5, CS[:, :], ALU.mult).then_inc(q["pe_scaled"], 1)
            dve.wait_ge(q["lat_root"], 1)
            for k in range(5):
                g = col("mqn", k) if k < 3 else col("mkn", k - 3)
                rr = R[:, 0:T] if k < 3 else R[:, T:2 * T]
                stt(out=A1[:, k, :], in0=A1[:, k, :], scalar=g, in1=rr, op0=ALU.mult,
                    op1=ALU.mult).then_inc(q["lat_scaled"], 1)
            for k in range(5):
                dve.wait_ge(q["lat_hi"], k + 1)
                v.tensor_tensor(XL[:, k, :], A1[:, k, :], XH[:, k, :].bitcast(F32),
                                ALU.subtract).then_inc(q["x_ready"], 1 if k < 4 else 4)
            dve.wait_ge(q["rope_summed"], 1)
            step.link(v.tensor_copy(KR[64:P, :], bank[6][64:P, 0:T]))

            def over_two(ap):
                return ap.rearrange("p (a t) -> p a t", a=1).to_broadcast([ap.shape[0], 2, T])

            for u in range(8):
                if u % 2 == 0:
                    split_lo(N0["mla_uq"] + u // 2 + 2)
                r = S[:, 2048 + u % 2 * 512:2560 + u % 2 * 512]
                t = S[:, 1024 + u % 2 * 512:1536 + u % 2 * 512]
                dve.wait_ge(q["mq_sum"], u + 1)
                step.link(v.tensor_scalar(r, bank[4 + u % 2][:, :], 1.0 / 96, EPS, ALU.mult, ALU.add))
                v.reciprocal(r, r).then_inc(q["mq_var"], 1)
                step.link(v.tensor_tensor(two(t), two(t), over_two(CS[:, :]), ALU.mult))
                dve.wait_ge(q["mq_root"], u + 1)
                v.tensor_tensor(QH[:, 2 * u:2 * u + 2, :], two(t), two(r), ALU.mult).then_inc(q["mq_ready"], 1)
            for u in range(8):
                if u % 4 == 0:
                    split_lo(N0["mla_ukv"] + u // 4 + 2)
                r = S[:, 2048 + u % 2 * 512:2560 + u % 2 * 512]
                dve.wait_ge(q["mk_sum"], u + 1)
                step.link(v.tensor_tensor(two(r), two(bank[4 + u % 2][:, :]), over_two(KPS), ALU.add))
                step.link(v.tensor_scalar(r, r, 1.0 / 96, EPS, ALU.mult, ALU.add))
                v.reciprocal(r, r).then_inc(q["mk_var"], 1)
                dve.wait_ge(q["mk_root"], u + 1)
                stt(out=KH[0:64, 2 * u:2 * u + 2, :], in0=two(bank[u % 4][0:64, :]),
                    scalar=PAR[0:64, COL["mkh"]:COL["mkh"] + 1], in1=two(r[0:64, :]), op0=ALU.mult, op1=ALU.mult)
                v.tensor_tensor(KH[64:P, 2 * u:2 * u + 2, :], over_two(KR[64:P, :]), two(r[64:P, :]),
                                ALU.mult).then_inc(q["mk_ready"], 1)
            for r in range(4):
                j, half = r % 2, r // 2
                dve.wait_ge(q["mv_turn"], r + 1)
                v.tensor_copy(VT2[:, j, half * 512:(half + 1) * 512], bank[6 + r % 2][:, :]).then_inc(q["mv_turned"], 1)
            attention(HEADS1, MLA_H, 96 ** -0.5)
            cat_lo(A1)
            residual("mla_out", 32)

            norm("g11_up", 40, 120)
            gated_ffn("g11_up")
            down_stage("g11_down")
            residual("g11_down", 40, more=False)

        @block.gpsimd
        def _(pool):
            g = nc.gpsimd
            step = Steps(pool, q["pool_steps"])
            step.link(g.memset(UP[:, :, :, 0:PAD], 0.0))
            pool.dma_start(cond[:, :], cvec).then_inc(q["cond_loaded"], 16)
            pool.dma_start(posi[:, :], pos).then_inc(q["late_loaded"], 16)
            pool.dma_start(A2[:, 0:12, :].rearrange("p a t -> p (a t)"), small).then_inc(q["late_loaded"], 16)
            pool.dma_start(A2[:, 12:16, :].rearrange("p a t -> p (a t)"), tab[:, 0:4 * T]).then_inc(q["late_loaded"], 16)
            pool.dma_start(DIST, tab[:, 4 * T:6 * T]).then_inc(q["late_loaded"], 16)
            for k in range(2):
                pool.dma_start(modw[:, k, :], wmod[k]).then_inc(mod_loaded[k], 16)
            for e in evacuated:
                pool.wait_ge(e, 1)
            src = UP[:, 0]
            for lvl in range(4):
                w = 1 << lvl
                dst = UP[:, 1 + lvl % 2]
                prev = src if lvl == 0 else UP[:, 1 + (lvl - 1) % 2]
                if lvl == 0:
                    step.link(g.tensor_tensor(dst[:, :, PAD:], prev[:, :, PAD:], prev[:, :, PAD - w:PAD - w + T], ALU.add))
                else:
                    step.link(g.tensor_tensor(dst[:, lvl:, PAD:], prev[:, lvl:, PAD:],
                                              prev[:, lvl:, PAD - w:PAD - w + T], ALU.add))
            pool.wait_ge(q["late_loaded"], 16 * 4)
            for gi in range(4):
                own = UP[:, 1 + gi % 2, gi, PAD:]
                step.link(g.tensor_tensor(own, own, INV[:, gi, :], ALU.mult))
                last = g.tensor_tensor(UP[:, 0, gi, PAD:], own, UP[:, 0, gi, PAD:], ALU.subtract)
            last.then_inc(q["pooled"], 1)

            pool.wait_ge(q["cond_ready"], 1)

            def unit(k, n, i, layer, load):
                w = modw[:, k, :]
                pool.wait_ge(mod_loaded[k], plus(16 * (n // 2 + 1), i, 16))
                step.link(g.tensor_tensor(w, w, cond[:, :], ALU.mult))
                half = D // 2
                while half > 16:
                    step.link(g.tensor_tensor(w[:, 0:half], w[:, 0:half], w[:, half:2 * half], ALU.add))
                    half //= 2
                local = n - 72 * layer
                dst = (modp[:, local, :] if i is None else
                       modp[:, bass.ds(i * 2 + local, 1), :].rearrange("p a s -> p (a s)"))
                g.tensor_tensor(dst, w[:, 0:16], w[:, 16:32], ALU.add).then_inc(q["mod_summed"], 1)
                if load:
                    pool.wait_ge(q["mod_summed"], plus(n + 1, i, 2))
                    src = wmod[n + 2] if i is None else wmod[i * 2 + (n + 2)]
                    pool.dma_start(modw[:, k, :], src).then_inc(mod_loaded[k], 16)

            for layer in range(2):
                if layer:
                    pool.wait_ge(q["mod_taken"], 1)
                n0 = 72 * layer
                with pool.Fori(0, 35 + (layer == 0)) as i:
                    step.enter(i, 12)
                    unit(0, n0, i, layer, True)
                    unit(1, n0 + 1, i, layer, True)
                    step.leave(35 + (layer == 0))
                if layer:
                    unit(0, n0 + 70, None, layer, False)
                    unit(1, n0 + 71, None, layer, False)


def _feature_cols(a):
    return np.ascontiguousarray(a).reshape(-1, P).T


def _up_slabs(w):
    m = w.shape[1] // P
    t = w.reshape(KD, P, m, P).transpose(2, 1, 0, 3).reshape(m // 2, 2, P, KD * P)
    return t.transpose(0, 2, 1, 3).reshape(m // 2, P, SLAB)


def _down_slabs(w):
    k = w.shape[0] // P
    return w.reshape(k // 2, 2, P, D).transpose(0, 2, 1, 3).reshape(k // 2, P, SLAB)


def _side_by_side(a, b, each=2 * P):
    n = a.shape[1] // each
    return np.stack([a.reshape(-1, n, each), b.reshape(-1, n, each)], axis=2).reshape(a.shape[0], -1)


def _constants():
    p = np.arange(P)
    f = np.float32
    con = np.zeros((P, NCON), f)
    con[:, CON["ident"]:CON["ident"] + P] = np.eye(P, dtype=f)
    con[:, CON["ones"]:CON["ones"] + P] = 1
    con[:, CON["pair64"]:CON["pair64"] + P] = (p[:, None] // 64 == p[None, :] // 64)
    con[0:96, CON["rows96"]:CON["rows96"] + P] = 1
    con[64:96, CON["rope_rows"]:CON["rope_rows"] + P] = 1
    con[64:, CON["rope_sum"] + 64:CON["rope_sum"] + P] = (p[64:, None] % 32 == p[None, 64:] % 32)
    con[:, CON["mask_f"]:CON["mask_f"] + P] = np.where(p[None, :] >= p[:, None], 0, MASKED)
    con[:, CON["mask_b"]:CON["mask_b"] + P] = np.where(p[None, :] <= p[:, None], 0, MASKED)
    con[64:96, CON["phase"]] = np.pi / 2
    con[64:96, CON["sign"]] = 1
    con[96:112, CON["sign"]] = -1
    con[112:, CON["sign"]] = 1
    con[0:64, CON["nope"]] = 1
    t = np.arange(T)
    windows = [1 / np.minimum(t + 1, w).astype(f) for w in (2, 4, 8, 16)]
    inv = np.broadcast_to(np.concatenate(windows).astype(f), (P, 4 * T))
    rows = np.arange(T).reshape(2, P).T
    dist = np.where(t[None, None, :] <= rows[:, :, None], t[None, None, :] - rows[:, :, None], -1e30)
    tab = np.concatenate([inv, dist.reshape(P, 2 * T).astype(f)], axis=1)
    freq = np.float32(10000.0) ** (-np.arange(0, 32, 2, dtype=f) / np.float32(32))
    inv_freq = np.concatenate([np.zeros(64, f), np.tile(freq.astype(f), 4)])
    return con, np.ascontiguousarray(tab), inv_freq[:, None]


def _layout(i):
    rope = [np.arange(0, 16), np.arange(16, 32), np.arange(16, 32), np.arange(0, 16)]
    rope = np.concatenate(rope)
    rg = i["rg_w_in"][0]
    ssd = i["ssd_w_in_2"][0]
    mla = i["mla_w_in_2"][0]
    f32 = np.float32
    ssd_in = np.concatenate([ssd[:, 4096:6144], ssd[:, 2048:4096], ssd[:, 6144:6208],
                             np.zeros((D, 2 * P - 64), f32), ssd[:, 0:2048]], axis=1)
    mla_in = np.concatenate([mla[:, 0:640], np.zeros((D, 64), f32), mla[:, 640 + rope]], axis=1)
    uq = i["mla_w_uq_2"][0].reshape(3, P, MLA_H, 96)
    uq = np.concatenate([uq[..., 0:64], uq[..., 64 + rope]], axis=3)
    uq = np.concatenate([uq, np.zeros((1,) + uq.shape[1:], f32)], axis=0)
    uq = uq.transpose(2, 1, 0, 3).reshape(4, 4, P, 4 * P).transpose(0, 2, 1, 3).reshape(4, P, SLAB)
    ukv = i["mla_w_ukv_2"][0].reshape(2, P, MLA_H, P)
    ukv = ukv.transpose(2, 1, 0, 3).reshape(2, 8, P, 2 * P).transpose(0, 2, 1, 3).reshape(2, P, SLAB)

    def ffn1(layer):
        w = i["ffn_w_in"][layer]
        return [_up_slabs(_side_by_side(w[:, 0:FF], w[:, FF:])), _down_slabs(i["ffn_w_out"][layer])]

    def ffn2(layer, k):
        return [_up_slabs(_side_by_side(i["ffn_w_gate_2"][layer, k], i["ffn_w_up_2"][layer, k])),
                _down_slabs(i["ffn_w_down_2"][layer, k])]

    slabs = ([_up_slabs(i["pa_w_in"][0]), _up_slabs(i["pa_w_out"][0])] + ffn1(0)
             + [_up_slabs(_side_by_side(rg[:, 0:1280], rg[:, 1280:], P)), _down_slabs(i["rg_w_out"][0])]
             + ffn1(1) + ffn2(0, 0) + [_up_slabs(ssd_in), _down_slabs(i["ssd_w_out_2"][0])]
             + ffn2(0, 1) + ffn2(1, 0)
             + [_up_slabs(mla_in), uq, ukv, _up_slabs(i["mla_w_out_2"][0])] + ffn2(1, 1))
    slabs = np.concatenate(slabs, axis=0)
    assert slabs.shape == (NSLABS, P, SLAB), slabs.shape

    con, tab, inv_freq = _constants()
    cw, cb = i["ssd_conv_w_2"][0], i["ssd_conv_b_2"][0]

    def order(a):
        return np.concatenate([a[..., 2048:4096], a[..., 0:2048]], axis=-1)

    def rows(a):
        return np.concatenate([np.ravel(a), np.zeros(P - a.size, f32)])[:, None]

    par = {"nmix0": i["norm_mix"][0], "nmix1": i["norm_mix"][1], "nffn0": i["norm_ffn"][0],
           "nffn1": i["norm_ffn"][1], "pool_scale": i["pa_pool_scale"][0],
           "q_gain": np.tile(i["pa_q_gain"][0], 2), "k_gain": np.tile(i["pa_k_gain"][0], 2),
           "fconv0": i["ffn_conv_w"][0], "fconvb0": i["ffn_conv_b"][0],
           "fconv1": i["ffn_conv_w"][1], "fconvb1": i["ffn_conv_b"][1],
           "rconv": i["rg_conv_w"][0], "rconvb": i["rg_conv_b"][0], "rba": i["rg_b_a"][0],
           "rbx": i["rg_b_x"][0], "lam": i["rg_lambda"][0], "ng": i["norm_g_2"], "bmod": i["b_mod_2"],
           "sconv": order(cw), "sconvb": order(cb), "dt_bias": rows(i["ssd_dt_bias_2"][0]),
           "a_log": rows(i["ssd_a_log_2"][0]), "skip": np.repeat(i["ssd_d_2"][0], 64),
           "snorm": i["ssd_norm_g_2"][0], "mqn": i["mla_q_norm_g_2"][0], "mkn": i["mla_kv_norm_g_2"][0],
           "mqh": i["mla_q_head_g_2"][0][np.concatenate([np.arange(64), 64 + rope])],
           "mkh": i["mla_k_head_g_2"][0][np.concatenate([np.arange(64), 64 + rope])],
           "inv_freq": inv_freq}
    par = np.concatenate([_feature_cols(par[k]) for k in COL], axis=1)
    assert par.shape == (P, NPAR), par.shape
    small = np.concatenate([i["pa_pool_w"][0], i["rg_w_a"][0], i["rg_w_x"][0]], axis=0)
    small = small.transpose(1, 0, 2).reshape(P, 24 * P)
    return {
        "x": i["x"][0].T.reshape(KD, P, T).transpose(1, 0, 2),
        "slabs": slabs, "par": par, "con": con, "tab": tab, "small": small,
        "cvec": np.broadcast_to(i["c_2"], (P, D)), "pos": np.broadcast_to(i["positions_2"], (P, T)),
        "wmod": i["w_mod_2"].transpose(0, 2, 1).reshape(144, P, D),
    }


def kernel(**inputs):
    import concourse.bacc as bacc
    from concourse.bass_utils import run_bass_kernel_spmd

    laid = {k: np.ascontiguousarray(a) for k, a in _layout({k: np.asarray(a) for k, a in inputs.items()}).items()}
    nc = bacc.Bacc("TRN2", target_bir_lowering=False, num_devices=1,
                   dynamic_dma_scratch_size=DMA_SCRATCH)
    args = {k: nc.dram_tensor(f"{k}_dram", a.shape, mybir.dt.from_np(a.dtype), kind="ExternalInput").ap()
            for k, a in laid.items()}
    out = nc.dram_tensor("out_dram", (P, KD, T), F32, kind="ExternalOutput").ap()
    build(nc, args["x"], args["slabs"], args["par"], args["con"], args["tab"], args["small"],
          args["cvec"], args["pos"], args["wmod"], out)
    r = run_bass_kernel_spmd(nc, [{f"{k}_dram": a for k, a in laid.items()}], core_ids=[0])
    y = r.results[0]["out_dram"]
    return np.ascontiguousarray(y.transpose(1, 0, 2).reshape(D, T).T).reshape(1, T, D)
```

```python
from contextlib import ExitStack

import numpy as np

import concourse.bass as bass
from concourse import mybir

F32 = mybir.dt.float32
F32R = mybir.dt.float32r
I32 = mybir.dt.int32
BF16 = mybir.dt.bfloat16
ALU = mybir.AluOpType
ACT = mybir.ActivationFunctionType
AX = mybir.AxisListType

P = 128
T = 256
D = 1024
KD = D // P
FF = 2816
KF = FF // P
SLAB = 16 * P
RAW = 4
SPLIT = 2
HALF = SLAB // 2
RNN = 10
HEADS1, HD1 = 8, 64
SSD_H, SSD_G = 32, 8
MLA_H = 16
EPS = 1e-6
DMA_SCRATCH = 8192
MASKED = -(2.0 ** 100)

STAGES = [("pa_in", 8), ("pa_out", 4), ("f0_up", 22), ("f0_down", 11),
          ("rg_in", 10), ("rg_out", 5), ("f1_up", 22), ("f1_down", 11),
          ("g00_up", 22), ("g00_down", 11), ("ssd_in", 25), ("ssd_out", 8),
          ("g01_up", 22), ("g01_down", 11), ("g10_up", 22), ("g10_down", 11),
          ("mla_in", 3), ("mla_uq", 4), ("mla_ukv", 2), ("mla_out", 4),
          ("g11_up", 22), ("g11_down", 11)]
N0, _n = {}, 0
for _name, _s in STAGES:
    N0[_name] = _n
    _n += _s
NSLABS = _n
SLABS = dict(STAGES)
UPS = ["pa_in", "f0_up", "rg_in", "f1_up", "g00_up", "ssd_in", "g01_up", "g10_up",
       "mla_in", "g11_up"]
EV0, OD0, _e, _o = {}, {}, 0, 0
for _name in UPS:
    EV0[_name], OD0[_name] = _e, _o
    _e += (SLABS[_name] + 1) // 2
    _o += SLABS[_name] // 2

RESID, SUMS, HID, _h = {}, {}, {}, 0
for _name, _s in STAGES:
    if _name.endswith(("down", "out")):
        RESID[_name] = 8 * len(RESID)
        if _name not in ("pa_out", "mla_out"):
            HID[_name] = _h
            SUMS[_name] = 4 * len(SUMS)
            _h += _s
LIN, _l = {}, 0
for _name, _s in [("f0_up", 22), ("rg_in", 10), ("f1_up", 22), ("ssd_in", 16)]:
    LIN[_name] = _l
    _l += _s

COL, _c = {}, 0
for _name, _s in [("nmix0", 8), ("nmix1", 8), ("nffn0", 8), ("nffn1", 8), ("pool_scale", 4),
                  ("q_gain", 1), ("k_gain", 1),
                  ("fconv0", 3 * 44), ("fconvb0", 44), ("fconv1", 3 * 44), ("fconvb1", 44),
                  ("rconv", 40), ("rconvb", 10), ("rba", 10), ("rbx", 10), ("lam", 10),
                  ("ng", 48), ("bmod", 144),
                  ("sconv", 5 * 32), ("sconvb", 32), ("dt_bias", 1), ("a_log", 1), ("skip", 16),
                  ("snorm", 16), ("mqn", 3), ("mkn", 2), ("mqh", 1), ("mkh", 1), ("inv_freq", 1)]:
    COL[_name] = _c
    _c += _s
NPAR = _c
CON, _c = {}, 0
for _name, _s in [("ident", 128), ("ones", 128), ("pair64", 128), 
                  ("rope_sum", 128), ("mask_f", 128), ("mask_b", 128),
                  ("select", 64), ("phase", 1), ("sign", 1), ("nope", 1)]:
    CON[_name] = _c
    _c += _s
NCON = _c


TWO_PI = float(2 * np.pi)
ROUND = float(3 << 22)
_t1 = 6.28125
_t2 = float(np.float32(np.round((2 * np.pi - _t1) * 2 ** 22) / 2 ** 22))
TURN = (_t1, _t2, float(np.float32(2 * np.pi - _t1 - _t2)))
DOWN = {"f0_up": "f0_down", "f1_up": "f1_down", "g00_up": "g00_down", "g01_up": "g01_down",
        "g10_up": "g10_down", "g11_up": "g11_down"}


class Steps:

    def __init__(self, eng, sem):
        self.eng, self.sem, self.n, self.off = eng, sem, 0, None

    def put(self, ins):
        ins.then_inc(self.sem, 1)
        self.n += 1
        return self.n

    def wait(self, n):
        self.eng.wait_ge(self.sem, n if self.off is None else self.off + n)

    def link(self, ins):
        self.wait(self.put(ins))

    def enter(self, i, per):
        self.start, self.per, self.off = self.n, per, i * per

    def leave(self, times):
        assert self.n - self.start == self.per, (self.n - self.start, self.per)
        self.n, self.off = self.start + times * self.per, None


def plus(a, i, k):
    return a if i is None else i * k + a


def build(nc, x, slabs, par, con, tab, small, cvec, pos, wmod, out):
    with ExitStack() as ctx:
        def sb(name, shape, dt=F32):
            return ctx.enter_context(nc.sbuf_tensor(name, shape, dt))

        def sem(name):
            return ctx.enter_context(nc.semaphore(name))

        def over(name, shape, dt, at):
            return nc.alloc_sbuf_tensor_at(name, shape, dt, offset=at)

        raw = sb("raw", [P, RAW, SLAB])
        hi = sb("hi", [P, SPLIT, SLAB], F32R)
        lo = sb("lo", [P, SPLIT, SLAB], F32R)
        X = sb("X", [P, KD, T])
        XH = sb("XH", [P, KD, T], F32R)
        XL = sb("XL", [P, KD, T], F32R)
        hh_at = (nc.sbuf_base + 31) // 32 * 32
        HH = sb("HH", [P, KF, T], F32R)
        hl_at = (nc.sbuf_base + 31) // 32 * 32
        HL = sb("HL", [P, KF, T], F32R)
        A1 = sb("A1", [P, 16, T])
        A2 = sb("A2", [P, 16, T])
        S = sb("S", [P, 4096])
        PAR = sb("PAR", [P, NPAR])
        CN = sb("CN", [P, NCON])
        modw = sb("modw", [P, 2, D])
        cond = sb("cond", [P, D])
        posi = sb("posi", [P, T], I32)
        modp = sb("modp", [P, 72, 16])
        MOD = sb("MOD", [P, 2 * 72])
        MG = sb("MG", [P, 2 * 24])
        GT = sb("GT", [P, 2 * 24])
        R = sb("R", [P, 2 * T])
        c4 = sb("c4", [P, 4 * RNN])
        tiny = sb("tiny", [P, 256])
        zero = sb("zero", [1, P], BF16)
        CS = sb("CS", [P, T])
        acr = sb("acr", [P, T], F32R)
        cols = sb("cols", [P, 4, 64])
        identr = sb("identr", [P, P], F32R)
        selr = sb("selr", [P, 64], F32R)
        maskr = sb("maskr", [P, 2 * P], F32R)
        TAIL = 12 * T * 4
        GG = over("GG", [P, RNN, T], F32, hh_at + TAIL)
        IX = over("IX", [P, RNN, T], F32, hl_at + TAIL)
        XS = over("XS", [P, 16, T], F32, hh_at)
        XST = over("XST", [P, 2, 16, P], F32, hl_at)
        EX = over("EX", [P, 2, 6, P], F32, hh_at + 16 * T * 4)
        MT = over("MT", [P, 2, 2, T], F32, hl_at + 16 * T * 4)
        QH = over("QH", [P, MLA_H, T], F32, hh_at)
        KH = over("KH", [P, MLA_H, T], F32, hl_at)
        SW = A2[:, 0:12, :].rearrange("p a (b c) -> p (a b) c", c=P)
        INV = A2[:, 12:16, :]
        DIST = A1[:, 8:10, :].rearrange("p a t -> p (a t)")
        VT1 = A1[:, 10:14, :].rearrange("p (k a) t -> p k (a t)", k=2)
        VT2 = A2[:, 0:8, :].rearrange("p (k a) t -> p k (a t)", k=2)
        KPS, KR = A2[:, 8, :], A2[:, 9, :]
        PAD = 16
        UP = over("UP", [P, 3, 4, PAD + T], F32, hh_at)
        VRAW = over("VRAW", [P, 4, T], F32, hl_at)
        CAT1 = over("CAT1", [P, KD, T], F32, hl_at + 4 * T * 4)

        bank = [ctx.enter_context(nc.psum_tensor(f"bank{b}", [P, 512], F32)) for b in range(8)]


        names = """par_loaded late_loaded hi_ready lo_ready slab_used even_evacuated odd_evacuated
            x_ready h_ready pair_summed resid_ready squares_ready squares_folded sum_ready
            norm_ready diag_ready spread_ready scaled_ready xh_ready lin_ready gelu_ready
            first_queries vec_steps act_steps pool_steps identr_ready cond_ready cond_loaded
            mod_summed mod_taken mod_ready zero_ready angle_ready table_ready decay_z
            decay_u decay_l c4_ready qk_squares qk_sum qk_var qk_norm v_turned vt_ready
            pooled pool_mixed cat_hi scores_ready shift_ready exp_ready prob_ready
            turn_ready turned_ready head_ready head_kept ri_ready it_ready ix_ready rg_exp
            rg_arg rg_root silu_ready dt_z dt_u dt_log exponents_ready xs_turn xs_turned
            col_turn cols_ready cb_ready expo_ready decay_ready mt_ready y_ready yz_ready
            ysq_ready ysum_ready ysum_kept yroot_ready ydiag_ready yspread_ready yn_ready
            yh_ready decay_made lat_kept lat_sum lat_root lat_hi pe_scaled rope_summed
            mq_kept mq_sum mq_var mq_root mq_ready mk_kept mk_sum mk_var mk_root mk_diag
            mk_spread mk_ready mv_turn mv_turned out_stored""".split()
        q = {name: sem(name) for name in names}
        raw_loaded = [sem(f"raw_loaded{k}") for k in range(RAW)]
        mod_loaded = [sem(f"mod_loaded{k}") for k in range(2)]
        evacuated = (q["even_evacuated"], q["odd_evacuated"])

        block = ctx.enter_context(nc.Block())

        def col(name, k=0, i=None, step=0):
            at = COL[name] + k
            return PAR[:, at:at + 1] if i is None else PAR[:, bass.ds(i * step + at, 1)]

        def col_span(name, w, k=0):
            return PAR[:, COL[name] + k:COL[name] + k + w]

        def con_mat(name, w=P):
            return CN[:, CON[name]:CON[name] + w]

        ident, ones = con_mat("ident"), con_mat("ones")

        def up_count(name, s):
            return evacuated[s % 2], (EV0, OD0)[s % 2][name] + s // 2 + 1

        @block.sync
        def _(sp):
            sp.dma_start(X[:], x).then_inc(q["par_loaded"], 16)
            sp.dma_start(CN[:], con).then_inc(q["par_loaded"], 16)
            sp.dma_start(PAR[:], par).then_inc(q["par_loaded"], 16)

            def load(k, n, i=None):
                sp.wait_ge(q["lo_ready"], plus(2 * (n - RAW + 1), i, 2 * RAW))
                src = slabs[n] if i is None else slabs[i * RAW + n]
                sp.dma_start(raw[:, k, :], src).then_inc(raw_loaded[k], 16)

            for n in range(RAW):
                sp.dma_start(raw[:, n, :], slabs[n]).then_inc(raw_loaded[n], 16)
            loops = (NSLABS - RAW) // RAW
            with sp.Fori(0, loops) as i:
                for k in range(RAW):
                    load(k, RAW + k, i)
            for n in range(RAW + loops * RAW, NSLABS):
                load(n % RAW, n)
            for k in range(4):
                sp.wait_ge(q["resid_ready"], RESID["g11_down"] + 2 * k + 2)
                sp.dma_start(out[:, 2 * k:2 * k + 2, :], X[:, 2 * k:2 * k + 2, :]).then_inc(q["out_stored"], 16)
            sp.wait_ge(q["out_stored"], 64)

        @block.tensor
        def _(pe):
            mm = nc.tensor.matmul

            def three(dst, n, j, xh, xl, start):
                k = n % SPLIT
                wh, wl = hi[:, k, j * P:(j + 1) * P], lo[:, k, j * P:(j + 1) * P]
                mm(dst, wh, xh, start=start, stop=False, skip_group_check=True)
                mm(dst, wh, xl, start=False, stop=False, skip_group_check=True)
                return mm(dst, wl, xh, start=False, stop=False, skip_group_check=True)

            def up_slab(stage, s, i=None):
                n = N0[stage] + s
                if s >= 4 or i is not None:
                    e, v = up_count(stage, s)
                    pe.wait_ge(e, plus(v - 2, i, 2))
                for m in range(2):
                    pe.wait_ge(q["lo_ready"], plus(2 * n + m + 1, i, 8))
                    for kt in range(KD):
                        last = three(bank[n % 4][:, m * T:(m + 1) * T], n, m * KD + kt,
                                     XH[:, kt, :], XL[:, kt, :], start=(m == 0 and kt == 0))
                last.then_inc(q["slab_used"], 1)

            def first_up_slab(stage, preps):
                n = N0[stage]
                pe.wait_ge(q["lo_ready"], 2 * n + 2)
                for kt in range(KD):
                    pe.wait_ge(q["x_ready"], KD * (preps - 1) + kt + 1)
                    for m in range(2):
                        last = three(bank[n % 4][:, m * T:(m + 1) * T], n, m * KD + kt,
                                     XH[:, kt, :], XL[:, kt, :], start=(m == 0 and kt == 0))
                last.then_inc(q["slab_used"], 1)

            def up_stage(stage, preps, between=None):
                loops = SLABS[stage] // 4 - 1 if SLABS[stage] >= 16 and between is None else 0
                first_up_slab(stage, preps)
                for s in range(1, 4 if loops else SLABS[stage]):
                    up_slab(stage, s)
                    if between is not None:
                        between(s)
                if loops:
                    with pe.Fori(0, loops) as i:
                        for s in range(4, 8):
                            up_slab(stage, s, i)
                    for s in range(4 + 4 * loops, SLABS[stage]):
                        up_slab(stage, s)

            def down_slab(stage, s, i=None):
                n = N0[stage] + s
                pe.wait_ge(q["h_ready"], plus(HID[stage] + s + 1, i, 4))
                for kk in range(2):
                    pe.wait_ge(q["lo_ready"], plus(2 * n + kk + 1, i, 8))
                    for m in range(KD):
                        if i is None:
                            xh, xl = HH[:, 2 * s + kk, :], HL[:, 2 * s + kk, :]
                        else:
                            xh = HH[:, bass.ds(i * 8 + 2 * s + kk, 1), :].rearrange("p a t -> p (a t)")
                            xl = HL[:, bass.ds(i * 8 + 2 * s + kk, 1), :].rearrange("p a t -> p (a t)")
                        last = three(bank[4 + m // 2][:, m % 2 * T:(m % 2 + 1) * T], n, kk * KD + m,
                                     xh, xl, start=False)
                return last.then_inc(q["slab_used"], 1)

            def down_stage(stage, before=None):
                pe.wait_ge(q["h_ready"], HID[stage] + 1)
                for b in range(4, 8):
                    mm(bank[b][:, 0:2], zero[:, :], zero[:, 0:2], start=True, stop=False,
                       skip_group_check=True)
                loops = SLABS[stage] // 4 if SLABS[stage] > 8 else 0
                if loops:
                    with pe.Fori(0, loops) as i:
                        for s in range(4):
                            down_slab(stage, s, i)
                for s in range(4 * loops, SLABS[stage] - 1):
                    if before is not None:
                        before(s)
                    down_slab(stage, s)
                s = SLABS[stage] - 1
                n = N0[stage] + s
                pe.wait_ge(q["h_ready"], HID[stage] + s + 1)
                pe.wait_ge(q["lo_ready"], 2 * n + 2)
                for m in range(KD):
                    for kk in range(2):
                        last = three(bank[4 + m // 2][:, m % 2 * T:(m % 2 + 1) * T], n, kk * KD + m,
                                     HH[:, 2 * s + kk, :], HL[:, 2 * s + kk, :], start=False)
                    if m % 2 and m < KD - 1:
                        last.then_inc(q["pair_summed"], 1)
                last.then_inc(q["slab_used"], 1)

            norms = [0]

            def norm(bank_of_sums=3):
                k = norms[0]
                norms[0] += 1
                sums = bank[bank_of_sums]
                pe.wait_ge(q["squares_folded"], k + 1)
                for m in (0, 1, 6, 7):
                    if m >= 6:
                        pe.wait_ge(q["squares_ready"], 8 * k + m + 1)
                    for j in range(2):
                        last = mm(sums[:, j:j + 1], S[:, m * T + j * P:m * T + (j + 1) * P], ones[:, 0:1],
                                  start=(m == 0 and j == 0), stop=False, skip_group_check=True)
                last.then_inc(q["sum_ready"], 1)
                pe.wait_ge(q["diag_ready"], k + 1)
                mm(bank[4][:, 0:T], ones, R[:, 0:T], start=True, stop=True).then_inc(q["spread_ready"], 1)

            def attention(done, heads, query, key, value, pairs):
                def scores(h):
                    if h >= 2:
                        pe.wait_ge(q["exp_ready"], done + h - 1)
                    for j in range(2):
                        last = mm(bank[h % 2][:, j * T:(j + 1) * T], query(h, j), key(h),
                                  start=(j == 0), stop=(j == 1), skip_group_check=True)
                    last.then_inc(q["scores_ready"], 1)

                def turn(h):
                    pe.wait_ge(q["prob_ready"], done + h + 1)
                    if h >= 2:
                        pe.wait_ge(q["turned_ready"], done + h - 1)
                    for k in range(2):
                        for j in range(2):
                            at = (h % 2) * 512 + j * T + k * P
                            last = nc.tensor.transpose(bank[2 + h % 2][:, k * T + j * P:k * T + (j + 1) * P],
                                                       S[:, at:at + P], ident)
                    last.then_inc(q["turn_ready"], 1)

                def output(h):
                    pe.wait_ge(q["turned_ready"], done + h + 1)
                    pair, row = h // 2, h % 2 * 64
                    if row == 0 and pair >= 2:
                        pe.wait_ge(q["head_kept"], pairs + pair - 1)
                    for k in range(2):
                        at = 1024 + (h % 2) * 512 + k * T
                        last = mm(bank[4 + pair % 2][row:row + 64, 0:T], value(h, k),
                                  S[:, at:at + T], start=(k == 0), stop=(k == 1), skip_group_check=True)
                    last.then_inc(q["head_ready"], 1)

                scores(0)
                scores(1)
                for h in range(heads):
                    if h + 2 < heads:
                        scores(h + 2)
                    turn(h)
                    if h:
                        output(h - 1)
                output(heads - 1)

            pe.wait_ge(q["par_loaded"], 48)
            pe.wait_ge(q["zero_ready"], 1)
            norm()

            def qk_sum(s):
                pe.wait_ge(q["qk_squares"], s - 1)
                mm(bank[2 + s][:, :], con_mat("pair64"), S[:, (s - 2) * 512:(s - 1) * 512],
                   start=True, stop=True).then_inc(q["qk_sum"], 1)

            up_stage("pa_in", 1, lambda s: qk_sum(s - 1) if 3 <= s <= 6 else None)
            pe.wait_ge(q["even_evacuated"], 4)
            pe.wait_ge(q["odd_evacuated"], 4)
            for j in range(2):
                for v in range(4):
                    last = nc.tensor.transpose(bank[2 + j][:, v * P:(v + 1) * P],
                                               VRAW[:, v, j * P:(j + 1) * P], ident)
            last.then_inc(q["v_turned"], 1)
            pe.wait_ge(q["vt_ready"], 1)
            attention(0, HEADS1,
                      lambda h, j: A1[h % 2 * 64:h % 2 * 64 + 64, h // 2, j * P:(j + 1) * P],
                      lambda h: A1[h % 2 * 64:h % 2 * 64 + 64, 4 + h // 2, :],
                      lambda h, k: VT1[:, k, h * HD1:(h + 1) * HD1], 0)
            pe.wait_ge(q["pooled"], 1)
            pe.wait_ge(q["late_loaded"], 16 * 4)
            for g in range(4):
                last = mm(bank[6 + g // 2][:, g % 2 * T:(g % 2 + 1) * T], SW[:, g, :],
                          UP[:, 0, g, PAD:PAD + T], start=(g % 2 == 0), stop=(g % 2 == 1),
                          skip_group_check=True)
            last.then_inc(q["pool_mixed"], 1)
            up_stage("pa_out", 2)

            norm(6)
            up_stage("f0_up", 3)
            down_stage("f0_down")

            norm()

            def gates(s):
                pe.wait_ge(*up_count("rg_in", s))
                if s >= 2:
                    pe.wait_ge(q["it_ready"], s - 1)
                at = s % 2 * T
                mm(bank[4 + s % 2][:, 0:T], SW[:, 4 + s, :], S[:, at:at + T], start=True, stop=False,
                   skip_group_check=True)
                mm(bank[4 + s % 2][:, T:2 * T], SW[:, 14 + s, :], S[:, at:at + T], start=False,
                   stop=True, skip_group_check=True).then_inc(q["ri_ready"], 1)

            up_stage("rg_in", 4, lambda s: gates(s - 1) if s >= 1 else None)
            gates(RNN - 1)
            down_stage("rg_out")

            norm()
            up_stage("f1_up", 5)
            down_stage("f1_down")

            norm()
            up_stage("g00_up", 6)
            down_stage("g00_down")

            norm()

            def turn_x(r):
                if r >= 4:
                    pe.wait_ge(q["xs_turned"], r - 3)
                for v in range(4):
                    last = nc.tensor.transpose(bank[4 + r % 4][:, v * P:(v + 1) * P],
                                               XS[:, r // 2 * 4 + v, r % 2 * P:(r % 2 + 1) * P], ident)
                last.then_inc(q["xs_turn"], 1)

            def ssd_between(s):
                if s == 18:
                    pe.wait_ge(q["silu_ready"], 16)
                if s in (18, 19):
                    for r in range(4):
                        turn_x(4 * (s - 18) + r)
                if s == 22:
                    pe.wait_ge(q["exponents_ready"], 1)
                    pe.wait_ge(q["xs_turned"], 8)
                    for v in range(4):
                        src = S[0:64, 2048 + (v // 2) * T + v % 2 * P:2048 + (v // 2) * T + v % 2 * P + P]
                        last = nc.tensor.transpose(bank[4][:, v * 64:(v + 1) * 64], src,
                                                   CN[0:64, CON["ident"]:CON["ident"] + 64])
                    last.then_inc(q["col_turn"], 1)

            up_stage("ssd_in", 7, ssd_between)

            def expo(h):
                if h >= 2:
                    pe.wait_ge(q["decay_ready"], h - 1)
                b = 2 + 2 * (h % 2)
                for d in range(2):
                    sel = selr[:, 32 * d + h:32 * d + h + 1].to_broadcast([P, P])
                    mm(bank[b + d][:, :], sel, acr[:, :].rearrange("p (a t) -> p a t", a=1).to_broadcast([P, 2, T]),
                       start=True, stop=False, skip_group_check=True)
                    for at in (0, 3 * P):
                        last = mm(bank[b + d][:, at:at + P], identr[:, :], maskr[:, d * P:(d + 1) * P],
                                  start=False, stop=False, skip_group_check=True)
                last.then_inc(q["expo_ready"], 1)

            def cb(g):
                if g >= 2:
                    pe.wait_ge(q["mt_ready"], 4 * (g - 1))
                for j in range(2):
                    last = mm(bank[g % 2][:, j * T:(j + 1) * T], A2[:, g, j * P:(j + 1) * P], A2[:, 8 + g, :],
                              start=(j == 0), stop=(j == 1), skip_group_check=True)
                last.then_inc(q["cb_ready"], 1)

            pe.wait_ge(q["even_evacuated"], EV0["ssd_in"] + 13)
            pe.wait_ge(q["odd_evacuated"], OD0["ssd_in"] + 12)
            pe.wait_ge(q["cols_ready"], 1)
            pe.wait_ge(q["identr_ready"], 1)
            cb(0)
            expo(0)
            expo(1)

            def group_sums(g, b):
                pe.wait_ge(q["ysq_ready"], g + 1)
                for k in range(2):
                    for j in range(2):
                        at = g % 2 * 512 + k * T + j * P
                        last = mm(bank[b][:, T + j:T + j + 1], S[:, at:at + P], ones[:, 0:1],
                                  start=(k == 0 and j == 0), stop=(k == 1), skip_group_check=True)
                return last

            for h in range(SSD_H):
                if h + 2 < SSD_H:
                    expo(h + 2)
                if h % 4 == 0 and h // 4 + 1 < SSD_G:
                    cb(h // 4 + 1)
                pair, row = h // 2, h % 2 * 64
                if row == 0 and pair >= 2:
                    pe.wait_ge(q["yz_ready"], pair - 1)
                if row == 0 and pair % 2 and pair >= 3:
                    group_sums((pair - 3) // 2, 6 + pair % 2)
                pe.wait_ge(q["mt_ready"], h + 1)
                for j in range(2):
                    last = mm(bank[6 + pair % 2][row:row + 64, 0:T], XST[:, j, pair, row:row + 64],
                              MT[:, h % 2, j, :], start=(j == 0), stop=(j == 1), skip_group_check=True)
                last.then_inc(q["y_ready"], 1)
            group_sums(SSD_G - 1, 6).then_inc(q["ysum_ready"], 1)

            def spread(g):
                pe.wait_ge(q["ydiag_ready"], g + 1)
                if g >= 4:
                    pe.wait_ge(q["yn_ready"], g - 3)
                mm(bank[g % 4][:, 0:T], ones, A2[:, g, :], start=True, stop=True).then_inc(q["yspread_ready"], 1)

            for g in range(4):
                spread(g)
            down_stage("ssd_out", lambda s: [spread(2 * s + 4), spread(2 * s + 5)] if s < 2 else None)

            norm()
            up_stage("g01_up", 8)
            down_stage("g01_down")
            norm()
            up_stage("g10_up", 9)
            down_stage("g10_down")

            norm()
            up_stage("mla_in", 10)
            pe.wait_ge(q["lat_kept"], 3)
            for c, tiles in ((0, (0, 1, 2)), (2, (3, 4))):
                for j in range(2):
                    for k in tiles:
                        mm(bank[4][:, c + j:c + j + 1], S[:, k * T + j * P:k * T + (j + 1) * P], ones[:, 0:1],
                           start=(c == 0 and j == 0 and k == 0), stop=False, skip_group_check=True)
            for j in range(2):
                mm(bank[4][:, 4 + j:5 + j], A2[64:96, 8, j * P:(j + 1) * P],
                   CN[64:96, CON["ones"]:CON["ones"] + 1], start=False, stop=False, skip_group_check=True)
            for k in (3, 4):
                last = mm(bank[5][:, 0:T], ones, S[:, k * T:(k + 1) * T], start=(k == 3), stop=(k == 4))
            last.then_inc(q["lat_sum"], 1)
            pe.wait_ge(q["pe_scaled"], 1)
            mm(bank[6][:, 0:T], con_mat("rope_sum"), A1[:, 5, :], start=True,
               stop=True).then_inc(q["rope_summed"], 1)
            pe.wait_ge(q["x_ready"], 88)

            def head_sums(b, at, u, rows, c):
                for hh in range(2):
                    for j in range(2):
                        last = mm(bank[b][:, c + 2 * hh + j:c + 2 * hh + j + 1],
                                  S[0:rows, at + hh * T + j * P:at + hh * T + (j + 1) * P],
                                  CN[0:rows, CON["ones"]:CON["ones"] + 1],
                                  start=(c == 0 and hh == 0 and j == 0), stop=False, skip_group_check=True)
                return last

            def mq_sum(u):
                pe.wait_ge(q["mq_kept"], u + 1)
                head_sums(7, u % 2 * 512, u, 96, 4 * u).then_inc(q["mq_sum"], 1)

            for s in range(4):
                n = N0["mla_uq"] + s
                for m in range(4):
                    if m % 2 == 0:
                        pe.wait_ge(q["lo_ready"], 2 * n + m // 2 + 1)
                        if s >= 2:
                            pe.wait_ge(q["mq_kept"], 2 * s + m // 2 - 3)
                    for kt in range(3):
                        last = three(bank[s % 2 * 2 + m // 2][:, m % 2 * T:(m % 2 + 1) * T], n, 4 * m + kt,
                                     XH[:, kt, :], XL[:, kt, :], start=(m % 2 == 0 and kt == 0))
                    if m == 1:
                        last.then_inc(q["first_queries"], 1)
                last.then_inc(q["slab_used"], 1)
                if s:
                    mq_sum(2 * s - 2)
                    mq_sum(2 * s - 1)
            mq_sum(6)
            mq_sum(7)

            def mk_sum(u):
                pe.wait_ge(q["mk_kept"], u + 1)
                last = head_sums(4 + u // 4, u % 4 * 512, u, 64, 4 * (u % 4))
                if u % 4 == 3:
                    last.then_inc(q["mk_sum"], 1)

            def mk_spread(u):
                pe.wait_ge(q["mk_diag"], u + 1)
                if u >= 2:
                    pe.wait_ge(q["mk_ready"], u - 1)
                mm(bank[6 + u % 2][:, :], ones, S[:, 2048 + u % 2 * 512:2560 + u % 2 * 512], start=True,
                   stop=True).then_inc(q["mk_spread"], 1)

            for s in range(2):
                n = N0["mla_ukv"] + s
                for m in range(8):
                    if m % 4 == 0:
                        pe.wait_ge(q["lo_ready"], 2 * n + m // 4 + 1)
                    if m % 2 == 0:
                        if s == 0:
                            pe.wait_ge(q["mq_kept"], 5 + m // 2)
                        else:
                            pe.wait_ge(q["mk_kept"], m // 2 + 1)
                    for kt in range(2):
                        last = three(bank[m // 2][:, m % 2 * T:(m % 2 + 1) * T], n, 2 * m + kt,
                                     XH[:, 3 + kt, :], XL[:, 3 + kt, :], start=(m % 2 == 0 and kt == 0))
                    if m % 2 and s:
                        mk_sum(m // 2)
                last.then_inc(q["slab_used"], 1)
            for u in range(4):
                mk_spread(u)
            for u in range(4, 8):
                mk_sum(u)
            for r in range(4):
                j, half = r % 2, r // 2
                for v in range(8):
                    last = nc.tensor.transpose(bank[r][:, v * 64:(v + 1) * 64],
                                               A1[64:P, 8 * half + v, j * P:(j + 1) * P],
                                               CN[64:P, CON["ident"] + 64:CON["ident"] + P])
                last.then_inc(q["mv_turn"], 1)
            for u in range(4, 8):
                mk_spread(u)
            pe.wait_ge(q["mv_turned"], 4)
            pe.wait_ge(q["mk_ready"], 8)
            attention(HEADS1, MLA_H,
                      lambda h, j: QH[:, h, j * P:(j + 1) * P],
                      lambda h: KH[:, h, :],
                      lambda h, k: VT2[:, k, h * 64:(h + 1) * 64], HEADS1 // 2)
            up_stage("mla_out", 12)

            norm(6)
            up_stage("g11_up", 13)
            down_stage("g11_down")

        @block.scalar
        def _(act):
            f = nc.scalar.activation

            def split_hi(n, i=None):
                if n >= NSLABS:
                    return
                act.wait_ge(raw_loaded[n % RAW], plus(16 * (n // RAW + 1), i, 16))
                if n >= SPLIT:
                    act.wait_ge(q["slab_used"], plus(n - SPLIT + 1, i, 4))
                for h in range(2):
                    at = slice(h * HALF, (h + 1) * HALF)
                    f(hi[:, n % SPLIT, at], raw[:, n % RAW, at], ACT.Copy).then_inc(q["hi_ready"], 1)

            def down_stage(stage, between={}):
                loops = SLABS[stage] // 4 if SLABS[stage] > 8 and not between else 0
                if loops:
                    with act.Fori(0, loops) as i:
                        for s in range(4):
                            split_hi(N0[stage] + s + 2, i)
                for s in range(4 * loops, SLABS[stage] - 1):
                    split_hi(N0[stage] + s + 2)
                    if s in between:
                        between[s]()

            norms = [0]

            def norm(stage, layer=0, shift=None, bank_of_sums=3, then=None):
                k = norms[0]
                norms[0] += 1
                f(tiny[:, 61:62], tiny[:, 60:61], ACT.Sqrt)
                for m, w in ((0, 2), (2, 2), (4, 2), (6, 1), (7, 1)):
                    if k:
                        act.wait_ge(q["resid_ready"], 8 * (k - 1) + m + w)
                    f(S[:, m * T:(m + w) * T], X[:, m:m + w, :].rearrange("p a t -> p (a t)"),
                      ACT.Square).then_inc(q["squares_ready"], w)
                if k == 0:
                    split_hi(0)
                act.wait_ge(q["sum_ready"], k + 1)
                f(tiny[:, 52:54], bank[bank_of_sums][:, 0:2], ACT.Sqrt, scale=1.0 / D,
                  bias=tiny[:, 59:60]).then_inc(q["norm_ready"], 1)
                split_hi(N0[stage] + 1)
                for kt in range(KD):
                    act.wait_ge(q["scaled_ready"], 8 * k + kt + 1)
                    if shift is None:
                        f(XH[:, kt, :], S[:, kt * T:(kt + 1) * T], ACT.Copy).then_inc(q["xh_ready"], 1)
                    else:
                        f(XH[:, kt, :], S[:, kt * T:(kt + 1) * T], ACT.Identity,
                          bias=MOD[:, 72 * layer + shift + kt:72 * layer + shift + kt + 1]).then_inc(q["xh_ready"], 1)
                if then is not None:
                    f(tiny[:, 61:62], tiny[:, 60:61], then)

            def conv_ffn(stage, layer):
                def pair(p, i=None):
                    b = p % 2
                    for side in range(2):
                        n = N0[stage] + 2 * p + side
                        split_hi(n + 2, i)
                        act.wait_ge(q["slab_used"], plus(n + 1, i, 4))
                        if side == 0 and p >= 2:
                            act.wait_ge(q["h_ready"], plus(HID[DOWN[stage]] + p - 1, i, 2))
                        for m in range(2):
                            k = 2 * p + m + 22 * side
                            last = f(S[:, b * 1024 + side * 512 + m * T:b * 1024 + side * 512 + (m + 1) * T],
                                     bank[n % 4][:, m * T:(m + 1) * T], ACT.Identity,
                                     scale=col(f"fconv{layer}", 88 + k, i, 4),
                                     bias=col(f"fconvb{layer}", k, i, 4))
                        last.then_inc(q["lin_ready"], 1)
                    e, v = up_count(stage, 2 * p + 1)
                    act.wait_ge(e, plus(v, i, 2))
                    f(S[:, 2048 + b * 512:2560 + b * 512], S[:, b * 1024 + 512:b * 1024 + 1024],
                      ACT.Gelu_apprx_tanh).then_inc(q["gelu_ready"], 1)

                pair(0)
                pair(1)
                with act.Fori(0, 4) as i:
                    pair(2, i)
                    pair(3, i)
                pair(10)

            def gated_ffn(stage):
                def pair(p, i=None):
                    b = p % 2
                    n = N0[stage] + 2 * p
                    split_hi(n + 2, i)
                    act.wait_ge(q["slab_used"], plus(n + 1, i, 4))
                    if p >= 2:
                        act.wait_ge(q["h_ready"], plus(HID[DOWN[stage]] + p - 1, i, 2))
                    f(S[:, 2048 + b * 512:2560 + b * 512], bank[n % 4][:, :],
                      ACT.Silu).then_inc(evacuated[0], 1)
                    split_hi(n + 3, i)

                pair(0)
                pair(1)
                with act.Fori(0, 4) as i:
                    pair(2, i)
                    pair(3, i)
                pair(10)

            def attention(done, heads, scale, scores, cat, pairs):
                def exps(h):
                    act.wait_ge(q["shift_ready"], done + h + 1)
                    if h >= 2:
                        act.wait_ge(q["turn_ready"], done + h - 1)
                    for j in range(2):
                        at = h % 2 * 512 + j * T
                        last = f(S[:, at:at + T], scores(h, j), ACT.Exp, scale=scale(h, j),
                                 bias=tiny[:, h % 2 * 8 + 2 + j:h % 2 * 8 + 3 + j],
                                 accum_out=tiny[:, h % 2 * 8 + 4 + j:h % 2 * 8 + 5 + j])
                    last.then_inc(q["exp_ready"], 1)

                def keep_pair(p):
                    act.wait_ge(q["head_ready"], done + 2 * p + 2)
                    f(cat(p), bank[4 + p % 2][:, 0:T], ACT.Copy).then_inc(q["head_kept"], 1)

                exps(0)
                for h in range(heads):
                    if h + 1 < heads:
                        exps(h + 1)
                    act.wait_ge(q["turn_ready"], done + h + 1)
                    if h >= 2:
                        act.wait_ge(q["head_ready"], done + h - 1)
                    at = 1024 + h % 2 * 512
                    f(S[:, at:at + 512], bank[2 + h % 2][:, :], ACT.Copy).then_inc(q["turned_ready"], 1)
                    if h % 2 and h >= 3:
                        keep_pair((h - 3) // 2)
                keep_pair(heads // 2 - 1)

            cats = [0]

            def cat_hi(cat):
                cats[0] += 1
                for k in range(4):
                    last = f(XH[:, 2 * k:2 * k + 2, :], cat[:, 2 * k:2 * k + 2, :], ACT.Copy)
                    last.then_inc(q["cat_hi"], 1)

            act.wait_ge(q["zero_ready"], 1)
            act.wait_ge(q["par_loaded"], 48)
            norm("pa_in", then=ACT.Silu)
            act.wait_ge(q["cond_loaded"], 16)
            f(cond[:, :], cond[:, :], ACT.Silu).then_inc(q["cond_ready"], 1)

            for s in range(8):
                split_hi(s + 2)
                act.wait_ge(q["slab_used"], s + 1)
                if s < 2:
                    if s == 0:
                        act.wait_ge(q["pool_steps"], 1)
                    f(UP[:, 0, 2 * s:2 * s + 2, PAD:PAD + T],
                      bank[s % 4][:, :].rearrange("p (a t) -> p a t", a=2), ACT.Copy).then_inc(evacuated[s % 2], 1)
                elif s < 6:
                    f(S[:, (s - 2) * 512:(s - 1) * 512], bank[s % 4][:, :],
                      ACT.Square).then_inc(q["qk_squares"], 1)
                else:
                    f(VRAW[:, 2 * (s - 6):2 * (s - 5), :],
                      bank[s % 4][:, :].rearrange("p (a t) -> p a t", a=2), ACT.Copy).then_inc(evacuated[s % 2], 1)
                if 3 <= s <= 6:
                    at = 2048 + (s - 3) * 512
                    act.wait_ge(q["qk_var"], s - 2)
                    f(S[:, at:at + 512], S[:, at:at + 512], ACT.Sqrt).then_inc(q["qk_norm"], 1)
            act.wait_ge(q["v_turned"], 1)
            for j in range(2):
                last = f(VT1[:, j, :], bank[2 + j][:, :], ACT.Copy)
            last.then_inc(q["vt_ready"], 1)
            attention(0, HEADS1, lambda h, j: HD1 ** -0.5,
                      lambda h, j: S[:, h % 2 * 512 + j * T:h % 2 * 512 + (j + 1) * T],
                      lambda p: CAT1[:, 4 + p, :], 0)
            act.wait_ge(q["pool_mixed"], 1)
            for g in range(4):
                last = f(CAT1[:, g, :], bank[6 + g // 2][:, g % 2 * T:(g % 2 + 1) * T], ACT.Copy,
                         scale=col("pool_scale", g))
            last.then_inc(q["act_steps"], 1)
            act.wait_ge(q["act_steps"], 1)
            act.wait_ge(q["head_kept"], 4)
            cat_hi(CAT1)
            for s in range(3):
                split_hi(N0["pa_out"] + s + 2)


            norm("f0_up", bank_of_sums=6, then=ACT.Gelu_apprx_tanh)
            conv_ffn("f0_up", 0)
            def softplus_1():
                f(tiny[:, 20:30], col_span("lam", 10), ACT.Abs).then_inc(q["act_steps"], 1)
                act.wait_ge(q["act_steps"], 2)
                f(tiny[:, 20:30], tiny[:, 20:30], ACT.Exp, scale=-1.0).then_inc(q["decay_z"], 1)
                f(tiny[:, 50:51], col("a_log"), ACT.Exp).then_inc(q["decay_z"], 1)

            def softplus_2():
                act.wait_ge(q["decay_u"], 1)
                f(tiny[:, 40:50], tiny[:, 30:40], ACT.Ln).then_inc(q["decay_l"], 1)

            down_stage("f0_down", {3: softplus_1, 4: softplus_2})

            norm("rg_in", then=ACT.Gelu_apprx_tanh)

            def gate_tanhs(s):
                act.wait_ge(q["ri_ready"], s + 1)
                f(A1[:, s, :], bank[4 + s % 2][:, 0:T], ACT.Tanh, scale=0.5,
                  bias=c4[:, 2 * RNN + s:2 * RNN + s + 1])
                f(S[:, 512 + s % 2 * T:512 + (s % 2 + 1) * T], bank[4 + s % 2][:, T:2 * T], ACT.Tanh,
                  scale=0.5, bias=c4[:, 3 * RNN + s:3 * RNN + s + 1]).then_inc(q["it_ready"], 1)

            act.wait_ge(q["c4_ready"], 1)
            for s in range(RNN):
                n = N0["rg_in"] + s
                split_hi(n + 2)
                act.wait_ge(q["slab_used"], n + 1)
                f(GG[:, s, :], bank[n % 4][:, 0:T], ACT.Gelu_apprx_tanh).then_inc(q["act_steps"], 1)
                if s >= 2:
                    act.wait_ge(q["ix_ready"], s - 1)
                f(S[:, s % 2 * T:(s % 2 + 1) * T], bank[n % 4][:, T:2 * T], ACT.Identity,
                  scale=col("rconv", 30 + s), bias=col("rconvb", s)).then_inc(q["lin_ready"], 1)
                if s:
                    gate_tanhs(s - 1)
            gate_tanhs(RNN - 1)
            act.wait_ge(q["it_ready"], RNN)
            for s in range(RNN):
                at = 1024 + s * T
                f(S[:, at:at + T], A1[:, s, :], ACT.Tanh, scale=c4[:, s:s + 1],
                  bias=c4[:, s:s + 1]).then_inc(q["act_steps"], 1)
                act.wait_ge(q["act_steps"], 2 + RNN + s + 1)
                f(A1[:, s, :], A1[:, s, :], ACT.Exp, scale=c4[:, RNN + s:RNN + s + 1],
                  bias=c4[:, RNN + s:RNN + s + 1]).then_inc(q["rg_exp"], 1)
            for s in range(RNN):
                at = 1024 + s * T
                act.wait_ge(q["rg_arg"], s + 1)
                f(S[:, at:at + T], S[:, at:at + T], ACT.Sqrt).then_inc(q["rg_root"], 1)
            down_stage("rg_out")

            norm("f1_up", then=ACT.Gelu_apprx_tanh)
            conv_ffn("f1_up", 1)
            down_stage("f1_down")

            act.wait_ge(q["mod_ready"], 1)
            norm("g00_up", 0, 0, then=ACT.Silu)
            gated_ffn("g00_up")

            def rope_table():
                act.wait_ge(q["angle_ready"], 1)
                f(CS[:, :], CS[:, :], ACT.Sin).then_inc(q["table_ready"], 1)

            down_stage("g00_down", {4: rope_table})

            norm("ssd_in", 0, 24, then=ACT.Silu)

            def ssd_silu(s):
                e, v = up_count("ssd_in", s)
                act.wait_ge(e, v)
                dst = (A2 if s < 8 else XS)[:, 2 * (s % 8):2 * (s % 8) + 2, :]
                f(dst, S[:, s % 2 * 512:(s % 2 + 1) * 512].rearrange("p (a t) -> p a t", a=2),
                  ACT.Silu).then_inc(q["silu_ready"], 1)

            for s in range(25):
                n = N0["ssd_in"] + s
                split_hi(n + 2)
                act.wait_ge(q["slab_used"], n + 1)
                if s < 16:
                    if s >= 2:
                        act.wait_ge(q["silu_ready"], s - 1)
                    for m in range(2):
                        last = f(S[:, s % 2 * 512 + m * T:s % 2 * 512 + (m + 1) * T],
                                 bank[n % 4][:, m * T:(m + 1) * T], ACT.Identity,
                                 scale=col("sconv", 64 + 2 * s + m), bias=col("sconvb", 2 * s + m))
                    last.then_inc(q["lin_ready"], 1)
                    if s:
                        ssd_silu(s - 1)
                elif s == 16:
                    ssd_silu(15)
                    f(S[0:64, 2048:2304], bank[n % 4][0:64, 0:T], ACT.Identity,
                      bias=PAR[0:64, COL["dt_bias"]:COL["dt_bias"] + 1]).then_inc(evacuated[0], 1)
                else:
                    f(A1[:, 2 * (s - 17):2 * (s - 16), :],
                      bank[n % 4][:, :].rearrange("p (a t) -> p a t", a=2), ACT.Silu).then_inc(evacuated[s % 2], 1)
                if s == 17:
                    act.wait_ge(evacuated[0], EV0["ssd_in"] + 9)
                    f(S[0:64, 2304:2560], S[0:64, 2048:2304], ACT.Abs).then_inc(q["act_steps"], 1)
                    act.wait_ge(q["act_steps"], 2 + 2 * RNN + 1)
                    f(S[0:64, 2304:2560], S[0:64, 2304:2560], ACT.Exp, scale=-1.0).then_inc(q["dt_z"], 1)
                if s == 18:
                    act.wait_ge(q["dt_u"], 1)
                    f(S[0:64, 2816:3072], S[0:64, 2560:2816], ACT.Ln).then_inc(q["dt_log"], 1)
            act.wait_ge(q["cols_ready"], 1)

            def group_squares(g):
                act.wait_ge(q["yz_ready"], 2 * g + 2)
                f(S[:, g % 2 * 512:(g % 2 + 1) * 512].rearrange("p (a t) -> p a t", a=2),
                  A1[:, 2 * g:2 * g + 2, :], ACT.Square).then_inc(q["ysq_ready"], 1)

            for h in range(SSD_H):
                act.wait_ge(q["expo_ready"], h + 1)
                if h >= 2:
                    act.wait_ge(q["mt_ready"], h - 1)
                b, E = 2 + 2 * (h % 2), EX[:, h % 2]
                f(E[:, 0:2, :].rearrange("p a t -> p (a t)"), bank[b][:, 0:T], ACT.Exp, bias=cols[:, 2, h:h + 1])
                f(E[:, 3, :], bank[b][:, T + P:2 * T], ACT.Exp, bias=cols[:, 3, h:h + 1])
                f(E[:, 4, :], bank[b + 1][:, 0:P], ACT.Exp, bias=cols[:, 2, 32 + h:33 + h])
                f(E[:, 2:6:3, :], bank[b + 1][:, T:2 * T].rearrange("p (a t) -> p a t", a=2), ACT.Exp,
                  bias=cols[:, 3, 32 + h:33 + h]).then_inc(q["decay_made"], 1)
                act.wait_ge(q["decay_made"], h + 1)
                f(E[:, 1, :], E[:, 1, :], ACT.Copy, scale=cols[:, 0, h:h + 1])
                f(E[:, 2, :], E[:, 2, :], ACT.Copy, scale=cols[:, 1, 32 + h:33 + h]).then_inc(q["decay_ready"], 1)
                if h % 4 == 2 and h >= 6:
                    group_squares((h - 6) // 4)
            group_squares(SSD_G - 1)
            f(tiny[:, 61:62], tiny[:, 60:61], ACT.Sqrt)
            act.wait_ge(q["ysum_kept"], 1)
            f(tiny[:, 80:96], tiny[:, 64:80], ACT.Sqrt, scale=1.0 / 256, bias=tiny[:, 59:60]).then_inc(q["yroot_ready"], 1)
            for g in range(SSD_G):
                act.wait_ge(q["yn_ready"], g + 1)
                f(HH[:, 2 * g:2 * g + 2, :], A1[:, 2 * g:2 * g + 2, :], ACT.Copy).then_inc(q["yh_ready"], 1)
            down_stage("ssd_out")

            norm("g01_up", 0, 48, then=ACT.Silu)
            gated_ffn("g01_up")
            down_stage("g01_down")
            act.wait_ge(q["mod_ready"], 2)
            norm("g10_up", 1, 0, then=ACT.Silu)
            gated_ffn("g10_up")
            down_stage("g10_down")

            norm("mla_in", 1, 24)
            for s in range(3):
                n = N0["mla_in"] + s
                split_hi(n + 2)
                act.wait_ge(q["slab_used"], n + 1)
                two = bank[n % 4][:, :].rearrange("p (a t) -> p a t", a=2)
                for t in (2 * s, 2 * s + 1):
                    g = col("mqn", t) if t < 3 else col("mkn", t - 3) if t < 5 else col("mkh")
                    last = f(A1[:, t, :], two[:, t % 2, :], ACT.Copy, scale=g)
                last.then_inc(evacuated[s % 2], 1)
                if s < 2:
                    last = f(S[:, 2 * s * T:2 * (s + 1) * T].rearrange("p (a t) -> p a t", a=2), two, ACT.Square)
                else:
                    f(S[:, 4 * T:5 * T], two[:, 0, :], ACT.Square)
                    last = f(KPS, two[:, 1, :], ACT.Square)
                last.then_inc(q["lat_kept"], 1)
            act.wait_ge(q["lat_kept"], 3)
            for t in range(5):
                f(XH[:, t, :], A1[:, t, :], ACT.Copy).then_inc(q["lat_hi"], 1)
            act.wait_ge(q["lat_sum"], 1)
            f(tiny[:, 116:118], bank[4][:, 0:2], ACT.Sqrt, scale=1.0 / 384, bias=tiny[:, 59:60])
            f(tiny[:, 118:120], bank[4][:, 2:4], ACT.Sqrt, scale=1.0 / 256, bias=tiny[:, 59:60])
            f(R[64:P, 0:T], bank[5][64:P, 0:T], ACT.Sqrt, scale=1.0 / 256,
              bias=tiny[64:P, 59:60]).then_inc(q["lat_root"], 1)

            for u in range(8):
                n = N0["mla_uq"] + u // 2
                if u % 2 == 0:
                    split_hi(n + 2)
                    act.wait_ge(q["first_queries"], u // 2 + 1)
                else:
                    act.wait_ge(q["slab_used"], n + 1)
                if u >= 2:
                    act.wait_ge(q["mq_sum"], u - 1)
                    act.wait_ge(q["mq_ready"], u - 1)
                src = bank[u // 2 % 2 * 2 + u % 2]
                f(S[:, u % 2 * 512:u % 2 * 512 + 512], src[:, :], ACT.Square)
                f(S[:, 1024 + u % 2 * 512:1536 + u % 2 * 512], src[:, :], ACT.Copy,
                  scale=col("mqh")).then_inc(q["mq_kept"], 1)
            act.wait_ge(q["mq_var"], 1)
            f(tiny[:, 160:192], tiny[:, 128:160], ACT.Sqrt, bias=tiny[:, 59:60]).then_inc(q["mq_root"], 1)
            act.wait_ge(q["mq_ready"], 8)

            for u in range(8):
                n = N0["mla_ukv"] + u // 4
                if u % 4 == 0:
                    split_hi(n + 2)
                    act.wait_ge(q["slab_used"], n + 1)
                if u == 4:
                    act.wait_ge(q["mk_sum"], 1)
                src = bank[u % 4]
                f(S[0:64, u % 4 * 512:u % 4 * 512 + 512], src[0:64, :], ACT.Square)
                f(KH[0:64, 2 * u:2 * u + 2, :], src[0:64, :].rearrange("p (a t) -> p a t", a=2), ACT.Copy,
                  scale=PAR[0:64, COL["mkh"]:COL["mkh"] + 1])
                f(A1[64:P, 2 * u:2 * u + 2, :], src[64:P, :].rearrange("p (a t) -> p a t", a=2),
                  ACT.Copy).then_inc(q["mk_kept"], 1)
                if u % 4 == 3:
                    s = u // 4
                    act.wait_ge(q["mk_var"], s + 1)
                    f(tiny[:, 224 + 16 * s:240 + 16 * s], tiny[:, 192 + 16 * s:208 + 16 * s], ACT.Sqrt,
                      bias=tiny[:, 59:60]).then_inc(q["mk_root"], 1)
            act.wait_ge(q["mk_ready"], 8)
            attention(HEADS1, MLA_H, lambda h, j: tiny[:, 160 + 2 * h + j:161 + 2 * h + j],
                      lambda h, j: bank[h % 2][:, j * T:(j + 1) * T],
                      lambda p: A1[:, p, :], HEADS1 // 2)
            act.wait_ge(q["head_kept"], 12)
            cat_hi(A1)
            for s in range(3):
                split_hi(N0["mla_out"] + s + 2)

            norm("g11_up", 1, 48, 6, ACT.Silu)
            gated_ffn("g11_up")
            down_stage("g11_down")

        @block.vector
        def _(dve):
            v = nc.vector
            step = Steps(dve, q["vec_steps"])
            stt = v.scalar_tensor_tensor

            def two(ap, a=2):
                return ap.rearrange("p (a t) -> p a t", a=a)

            def split_lo(n, i=None, halves=(0, 1)):
                if n >= NSLABS:
                    return
                for h in halves:
                    dve.wait_ge(q["hi_ready"], plus(2 * n + h + 1, i, 8))
                    at = slice(h * HALF, (h + 1) * HALF)
                    v.tensor_tensor(lo[:, n % SPLIT, at], raw[:, n % RAW, at],
                                    hi[:, n % SPLIT, at].bitcast(F32), ALU.subtract).then_inc(q["lo_ready"], 1)

            def down_stage(stage, between={}):
                loops = SLABS[stage] // 4 if SLABS[stage] > 8 and not between else 0
                if loops:
                    with dve.Fori(0, loops) as i:
                        for s in range(4):
                            split_lo(N0[stage] + s + 2, i)
                for s in range(4 * loops, SLABS[stage] - 2):
                    split_lo(N0[stage] + s + 2)
                    if s in between:
                        between[s]()

            def fold_squares(k):
                for pair in (1, 2):
                    dve.wait_ge(q["squares_ready"], 8 * k + 2 * pair + 2)
                    last = v.tensor_tensor(S[:, 0:2 * T], S[:, 0:2 * T], S[:, 2 * pair * T:2 * (pair + 1) * T],
                                           ALU.add)
                    if pair == 1:
                        step.link(last)
                last.then_inc(q["squares_folded"], 1)

            def residual(stage, gate=None, more=True):
                following = N0[stage] + SLABS[stage]
                if stage in HID:
                    split_lo(following, halves=(0,))
                for k in range(4):
                    if k == 3 and more:
                        fold_squares(norms[0])
                    if stage in HID:
                        b = 4 + k
                        if k < 3:
                            dve.wait_ge(q["pair_summed"], 3 * SUMS[stage] // 4 + k + 1)
                        else:
                            dve.wait_ge(q["slab_used"], N0[stage] + SLABS[stage])
                    else:
                        n = N0[stage] + k
                        b = n % 4
                        if k < 3:
                            split_lo(n + 2, halves=(0, 1) if k < 2 else (0,))
                        dve.wait_ge(q["slab_used"], n + 1)
                    if gate is None and k < 3:
                        v.tensor_tensor(X[:, 2 * k:2 * k + 2, :], two(bank[b][:, :]), X[:, 2 * k:2 * k + 2, :],
                                        ALU.add).then_inc(q["resid_ready"], 2)
                    elif gate is None:
                        for m in (6, 7):
                            v.tensor_tensor(X[:, m, :], bank[b][:, m % 2 * T:(m % 2 + 1) * T], X[:, m, :],
                                            ALU.add).then_inc(q["resid_ready"], 1)
                    else:
                        for m in (2 * k, 2 * k + 1):
                            stt(out=X[:, m, :], in0=bank[b][:, m % 2 * T:(m % 2 + 1) * T],
                                scalar=GT[:, gate + m:gate + m + 1], in1=X[:, m, :],
                                op0=ALU.mult, op1=ALU.add).then_inc(q["resid_ready"], 1)
                split_lo(following, halves=(1,))

            norms = [0]

            def norm(stage, gain=None, shift=None):
                k = norms[0]
                norms[0] += 1
                dve.wait_ge(q["norm_ready"], k + 1)
                step.link(v.reciprocal(tiny[:, 54:56], tiny[:, 52:54]))
                for j in range(2):
                    last = v.tensor_scalar(R[:, j * P:(j + 1) * P], ident, tiny[:, 54 + j:55 + j], None, ALU.mult)
                last.then_inc(q["diag_ready"], 1)
                dve.wait_ge(q["spread_ready"], k + 1)

                def rest(kt):
                    dve.wait_ge(q["xh_ready"], 8 * k + kt + 1)
                    high = XH[:, kt, :].bitcast(F32)
                    if shift is None:
                        last = v.tensor_tensor(XL[:, kt, :], S[:, kt * T:(kt + 1) * T], high, ALU.subtract)
                    else:
                        last = stt(out=XL[:, kt, :], in0=S[:, kt * T:(kt + 1) * T],
                                   scalar=MOD[:, shift + kt:shift + kt + 1], in1=high,
                                   op0=ALU.add, op1=ALU.subtract)
                    last.then_inc(q["x_ready"], 1)

                for kt in range(KD):
                    g = col(gain, kt) if shift is None else MG[:, gain + kt:gain + kt + 1]
                    stt(out=S[:, kt * T:(kt + 1) * T], in0=X[:, kt, :], scalar=g, in1=bank[4][:, 0:T],
                        op0=ALU.mult, op1=ALU.mult).then_inc(q["scaled_ready"], 1)
                    if kt >= 2:
                        rest(kt - 2)
                rest(KD - 2)
                rest(KD - 1)
                split_lo(N0[stage] + 1)

            def modulation(layer):
                dve.wait_ge(q["mod_summed"], 72 * (layer + 1))
                M = MOD[:, 72 * layer:72 * layer + 72]
                step.link(v.tensor_reduce(M, modp[:, :, :], AX.X, ALU.add))
                v.tensor_tensor(M, M, col_span("bmod", 72, 72 * layer), ALU.add).then_inc(q["mod_taken"], 1)
                dve.wait_ge(q["mod_taken"], layer + 1)
                for sub in range(3):
                    at = 24 * layer + 8 * sub
                    stt(out=MG[:, at:at + 8], in0=M[:, 24 * sub + 8:24 * sub + 16], scalar=1.0,
                        in1=col_span("ng", 8, at), op0=ALU.add, op1=ALU.mult)
                    last = v.tensor_scalar(GT[:, at:at + 8], M[:, 24 * sub + 16:24 * sub + 24],
                                           1.0 if sub == 1 else 0.5, None, ALU.mult)
                last.then_inc(q["mod_ready"], 1)
                dve.wait_ge(q["mod_ready"], layer + 1)

            def hidden(buf, stage, p, i=None, made=None):
                at = 2 * p
                hh, hl = ((HH[:, at:at + 2, :], HL[:, at:at + 2, :]) if i is None else
                          (HH[:, bass.ds(i * 4 + at, 2), :], HL[:, bass.ds(i * 4 + at, 2), :]))
                step.link(made)
                step.link(v.tensor_copy(hh, two(buf)))
                v.tensor_tensor(hl, two(buf), hh.bitcast(F32), ALU.subtract).then_inc(q["h_ready"], 1)

            def conv_ffn(stage, layer, gelus):
                def pair(p, i=None):
                    b = p % 2
                    for side in range(2):
                        n = N0[stage] + 2 * p + side
                        split_lo(n + 2, i)
                        dve.wait_ge(q["lin_ready"], plus(LIN[stage] + 2 * p + side + 1, i, 4))
                        marks = []
                        for tap in (1, 2):
                            for m in range(2):
                                k = 2 * p + m + 22 * side
                                at = b * 1024 + side * 512 + m * T
                                z = S[:, at + tap:at + T]
                                if tap == 2:
                                    step.wait(marks[m])
                                last = stt(out=z, in0=bank[n % 4][:, m * T:(m + 1) * T - tap],
                                           scalar=col(f"fconv{layer}", (2 - tap) * 44 + k, i, 4), in1=z,
                                           op0=ALU.mult, op1=ALU.add)
                                if tap == 1:
                                    marks.append(step.put(last))
                        last.then_inc(evacuated[side], 1)
                    dve.wait_ge(q["gelu_ready"], plus(gelus + p + 1, i, 2))
                    e, val = up_count(stage, 2 * p)
                    dve.wait_ge(e, plus(val, i, 2))
                    buf = S[:, 3072 + b * 512:3584 + b * 512]
                    hidden(buf, stage, p, i, v.tensor_tensor(
                        buf, S[:, 2048 + b * 512:2560 + b * 512], S[:, b * 1024:b * 1024 + 512], ALU.mult))

                pair(0)
                pair(1)
                with dve.Fori(0, 4) as i:
                    step.enter(i, 12)
                    pair(2, i)
                    pair(3, i)
                    step.leave(4)
                pair(10)

            def gated_ffn(stage):
                def gated_pair(p, i=None):
                    b = p % 2
                    n = N0[stage] + 2 * p
                    split_lo(n + 2, i)
                    split_lo(n + 3, i)
                    e, val = up_count(stage, 2 * p)
                    dve.wait_ge(e, plus(val, i, 2))
                    dve.wait_ge(q["slab_used"], plus(n + 2, i, 4))
                    buf = S[:, 3072 + b * 512:3584 + b * 512]
                    made = v.tensor_tensor(buf, S[:, 2048 + b * 512:2560 + b * 512], bank[(n + 1) % 4][:, :],
                                           ALU.mult)
                    step.link(made)
                    at = 2 * p
                    hh, hl = ((HH[:, at:at + 2, :], HL[:, at:at + 2, :]) if i is None else
                              (HH[:, bass.ds(i * 4 + at, 2), :], HL[:, bass.ds(i * 4 + at, 2), :]))
                    v.tensor_copy(hh, two(buf)).then_inc(evacuated[1], 1)
                    e, val = up_count(stage, 2 * p + 1)
                    dve.wait_ge(e, plus(val, i, 2))
                    v.tensor_tensor(hl, two(buf), hh.bitcast(F32), ALU.subtract).then_inc(q["h_ready"], 1)

                gated_pair(0)
                gated_pair(1)
                with dve.Fori(0, 4) as i:
                    step.enter(i, 2)
                    gated_pair(2, i)
                    gated_pair(3, i)
                    step.leave(4)
                gated_pair(10)

            def attention(done, heads, scale=None, slopes=None):
                def maxima(h):
                    dve.wait_ge(q["scores_ready"], done + h + 1)
                    if slopes is None:
                        s = two(bank[h % 2][:, :])
                    else:
                        if h >= 2:
                            dve.wait_ge(q["turn_ready"], done + h - 1)
                        buf = S[:, h % 2 * 512:h % 2 * 512 + 512]
                        step.link(stt(out=buf, in0=DIST, scalar=slopes[h] / scale, in1=bank[h % 2][:, :],
                                      op0=ALU.mult, op1=ALU.add))
                        s = two(buf)
                    t = tiny[:, h % 2 * 8:h % 2 * 8 + 8]
                    step.link(v.tensor_reduce(t[:, 0:2], s, AX.X, ALU.max))
                    if scale is None:
                        stt(out=t[:, 2:4], in0=t[:, 0:2], scalar=-1.0, in1=tiny[:, 160 + 2 * h:162 + 2 * h],
                            op0=ALU.mult, op1=ALU.mult).then_inc(q["shift_ready"], 1)
                    else:
                        v.tensor_scalar(t[:, 2:4], t[:, 0:2], -scale, None, ALU.mult).then_inc(q["shift_ready"], 1)

                maxima(0)
                for h in range(heads):
                    if h + 1 < heads:
                        maxima(h + 1)
                    t = tiny[:, h % 2 * 8:h % 2 * 8 + 8]
                    dve.wait_ge(q["exp_ready"], done + h + 1)
                    step.link(v.reciprocal(t[:, 6:8], t[:, 4:6]))
                    for j in range(2):
                        at = h % 2 * 512 + j * T
                        last = v.tensor_scalar(S[:, at:at + T], S[:, at:at + T], t[:, 6 + j:7 + j], None,
                                               ALU.mult)
                    last.then_inc(q["prob_ready"], 1)

            cats = [0]

            def cat_lo(cat):
                for k in range(4):
                    dve.wait_ge(q["cat_hi"], 4 * cats[0] + k + 1)
                    v.tensor_tensor(XL[:, 2 * k:2 * k + 2, :], cat[:, 2 * k:2 * k + 2, :],
                                    XH[:, 2 * k:2 * k + 2, :].bitcast(F32), ALU.subtract).then_inc(q["x_ready"], 2)
                cats[0] += 1

            def log1p_rest(z, u, lg, tmp, y, out_):
                step.link(v.tensor_scalar(tmp, u, 1.0, None, ALU.is_equal))
                step.link(stt(out=u, in0=u, scalar=-1.0, in1=tmp, op0=ALU.add, op1=ALU.add))
                step.link(v.reciprocal(u, u))
                step.link(v.tensor_tensor(lg, lg, u, ALU.mult))
                step.link(v.tensor_tensor(lg, lg, tmp, ALU.add))
                step.link(v.tensor_tensor(lg, lg, z, ALU.mult))
                return stt(out=out_, in0=y, scalar=0.0, in1=lg, op0=ALU.max, op1=ALU.add)

            v.memset(tiny[:, 60:61], 1.0)
            v.memset(tiny[:, 59:60], EPS)
            v.memset(zero[:, :], 0.0).then_inc(q["zero_ready"], 1)
            dve.wait_ge(q["par_loaded"], 48)
            v.tensor_copy(identr[:, :], ident)
            v.tensor_copy(selr[:, :], con_mat("select", 64))
            v.tensor_copy(maskr[:, :], CN[:, CON["mask_f"]:CON["mask_f"] + 2 * P]).then_inc(q["identr_ready"], 1)
            fold_squares(0)
            split_lo(0)
            norm("pa_in", "nmix0")

            def head_norm(s):
                at = 2048 + (s - 2) * 512
                dve.wait_ge(q["qk_norm"], s - 1)
                stt(out=A1[:, 2 * (s - 2):2 * (s - 1), :], in0=two(bank[s][:, :] if s < 4 else bank[s - 4][:, :]),
                    scalar=col("q_gain" if s < 4 else "k_gain"), in1=two(S[:, at:at + 512]),
                    op0=ALU.mult, op1=ALU.mult).then_inc(evacuated[s % 2], 1)

            for s in range(8):
                split_lo(s + 2)
                if 3 <= s <= 6:
                    dve.wait_ge(q["qk_sum"], s - 2)
                    at = 2048 + (s - 3) * 512
                    step.link(v.tensor_scalar(S[:, at:at + 512], bank[1 + s][:, :], 1.0 / HD1, EPS,
                                              ALU.mult, ALU.add))
                    v.reciprocal(S[:, at:at + 512], S[:, at:at + 512]).then_inc(q["qk_var"], 1)
                    head_norm(s - 1)
            dve.wait_ge(q["late_loaded"], 16 * 4)
            attention(0, HEADS1, HD1 ** -0.5, [2.0 ** -(h + 1) for h in range(HEADS1)])
            cat_lo(CAT1)
            residual("pa_out")

            norm("f0_up", "nffn0")
            conv_ffn("f0_up", 0, 0)
            z, u, lg = tiny[:, 20:30], tiny[:, 30:40], tiny[:, 40:50]

            def softplus_1():
                dve.wait_ge(q["decay_z"], 2)
                v.tensor_scalar(u, z, 1.0, None, ALU.add).then_inc(q["decay_u"], 1)

            def softplus_2():
                dve.wait_ge(q["decay_l"], 1)
                step.link(v.tensor_scalar(c4[:, 30:40], col_span("lam", 10), -1.0, None, ALU.mult))
                step.link(log1p_rest(z, u, lg, c4[:, 0:10], c4[:, 30:40], c4[:, 20:30]))
                v.tensor_scalar(c4[:, 10:20], c4[:, 20:30], -4.0, None, ALU.mult)
                step.link(v.tensor_scalar(c4[:, 0:10], c4[:, 20:30], 4.0, None, ALU.mult))
                v.tensor_scalar(c4[:, 20:30], col_span("rba", 10), 0.5, None, ALU.mult)
                v.tensor_scalar(c4[:, 30:40], col_span("rbx", 10), 0.5, None, ALU.mult).then_inc(q["c4_ready"], 1)

            down_stage("f0_down", {3: softplus_1, 4: softplus_2})
            residual("f0_down")

            norm("rg_in", "nmix1")

            def gated_input(s):
                t = S[:, 512 + s % 2 * T:512 + (s % 2 + 1) * T]
                dve.wait_ge(q["it_ready"], s + 1)
                step.link(v.tensor_scalar(t, t, 0.5, 0.5, ALU.mult, ALU.add))
                v.tensor_tensor(IX[:, s, :], t, S[:, s % 2 * T:(s % 2 + 1) * T], ALU.mult).then_inc(q["ix_ready"], 1)

            for s in range(RNN):
                n = N0["rg_in"] + s
                split_lo(n + 2)
                dve.wait_ge(q["lin_ready"], LIN["rg_in"] + s + 1)
                for tap in (1, 2, 3):
                    zt = S[:, s % 2 * T + tap:(s % 2 + 1) * T]
                    last = stt(out=zt, in0=bank[n % 4][:, T:2 * T - tap], scalar=col("rconv", (3 - tap) * 10 + s),
                               in1=zt, op0=ALU.mult, op1=ALU.add)
                    if tap < 3:
                        step.link(last)
                last.then_inc(evacuated[s % 2], 1)
                if s:
                    gated_input(s - 1)
            gated_input(RNN - 1)
            for s in range(RNN):
                a, th, sq = A1[:, s, :], S[:, 1024 + s * T:1280 + s * T], S[:, 3584 + s % 2 * T:3840 + s % 2 * T]
                dve.wait_ge(q["rg_exp"], s + 1)
                step.link(v.tensor_tensor(sq, a, a, ALU.mult))
                stt(out=th, in0=sq, scalar=1.0, in1=th, op0=ALU.add, op1=ALU.mult).then_inc(q["rg_arg"], 1)
            dve.wait_ge(q["ix_ready"], RNN)
            for s in range(RNN):
                a, th = A1[:, s, :], S[:, 1024 + s * T:1280 + s * T]
                dve.wait_ge(q["rg_root"], s + 1)
                step.link(v.tensor_tensor(th, th, IX[:, s, :], ALU.mult))
                step.link(v.tensor_tensor_scan(IX[:, s, :], a, th, 0.0, ALU.mult, ALU.add))
                step.link(v.tensor_tensor(GG[:, s, :], GG[:, s, :], IX[:, s, :], ALU.mult))
                step.link(v.tensor_copy(HH[:, s, :], GG[:, s, :]))
                last = v.tensor_tensor(HL[:, s, :], GG[:, s, :], HH[:, s, :].bitcast(F32), ALU.subtract)
                if s % 2:
                    last.then_inc(q["h_ready"], 1)
            down_stage("rg_out")
            residual("rg_out")

            norm("f1_up", "nffn1")
            conv_ffn("f1_up", 1, 11)
            modulation(0)
            down_stage("f1_down")
            residual("f1_down")

            norm("g00_up", 0, 0)
            gated_ffn("g00_up")

            def angles_1():
                step.link(v.tensor_copy(CS[:, :], posi[:, :]))
                step.link(v.tensor_scalar(CS[:, :], CS[:, :], col("inv_freq"), None, ALU.mult))
                step.link(v.tensor_scalar(R[:, 0:T], CS[:, :], con_mat("phase", 1), 1.0 / TWO_PI, ALU.add, ALU.mult))
                step.link(v.tensor_scalar(R[:, 0:T], R[:, 0:T], ROUND, None, ALU.add))
                step.link(v.tensor_scalar(R[:, 0:T], R[:, 0:T], -ROUND, None, ALU.add))

            def angles_2():
                for part in TURN:
                    step.link(stt(out=CS[:, :], in0=R[:, 0:T], scalar=-part, in1=CS[:, :], op0=ALU.mult, op1=ALU.add))
                step.link(v.tensor_scalar(CS[:, :], CS[:, :], con_mat("phase", 1), None, ALU.add))
                v.tensor_scalar(CS[:, :], CS[:, :], 3.1415925, -3.1415925, ALU.min, ALU.max).then_inc(q["angle_ready"], 1)

            def rope_table():
                dve.wait_ge(q["table_ready"], 1)
                step.link(v.tensor_scalar(CS[:, :], CS[:, :], con_mat("sign", 1), con_mat("nope", 1),
                                          ALU.mult, ALU.add))

            down_stage("g00_down", {1: angles_1, 3: angles_2, 5: rope_table})
            residual("g00_down", 0)

            norm("ssd_in", 8, 24)
            for s in range(25):
                n = N0["ssd_in"] + s
                split_lo(n + 2)
                if s < 16:
                    dve.wait_ge(q["lin_ready"], LIN["ssd_in"] + s + 1)
                    marks = [0, 0]
                    for k, d in ((0, 2), (1, 1), (3, -1), (4, -2)):
                        for m in range(2):
                            base = s % 2 * 512 + m * T
                            src = bank[n % 4][:, m * T:(m + 1) * T]
                            if d > 0:
                                zt, src = S[:, base + d:base + T], src[:, 0:T - d]
                            else:
                                zt, src = S[:, base:base + T + d], src[:, -d:T]
                            if k:
                                step.wait(marks[m])
                            last = stt(out=zt, in0=src, scalar=col("sconv", 32 * k + 2 * s + m), in1=zt,
                                       op0=ALU.mult, op1=ALU.add)
                            if k < 4:
                                marks[m] = step.put(last)
                    last.then_inc(evacuated[s % 2], 1)
                if s in (18, 19):
                    for r in range(4 * (s - 18), 4 * (s - 17)):
                        dve.wait_ge(q["xs_turn"], r + 1)
                        v.tensor_copy(XST[:, r % 2, r // 2 * 4:r // 2 * 4 + 4, :],
                                      bank[4 + r % 4][:, :].rearrange("p (a t) -> p a t", a=4)).then_inc(q["xs_turned"], 1)
                if s == 17:
                    dve.wait_ge(q["dt_z"], 1)
                    v.tensor_scalar(S[0:64, 2560:2816], S[0:64, 2304:2560], 1.0, None,
                                    ALU.add).then_inc(q["dt_u"], 1)
                if s == 20:
                    dve.wait_ge(q["dt_log"], 1)
                    y, z2, u2, l2, t2, o2 = (S[0:64, at:at + T] for at in (2048, 2304, 2560, 2816, 3072, 3328))
                    step.link(log1p_rest(z2, u2, l2, t2, y, o2))
                    step.link(v.tensor_copy(y, o2))
                    step.link(v.tensor_scalar(t2, y, tiny[0:64, 50:51], -1.0, ALU.mult, ALU.mult))
                    step.link(v.memset(u2, 1.0))
                    v.tensor_tensor_scan(z2[0:32, :], u2[0:32, :], t2[0:32, :], 0.0, ALU.mult, ALU.add)
                    step.link(v.tensor_tensor_scan(z2[32:64, ::-1], u2[32:64, :], t2[32:64, ::-1], 0.0,
                                                   ALU.mult, ALU.add))
                    step.link(v.tensor_copy(acr[0:64, :], z2))
                    v.tensor_tensor(acr[64:P, :], z2, acr[0:64, :].bitcast(F32),
                                    ALU.subtract).then_inc(q["exponents_ready"], 1)
            dve.wait_ge(q["col_turn"], 1)
            v.tensor_copy(cols[:, 0:2, :], bank[4][:, 0:128].rearrange("p (a t) -> p a t", a=2))
            v.tensor_scalar(cols[:, 2:4, :], bank[4][:, 128:256].rearrange("p (a t) -> p a t", a=2), -1.0, None,
                            ALU.mult).then_inc(q["cols_ready"], 1)
            dve.wait_ge(q["cols_ready"], 1)

            def gate_y(pair):
                t = S[:, 2048 + pair % 2 * T:2048 + (pair % 2 + 1) * T]
                dve.wait_ge(q["y_ready"], 2 * pair + 2)
                step.link(stt(out=t, in0=XS[:, pair, :], scalar=col("skip", pair),
                              in1=bank[6 + pair % 2][:, 0:T], op0=ALU.mult, op1=ALU.add))
                if pair % 2 and pair >= 3:
                    v.tensor_copy(tiny[:, 61 + pair:63 + pair], bank[6 + pair % 2][:, T:T + 2])
                v.tensor_tensor(A1[:, pair, :], A1[:, pair, :], t, ALU.mult).then_inc(q["yz_ready"], 1)

            for h in range(SSD_H):
                E, g = EX[:, h % 2], h // 4
                dve.wait_ge(q["decay_ready"], h + 1)
                a = v.tensor_scalar(E[:, 4, :], E[:, 4, :], cols[:, 0, 32 + h:33 + h], None, ALU.mult)
                m4 = step.put(a)
                m5 = step.put(v.tensor_scalar(E[:, 5, :], E[:, 5, :], cols[:, 1, 32 + h:33 + h], None, ALU.mult))
                step.wait(m4)
                stt(out=E[:, 0, :], in0=E[:, 0, :], scalar=cols[:, 0, h:h + 1], in1=E[:, 4, :],
                    op0=ALU.mult, op1=ALU.add)
                step.wait(m5)
                step.link(stt(out=E[:, 3, :], in0=E[:, 3, :], scalar=cols[:, 1, h:h + 1], in1=E[:, 5, :],
                              op0=ALU.mult, op1=ALU.add))
                if h % 4 == 0:
                    dve.wait_ge(q["cb_ready"], g + 1)
                if h >= 2:
                    dve.wait_ge(q["y_ready"], h - 1)
                v.tensor_tensor(MT[:, h % 2], E[:, 0:4, :].rearrange("p (j a) t -> p j (a t)", j=2),
                                two(bank[g % 2][:, :]), ALU.mult).then_inc(q["mt_ready"], 1)
                if h % 2 == 0 and h:
                    gate_y(h // 2 - 1)
            gate_y(15)
            dve.wait_ge(q["ysum_ready"], 1)
            v.tensor_copy(tiny[:, 78:80], bank[6][:, T:T + 2]).then_inc(q["ysum_kept"], 1)
            dve.wait_ge(q["yroot_ready"], 1)
            step.link(v.reciprocal(tiny[:, 96:112], tiny[:, 80:96]))

            def diagonal(g):
                for j in range(2):
                    last = v.tensor_scalar(A2[:, g, j * P:(j + 1) * P], ident,
                                           tiny[:, 96 + 2 * g + j:97 + 2 * g + j], None, ALU.mult)
                last.then_inc(q["ydiag_ready"], 1)

            def group_rest(g):
                dve.wait_ge(q["yh_ready"], g + 1)
                v.tensor_tensor(HL[:, 2 * g:2 * g + 2, :], A1[:, 2 * g:2 * g + 2, :],
                                HH[:, 2 * g:2 * g + 2, :].bitcast(F32), ALU.subtract).then_inc(q["h_ready"], 1)

            diagonal(0)
            diagonal(1)
            for g in range(SSD_G):
                if g + 2 < SSD_G:
                    diagonal(g + 2)
                dve.wait_ge(q["yspread_ready"], g + 1)
                for k in (2 * g, 2 * g + 1):
                    last = stt(out=A1[:, k, :], in0=A1[:, k, :], scalar=col("snorm", k), in1=bank[g % 4][:, 0:T],
                               op0=ALU.mult, op1=ALU.mult)
                last.then_inc(q["yn_ready"], 1)
                if g:
                    group_rest(g - 1)
            group_rest(SSD_G - 1)
            down_stage("ssd_out")
            residual("ssd_out", 8)

            norm("g01_up", 16, 48)
            gated_ffn("g01_up")
            modulation(1)
            down_stage("g01_down")
            residual("g01_down", 16)
            norm("g10_up", 24, 72)
            gated_ffn("g10_up")
            down_stage("g10_down")
            residual("g10_down", 24)

            norm("mla_in", 32, 96)
            for s in range(3):
                split_lo(N0["mla_in"] + s + 2)
            for k in range(5):
                dve.wait_ge(q["lat_hi"], k + 1)
                v.tensor_tensor(XL[:, k, :], A1[:, k, :], XH[:, k, :].bitcast(F32),
                                ALU.subtract).then_inc(q["x_ready"], 1 if k < 4 else 4)
            v5 = A1[:, 5, :]
            v.tensor_tensor(v5, v5, CS[:, :], ALU.mult).then_inc(q["pe_scaled"], 1)
            dve.wait_ge(q["lat_root"], 1)
            v.tensor_scalar(tiny[:, 112:114], bank[4][:, 4:6], 1.0 / 96, None, ALU.mult)
            step.link(v.reciprocal(tiny[:, 120:124], tiny[:, 116:120]))
            step.link(stt(out=tiny[:, 124:128], in0=tiny[:, 120:124], scalar=1.0 / 96, in1=tiny[:, 120:124],
                          op0=ALU.mult, op1=ALU.mult))
            dve.wait_ge(q["rope_summed"], 1)
            step.link(v.tensor_tensor(KR[64:P, :], bank[6][64:P, 0:T], R[64:P, 0:T], ALU.mult))

            def over_two(ap):
                return ap.rearrange("p (a t) -> p a t", a=1).to_broadcast([ap.shape[0], 2, T])

            for u in range(8):
                if u % 2 == 0:
                    split_lo(N0["mla_uq"] + u // 2 + 2)
                t = S[:, 1024 + u % 2 * 512:1536 + u % 2 * 512]
                dve.wait_ge(q["mq_kept"], u + 1)
                v.tensor_tensor(QH[:, 2 * u:2 * u + 2, :], two(t), over_two(CS[:, :]), ALU.mult).then_inc(q["mq_ready"], 1)

            def per_head(at, n):
                return tiny[:, at:at + 2].rearrange("p (a t) -> p a t", a=1).to_broadcast([P, n, 2])

            def heads_of(ap, n):
                return ap.rearrange("p (a t) -> p a t", a=n)

            raw_q, fac_q = tiny[:, 128:160], tiny[:, 160:192]
            dve.wait_ge(q["mq_sum"], 8)
            v.tensor_tensor(heads_of(raw_q, 16), heads_of(bank[7][:, 0:32], 16), per_head(124, 16),
                            ALU.mult).then_inc(q["mq_var"], 1)
            dve.wait_ge(q["mq_root"], 1)
            step.link(v.reciprocal(raw_q, fac_q))
            step.link(stt(out=heads_of(fac_q, 16), in0=heads_of(raw_q, 16), scalar=96 ** -0.5,
                          in1=per_head(120, 16), op0=ALU.mult, op1=ALU.mult))

            def key_diagonal(u):
                if u >= 2:
                    dve.wait_ge(q["mk_spread"], u - 1)
                for k in range(4):
                    at = 224 + 4 * u + k
                    last = v.tensor_scalar(S[:, 2048 + u % 2 * 512 + k * P:2048 + u % 2 * 512 + (k + 1) * P],
                                           ident, tiny[:, at:at + 1], None, ALU.mult)
                last.then_inc(q["mk_diag"], 1)

            for s in range(2):
                split_lo(N0["mla_ukv"] + s + 2)
                raw_k, fac_k = tiny[:, 192 + 16 * s:208 + 16 * s], tiny[:, 224 + 16 * s:240 + 16 * s]
                dve.wait_ge(q["mk_sum"], s + 1)
                step.link(v.tensor_tensor(heads_of(raw_k, 8), heads_of(bank[4 + s][:, 0:16], 8), per_head(126, 8),
                                          ALU.mult))
                v.tensor_tensor(heads_of(raw_k, 8), heads_of(raw_k, 8), per_head(112, 8),
                                ALU.add).then_inc(q["mk_var"], 1)
                dve.wait_ge(q["mk_root"], s + 1)
                step.link(v.reciprocal(raw_k, fac_k))
                step.link(v.tensor_tensor(heads_of(fac_k, 8), heads_of(raw_k, 8), per_head(122, 8), ALU.mult))
                key_diagonal(4 * s)
                for u in range(4 * s, 4 * s + 4):
                    if u % 4 < 3:
                        key_diagonal(u + 1)
                    dve.wait_ge(q["mk_spread"], u + 1)
                    low = KH[0:64, 2 * u:2 * u + 2, :]
                    v.tensor_tensor(low, low, two(bank[6 + u % 2][0:64, :]), ALU.mult)
                    v.tensor_tensor(KH[64:P, 2 * u:2 * u + 2, :], over_two(KR[64:P, :]),
                                    two(bank[6 + u % 2][64:P, :]), ALU.mult).then_inc(q["mk_ready"], 1)
            for r in range(4):
                j, half = r % 2, r // 2
                dve.wait_ge(q["mv_turn"], r + 1)
                v.tensor_scalar(VT2[:, j, half * 512:(half + 1) * 512], bank[r][:, :], tiny[:, 122 + j:123 + j],
                                None, ALU.mult).then_inc(q["mv_turned"], 1)
            attention(HEADS1, MLA_H)
            cat_lo(A1)
            residual("mla_out", 32)

            norm("g11_up", 40, 120)
            gated_ffn("g11_up")
            down_stage("g11_down")
            residual("g11_down", 40, more=False)

        @block.gpsimd
        def _(pool):
            g = nc.gpsimd
            step = Steps(pool, q["pool_steps"])
            step.link(g.memset(UP[:, :, :, 0:PAD], 0.0))
            pool.dma_start(cond[:, :], cvec).then_inc(q["cond_loaded"], 16)
            pool.dma_start(posi[:, :], pos).then_inc(q["late_loaded"], 16)
            pool.dma_start(A2[:, 0:12, :].rearrange("p a t -> p (a t)"), small).then_inc(q["late_loaded"], 16)
            pool.dma_start(A2[:, 12:16, :].rearrange("p a t -> p (a t)"), tab[:, 0:4 * T]).then_inc(q["late_loaded"], 16)
            pool.dma_start(DIST, tab[:, 4 * T:6 * T]).then_inc(q["late_loaded"], 16)
            for k in range(2):
                pool.dma_start(modw[:, k, :], wmod[k]).then_inc(mod_loaded[k], 16)
            for e in evacuated:
                pool.wait_ge(e, 1)
            src = UP[:, 0]
            for lvl in range(4):
                w = 1 << lvl
                dst = UP[:, 1 + lvl % 2]
                prev = src if lvl == 0 else UP[:, 1 + (lvl - 1) % 2]
                if lvl == 0:
                    step.link(g.tensor_tensor(dst[:, :, PAD:], prev[:, :, PAD:], prev[:, :, PAD - w:PAD - w + T], ALU.add))
                else:
                    step.link(g.tensor_tensor(dst[:, lvl:, PAD:], prev[:, lvl:, PAD:],
                                              prev[:, lvl:, PAD - w:PAD - w + T], ALU.add))
            pool.wait_ge(q["late_loaded"], 16 * 4)
            for gi in range(4):
                own = UP[:, 1 + gi % 2, gi, PAD:]
                step.link(g.tensor_tensor(own, own, INV[:, gi, :], ALU.mult))
                last = g.tensor_tensor(UP[:, 0, gi, PAD:], own, UP[:, 0, gi, PAD:], ALU.subtract)
            last.then_inc(q["pooled"], 1)

            pool.wait_ge(q["cond_ready"], 1)

            def unit(k, n, i, layer, load):
                w = modw[:, k, :]
                pool.wait_ge(mod_loaded[k], plus(16 * (n // 2 + 1), i, 16))
                step.link(g.tensor_tensor(w, w, cond[:, :], ALU.mult))
                half = D // 2
                while half > 16:
                    step.link(g.tensor_tensor(w[:, 0:half], w[:, 0:half], w[:, half:2 * half], ALU.add))
                    half //= 2
                local = n - 72 * layer
                dst = (modp[:, local, :] if i is None else
                       modp[:, bass.ds(i * 2 + local, 1), :].rearrange("p a s -> p (a s)"))
                g.tensor_tensor(dst, w[:, 0:16], w[:, 16:32], ALU.add).then_inc(q["mod_summed"], 1)
                if load:
                    pool.wait_ge(q["mod_summed"], plus(n + 1, i, 2))
                    src = wmod[n + 2] if i is None else wmod[i * 2 + (n + 2)]
                    pool.dma_start(modw[:, k, :], src).then_inc(mod_loaded[k], 16)

            for layer in range(2):
                if layer:
                    pool.wait_ge(q["mod_taken"], 1)
                n0 = 72 * layer
                with pool.Fori(0, 35 + (layer == 0)) as i:
                    step.enter(i, 12)
                    unit(0, n0, i, layer, True)
                    unit(1, n0 + 1, i, layer, True)
                    step.leave(35 + (layer == 0))
                if layer:
                    unit(0, n0 + 70, None, layer, False)
                    unit(1, n0 + 71, None, layer, False)


def _feature_cols(a):
    return np.ascontiguousarray(a).reshape(-1, P).T


def _up_slabs(w):
    m = w.shape[1] // P
    t = w.reshape(KD, P, m, P).transpose(2, 1, 0, 3).reshape(m // 2, 2, P, KD * P)
    return t.transpose(0, 2, 1, 3).reshape(m // 2, P, SLAB)


def _down_slabs(w):
    k = w.shape[0] // P
    return w.reshape(k // 2, 2, P, D).transpose(0, 2, 1, 3).reshape(k // 2, P, SLAB)


def _side_by_side(a, b, each=2 * P):
    n = a.shape[1] // each
    return np.stack([a.reshape(-1, n, each), b.reshape(-1, n, each)], axis=2).reshape(a.shape[0], -1)


def _constants():
    p = np.arange(P)
    f = np.float32
    con = np.zeros((P, NCON), f)
    con[:, CON["ident"]:CON["ident"] + P] = np.eye(P, dtype=f)
    con[:, CON["ones"]:CON["ones"] + P] = 1
    con[:, CON["pair64"]:CON["pair64"] + P] = (p[:, None] // 64 == p[None, :] // 64)
    con[64:, CON["rope_sum"] + 64:CON["rope_sum"] + P] = (p[64:, None] % 32 == p[None, 64:] % 32)
    con[:, CON["mask_f"]:CON["mask_f"] + P] = np.where(p[None, :] >= p[:, None], 0, MASKED)
    con[:, CON["mask_b"]:CON["mask_b"] + P] = np.where(p[None, :] <= p[:, None], 0, MASKED)
    con[:, CON["select"]:CON["select"] + 64] = (p[:, None] % 64 == p[None, 0:64])
    con[64:96, CON["phase"]] = np.pi / 2
    con[64:96, CON["sign"]] = 1
    con[96:112, CON["sign"]] = -1
    con[112:, CON["sign"]] = 1
    con[0:64, CON["nope"]] = 1
    t = np.arange(T)
    windows = [1 / np.minimum(t + 1, w).astype(f) for w in (2, 4, 8, 16)]
    inv = np.broadcast_to(np.concatenate(windows).astype(f), (P, 4 * T))
    rows = np.arange(T).reshape(2, P).T
    dist = np.where(t[None, None, :] <= rows[:, :, None], t[None, None, :] - rows[:, :, None], -1e30)
    tab = np.concatenate([inv, dist.reshape(P, 2 * T).astype(f)], axis=1)
    freq = np.float32(10000.0) ** (-np.arange(0, 32, 2, dtype=f) / np.float32(32))
    inv_freq = np.concatenate([np.zeros(64, f), np.tile(freq.astype(f), 4)])
    return con, np.ascontiguousarray(tab), inv_freq[:, None]


def _layout(i):
    rope = [np.arange(0, 16), np.arange(16, 32), np.arange(16, 32), np.arange(0, 16)]
    rope = np.concatenate(rope)
    rg = i["rg_w_in"][0]
    ssd = i["ssd_w_in_2"][0]
    mla = i["mla_w_in_2"][0]
    f32 = np.float32
    ssd_in = np.concatenate([ssd[:, 4096:6144], ssd[:, 2048:4096], ssd[:, 6144:6208],
                             np.zeros((D, 2 * P - 64), f32), ssd[:, 0:2048]], axis=1)
    mla_in = np.concatenate([mla[:, 0:640], np.zeros((D, 64), f32), mla[:, 640 + rope]], axis=1)
    uq = i["mla_w_uq_2"][0].reshape(3, P, MLA_H, 96)
    uq = np.concatenate([uq[..., 0:64], uq[..., 64 + rope]], axis=3)
    uq = np.concatenate([uq, np.zeros((1,) + uq.shape[1:], f32)], axis=0)
    uq = uq.transpose(2, 1, 0, 3).reshape(4, 4, P, 4 * P).transpose(0, 2, 1, 3).reshape(4, P, SLAB)
    ukv = i["mla_w_ukv_2"][0].reshape(2, P, MLA_H, P)
    ukv = ukv.transpose(2, 1, 0, 3).reshape(2, 8, P, 2 * P).transpose(0, 2, 1, 3).reshape(2, P, SLAB)

    def ffn1(layer):
        w = i["ffn_w_in"][layer]
        return [_up_slabs(_side_by_side(w[:, 0:FF], w[:, FF:])), _down_slabs(i["ffn_w_out"][layer])]

    def ffn2(layer, k):
        return [_up_slabs(_side_by_side(i["ffn_w_gate_2"][layer, k], i["ffn_w_up_2"][layer, k])),
                _down_slabs(i["ffn_w_down_2"][layer, k])]

    slabs = ([_up_slabs(i["pa_w_in"][0]), _up_slabs(i["pa_w_out"][0])] + ffn1(0)
             + [_up_slabs(_side_by_side(rg[:, 0:1280], rg[:, 1280:], P)), _down_slabs(i["rg_w_out"][0])]
             + ffn1(1) + ffn2(0, 0) + [_up_slabs(ssd_in), _down_slabs(i["ssd_w_out_2"][0])]
             + ffn2(0, 1) + ffn2(1, 0)
             + [_up_slabs(mla_in), uq, ukv, _up_slabs(i["mla_w_out_2"][0])] + ffn2(1, 1))
    slabs = np.concatenate(slabs, axis=0)
    assert slabs.shape == (NSLABS, P, SLAB), slabs.shape

    con, tab, inv_freq = _constants()
    cw, cb = i["ssd_conv_w_2"][0], i["ssd_conv_b_2"][0]

    def order(a):
        return np.concatenate([a[..., 2048:4096], a[..., 0:2048]], axis=-1)

    def rows(a):
        return np.concatenate([np.ravel(a), np.zeros(P - a.size, f32)])[:, None]

    par = {"nmix0": i["norm_mix"][0], "nmix1": i["norm_mix"][1], "nffn0": i["norm_ffn"][0],
           "nffn1": i["norm_ffn"][1], "pool_scale": i["pa_pool_scale"][0],
           "q_gain": np.tile(i["pa_q_gain"][0], 2), "k_gain": np.tile(i["pa_k_gain"][0], 2),
           "fconv0": i["ffn_conv_w"][0], "fconvb0": i["ffn_conv_b"][0],
           "fconv1": i["ffn_conv_w"][1], "fconvb1": i["ffn_conv_b"][1],
           "rconv": i["rg_conv_w"][0], "rconvb": i["rg_conv_b"][0], "rba": i["rg_b_a"][0],
           "rbx": i["rg_b_x"][0], "lam": i["rg_lambda"][0], "ng": i["norm_g_2"], "bmod": i["b_mod_2"],
           "sconv": order(cw), "sconvb": order(cb), "dt_bias": rows(i["ssd_dt_bias_2"][0]),
           "a_log": rows(i["ssd_a_log_2"][0]), "skip": np.repeat(i["ssd_d_2"][0], 64),
           "snorm": i["ssd_norm_g_2"][0], "mqn": i["mla_q_norm_g_2"][0], "mkn": i["mla_kv_norm_g_2"][0],
           "mqh": i["mla_q_head_g_2"][0][np.concatenate([np.arange(64), 64 + rope])],
           "mkh": i["mla_k_head_g_2"][0][np.concatenate([np.arange(64), 64 + rope])],
           "inv_freq": inv_freq}
    par = np.concatenate([_feature_cols(par[k]) for k in COL], axis=1)
    assert par.shape == (P, NPAR), par.shape
    small = np.concatenate([i["pa_pool_w"][0], i["rg_w_a"][0], i["rg_w_x"][0]], axis=0)
    small = small.transpose(1, 0, 2).reshape(P, 24 * P)
    return {
        "x": i["x"][0].T.reshape(KD, P, T).transpose(1, 0, 2),
        "slabs": slabs, "par": par, "con": con, "tab": tab, "small": small,
        "cvec": np.broadcast_to(i["c_2"], (P, D)), "pos": np.broadcast_to(i["positions_2"], (P, T)),
        "wmod": i["w_mod_2"].transpose(0, 2, 1).reshape(144, P, D),
    }


def kernel(**inputs):
    import concourse.bacc as bacc
    from concourse.bass_utils import run_bass_kernel_spmd

    laid = {k: np.ascontiguousarray(a) for k, a in _layout({k: np.asarray(a) for k, a in inputs.items()}).items()}
    nc = bacc.Bacc("TRN2", target_bir_lowering=False, num_devices=1,
                   dynamic_dma_scratch_size=DMA_SCRATCH)
    args = {k: nc.dram_tensor(f"{k}_dram", a.shape, mybir.dt.from_np(a.dtype), kind="ExternalInput").ap()
            for k, a in laid.items()}
    out = nc.dram_tensor("out_dram", (P, KD, T), F32, kind="ExternalOutput").ap()
    build(nc, args["x"], args["slabs"], args["par"], args["con"], args["tab"], args["small"],
          args["cvec"], args["pos"], args["wmod"], out)
    r = run_bass_kernel_spmd(nc, [{f"{k}_dram": a for k, a in laid.items()}], core_ids=[0])
    y = r.results[0]["out_dram"]
    return np.ascontiguousarray(y.transpose(1, 0, 2).reshape(D, T).T).reshape(1, T, D)
```
